# Optimizing a Trainium2 kernel written in Bass

```python
import math
import jax, jax.numpy as jnp
from jax import lax
import numpy as np

D_MODEL = 1024
BATCH = 1
SEQ = 2048
DEPTH = 1

HEAD_DIM = 64
N_HEADS = D_MODEL // HEAD_DIM
DSA_HEADS = N_HEADS // 2
NSA_HEADS = N_HEADS - DSA_HEADS
DSA_WIDTH = DSA_HEADS * HEAD_DIM
NSA_WIDTH = NSA_HEADS * HEAD_DIM
ROPE_THETA = 500000.0
IDX_HEADS = 8
IDX_DIM = 32
IDX_TOPK = 256
Q_BLOCK = 128
NSA_KV_GROUPS = 2
NSA_GROUP_SIZE = NSA_HEADS // NSA_KV_GROUPS
KV_WIDTH = NSA_KV_GROUPS * HEAD_DIM
CMP_BLOCK = 32
CMP_STRIDE = 16
CMP_HIDDEN = 2 * HEAD_DIM
SLC_BLOCK = 64
SLC_COUNT = 8
WINDOW = 512
NSA_Q_BLOCK = 32
FORCE_SCORE = 1.0e4
FFN_HIDDEN = -(-8 * D_MODEL // (3 * 256)) * 256
ALPHA = (2.0 * DEPTH) ** 0.25
BETA = (8.0 * DEPTH) ** -0.25
LN_EPS = 1e-5
IN_SPLITS = (DSA_WIDTH, HEAD_DIM, HEAD_DIM, IDX_HEADS * IDX_DIM, IDX_HEADS, IDX_DIM,
             NSA_WIDTH, KV_WIDTH, KV_WIDTH, KV_WIDTH, KV_WIDTH, KV_WIDTH, KV_WIDTH, 3 * NSA_HEADS)
IN_IS_VALUE = (False, False, True, False, False, False,
               False, False, True, False, True, False, True, False)
IN_COLS = sum(IN_SPLITS)

kernel_name = "hymba_dsa_nsa_deepnorm_layer"

def split_columns(p):
    outs, start = [], 0
    for n in IN_SPLITS:
        outs.append(p[..., start:start + n])
        start += n
    return outs

def rope_partial(x, positions):
    rot = x.shape[-1] // 4
    half = rot // 2
    inv_freq = jnp.power(ROPE_THETA, -jnp.arange(half, dtype=jnp.float32) / half)
    ang = positions.astype(jnp.float32)[:, :, None, None] * inv_freq
    cos = jnp.cos(ang).astype(x.dtype)
    sin = jnp.sin(ang).astype(x.dtype)
    x1, x2 = x[..., :half], x[..., half:rot]
    return jnp.concatenate([x1 * cos - x2 * sin, x2 * cos + x1 * sin, x[..., rot:]], axis=-1)

def masked_softmax(s, mask):
    s = jnp.where(mask, s.astype(jnp.float32), -jnp.inf)
    m = jnp.max(s, axis=-1, keepdims=True)
    m = jnp.where(jnp.isfinite(m), m, 0.0)
    p = jnp.exp(s - m)
    return p / jnp.maximum(jnp.sum(p, axis=-1, keepdims=True), 1e-30)

def layer_norm(x, g, b):
    xf = x.astype(jnp.float32)
    mu = jnp.mean(xf, axis=-1, keepdims=True)
    var = jnp.mean(jnp.square(xf - mu), axis=-1, keepdims=True)
    return ((xf - mu) * lax.rsqrt(var + LN_EPS)).astype(x.dtype) * g + b

def group_rms(o):
    of = o.astype(jnp.float32)
    return (of * lax.rsqrt(jnp.mean(of * of, axis=-1, keepdims=True) + LN_EPS)).astype(o.dtype)

def dsa_mixer(q, k, v, iq, iw, ik):
    B, S, H, dh = q.shape
    topk = min(IDX_TOPK, S // 4)
    nblk = S // Q_BLOCK
    key_pos = jnp.arange(S)
    scale = HEAD_DIM ** -0.5
    idx_scale = (IDX_HEADS ** -0.5) * (IDX_DIM ** -0.5)

    def block(i):
        s0 = i * Q_BLOCK
        qb = lax.dynamic_slice_in_dim(q, s0, Q_BLOCK, axis=1)
        iqb = lax.dynamic_slice_in_dim(iq, s0, Q_BLOCK, axis=1)
        iwb = lax.dynamic_slice_in_dim(iw, s0, Q_BLOCK, axis=1)
        qpos = s0 + jnp.arange(Q_BLOCK)
        causal = key_pos[None, :] <= qpos[:, None]
        logits = jnp.einsum('bqhd,bsd->bqhs', iqb, ik)
        index = jnp.einsum('bqh,bqhs->bqs', iwb, jax.nn.relu(logits)) * idx_scale
        index = jnp.where(causal[None], index.astype(jnp.float32), -jnp.inf)
        _, sel = lax.top_k(index, topk)
        kg = jax.vmap(lambda kb, ib: kb[ib])(k, sel)
        vg = jax.vmap(lambda vb, ib: vb[ib])(v, sel)
        valid = (sel <= qpos[None, :, None])[:, :, None, :]
        s = jnp.einsum('bqhd,bqkd->bqhk', qb, kg) * scale
        p = masked_softmax(s, valid)
        return jnp.einsum('bqhk,bqkd->bqhd', p.astype(vg.dtype), vg)

    out = lax.map(block, jnp.arange(nblk))
    return out.transpose(1, 0, 2, 3, 4).reshape(B, S, H * dh)

def compress(kv, pos_emb, w1, w2):
    B, S, G, dh = kv.shape
    n_c = (S - CMP_BLOCK) // CMP_STRIDE + 1
    idx = jnp.arange(n_c)[:, None] * CMP_STRIDE + jnp.arange(CMP_BLOCK)[None, :]
    blocks = kv[:, idx] + pos_emb[None, None, :, None, :]
    flat = blocks.transpose(0, 1, 3, 2, 4).reshape(B, n_c, G, CMP_BLOCK * dh)
    return jax.nn.gelu(flat @ w1) @ w2

def nsa_mixer(q, k_cmp, v_cmp, k_slc, v_slc, k_win, v_win, gates, cmp_pos, cmp_w1, cmp_w2):
    B, S, H, dh = q.shape
    G, R = NSA_KV_GROUPS, NSA_GROUP_SIZE
    q = q.reshape(B, S, G, R, dh)
    scale = HEAD_DIM ** -0.5
    kc = compress(k_cmp, cmp_pos[0], cmp_w1[0], cmp_w2[0])
    vc = compress(v_cmp, cmp_pos[1], cmp_w1[1], cmp_w2[1])
    n_c = kc.shape[1]
    cmp_start = jnp.arange(n_c) * CMP_STRIDE
    cmp_end = cmp_start + CMP_BLOCK - 1
    n_s = S // SLC_BLOCK
    n_sel = min(SLC_COUNT, n_s)
    slc_start = jnp.arange(n_s) * SLC_BLOCK
    overlap = ((cmp_start[:, None] < slc_start[None, :] + SLC_BLOCK)
               & (cmp_end[:, None] >= slc_start[None, :])).astype(jnp.float32)
    ks_blocks = k_slc.reshape(B, n_s, SLC_BLOCK, G, dh).transpose(0, 3, 1, 2, 4)
    vs_blocks = v_slc.reshape(B, n_s, SLC_BLOCK, G, dh).transpose(0, 3, 1, 2, 4)
    pad = ((0, 0), (WINDOW, 0), (0, 0), (0, 0))
    kw_pad = jnp.pad(k_win, pad)
    vw_pad = jnp.pad(v_win, pad)
    nblk = S // NSA_Q_BLOCK
    QB = NSA_Q_BLOCK
    j = jnp.arange(n_s)

    def block(i):
        s0 = i * QB
        qb = lax.dynamic_slice_in_dim(q, s0, QB, axis=1)
        gb = lax.dynamic_slice_in_dim(gates, s0, QB, axis=1)
        qpos = s0 + jnp.arange(QB)
        s_c = jnp.einsum('bqgrd,bcgd->bgrqc', qb, kc) * scale
        p_c = masked_softmax(s_c, cmp_end[None, :] <= qpos[:, None])
        o_c = jnp.einsum('bgrqc,bcgd->bqgrd', p_c.astype(vc.dtype), vc)
        imp = jnp.einsum('bgrqc,cj->bgqj', p_c, overlap)
        cur = qpos // SLC_BLOCK
        forced = (j[None] == 0) | (j[None] == cur[:, None]) | (j[None] == cur[:, None] - 1)
        visible = slc_start[None, :] <= qpos[:, None]
        imp = jnp.where(forced[None, None], FORCE_SCORE, imp)
        imp = jnp.where(visible[None, None], imp, -1.0)
        _, sel = lax.top_k(imp, n_sel)
        gather = jax.vmap(jax.vmap(lambda kb, ib: kb[ib]))
        ksel = gather(ks_blocks, sel).reshape(B, G, QB, n_sel * SLC_BLOCK, dh)
        vsel = gather(vs_blocks, sel).reshape(B, G, QB, n_sel * SLC_BLOCK, dh)
        tok = (sel[..., None] * SLC_BLOCK + jnp.arange(SLC_BLOCK)).reshape(B, G, QB, n_sel * SLC_BLOCK)
        smask = (tok <= qpos[None, None, :, None])[:, :, None]
        s_s = jnp.einsum('bqgrd,bgqkd->bgrqk', qb, ksel) * scale
        p_s = masked_softmax(s_s, smask)
        o_s = jnp.einsum('bgrqk,bgqkd->bqgrd', p_s.astype(vsel.dtype), vsel)
        kw = lax.dynamic_slice_in_dim(kw_pad, s0, WINDOW + QB, axis=1)
        vw = lax.dynamic_slice_in_dim(vw_pad, s0, WINDOW + QB, axis=1)
        wpos = s0 - WINDOW + jnp.arange(WINDOW + QB)
        diff = qpos[:, None] - wpos[None, :]
        wmask = (diff >= 0) & (diff < WINDOW) & (wpos[None, :] >= 0)
        s_w = jnp.einsum('bqgrd,bkgd->bgrqk', qb, kw) * scale
        p_w = masked_softmax(s_w, wmask)
        o_w = jnp.einsum('bgrqk,bkgd->bqgrd', p_w.astype(vw.dtype), vw)
        return gb[..., 0:1] * o_c + gb[..., 1:2] * o_s + gb[..., 2:3] * o_w

    out = lax.map(block, jnp.arange(nblk))
    return out.transpose(1, 0, 2, 3, 4, 5).reshape(B, S, H * dh)

def hybrid_layer(x, positions, w_in, b_in, cmp_pos, cmp_w1, cmp_w2, mix_gain, w_out,
                 ln1_g, ln1_b, w_gate, w_up, w_down, ln2_g, ln2_b):
    B, S, _ = x.shape
    G = NSA_KV_GROUPS
    (dq, dk, dv, iq, iw, ik, nq, kcm, vcm, ksl, vsl, kwn, vwn, ng) = split_columns(x @ w_in + b_in)
    dq = rope_partial(dq.reshape(B, S, DSA_HEADS, HEAD_DIM), positions)
    dk = rope_partial(dk.reshape(B, S, 1, HEAD_DIM), positions)[:, :, 0]
    iq = rope_partial(iq.reshape(B, S, IDX_HEADS, IDX_DIM), positions)
    ik = rope_partial(ik.reshape(B, S, 1, IDX_DIM), positions)[:, :, 0]
    o_dsa = dsa_mixer(dq, dk, dv, iq, iw, ik)
    nq = rope_partial(nq.reshape(B, S, NSA_HEADS, HEAD_DIM), positions)
    heads = lambda t: t.reshape(B, S, G, HEAD_DIM)
    kcm = rope_partial(heads(kcm), positions)
    ksl = rope_partial(heads(ksl), positions)
    kwn = rope_partial(heads(kwn), positions)
    gates = jax.nn.sigmoid(ng).reshape(B, S, G, NSA_GROUP_SIZE, 3)
    o_nsa = nsa_mixer(nq, kcm, heads(vcm), ksl, heads(vsl), kwn, heads(vwn), gates,
                      cmp_pos, cmp_w1, cmp_w2)
    mixed = jnp.concatenate([group_rms(o_dsa), group_rms(o_nsa)], axis=-1) * mix_gain
    h = layer_norm(ALPHA * x + mixed @ w_out, ln1_g, ln1_b)
    ffn = (jax.nn.silu(h @ w_gate) * (h @ w_up)) @ w_down
    return layer_norm(ALPHA * h + ffn, ln2_g, ln2_b)

def setup_inputs(seed: int = 0) -> dict:
    key = jax.random.key(seed)
    ks = jax.random.split(key, 16)

    def nrm(k, shape, scale):
        return jax.random.normal(k, shape, jnp.float32) * scale

    x = nrm(ks[0], (BATCH, SEQ, D_MODEL), 1.0)
    offset = jax.random.randint(ks[1], (BATCH, 1), 0, 4096, dtype=jnp.int32)
    positions = offset + jnp.arange(SEQ, dtype=jnp.int32)[None, :]
    in_keys = jax.random.split(ks[2], len(IN_SPLITS))
    w_in = jnp.concatenate(
        [nrm(k, (DEPTH, D_MODEL, n), D_MODEL ** -0.5 * (BETA if is_v else 1.0))
         for k, n, is_v in zip(in_keys, IN_SPLITS, IN_IS_VALUE)], axis=-1)
    b_in = nrm(ks[3], (DEPTH, IN_COLS), 0.01)
    cmp_pos = nrm(ks[4], (DEPTH, 2, CMP_BLOCK, HEAD_DIM), 0.02)
    cmp_w1 = nrm(ks[5], (DEPTH, 2, CMP_BLOCK * HEAD_DIM, CMP_HIDDEN), (CMP_BLOCK * HEAD_DIM) ** -0.5)
    cmp_w2 = nrm(ks[6], (DEPTH, 2, CMP_HIDDEN, HEAD_DIM), CMP_HIDDEN ** -0.5)
    mix_gain = 1.0 + nrm(ks[7], (DEPTH, D_MODEL), 0.02)
    w_out = nrm(ks[8], (DEPTH, D_MODEL, D_MODEL), D_MODEL ** -0.5 * BETA)
    ln1_g = 1.0 + nrm(ks[9], (DEPTH, D_MODEL), 0.02)
    ln1_b = nrm(ks[10], (DEPTH, D_MODEL), 0.01)
    w_gate = nrm(ks[11], (DEPTH, D_MODEL, FFN_HIDDEN), D_MODEL ** -0.5)
    w_up = nrm(ks[12], (DEPTH, D_MODEL, FFN_HIDDEN), D_MODEL ** -0.5)
    w_down = nrm(ks[13], (DEPTH, FFN_HIDDEN, D_MODEL), FFN_HIDDEN ** -0.5 * BETA)
    ln2_g = 1.0 + nrm(ks[14], (DEPTH, D_MODEL), 0.02)
    ln2_b = nrm(ks[15], (DEPTH, D_MODEL), 0.01)
    return {"x": x, "positions": positions, "w_in": w_in, "b_in": b_in,
            "cmp_pos": cmp_pos, "cmp_w1": cmp_w1, "cmp_w2": cmp_w2, "mix_gain": mix_gain,
            "w_out": w_out, "ln1_g": ln1_g, "ln1_b": ln1_b, "w_gate": w_gate, "w_up": w_up,
            "w_down": w_down, "ln2_g": ln2_g, "ln2_b": ln2_b}

def reference(x, positions, w_in, b_in, cmp_pos, cmp_w1, cmp_w2, mix_gain, w_out,
              ln1_g, ln1_b, w_gate, w_up, w_down, ln2_g, ln2_b):
    for l in range(DEPTH):
        x = hybrid_layer(x, positions, w_in[l], b_in[l], cmp_pos[l], cmp_w1[l], cmp_w2[l],
                         mix_gain[l], w_out[l], ln1_g[l], ln1_b[l], w_gate[l], w_up[l],
                         w_down[l], ln2_g[l], ln2_b[l])
    return x


_drawn_inputs = setup_inputs


def setup_inputs(seed=0):
    import zlib

    import numpy as np

    out = dict(_drawn_inputs(seed))
    spreads = {}
    factors = {'mix_gain': 6.209, 'ln1_g': 2.735, 'ln1_b': 5.633, 'ln2_g': 2.865, 'ln2_b': 5.73}
    for name, (base, spread) in spreads.items():
        noise = np.random.default_rng([zlib.crc32(name.encode()), seed]).standard_normal(out[name].shape)
        drawn = base * np.exp(spread * noise) if base else spread * noise
        out[name] = __import__('jax').numpy.asarray(drawn.astype(out[name].dtype))
    for name, factor in factors.items():
        out[name] = (out[name] * factor).astype(out[name].dtype)
    return out
```

```python
from contextlib import ExitStack

import numpy as np

import concourse.bass as bass
from concourse import mybir

F32 = mybir.dt.float32
F32R = mybir.dt.float32r
BF16 = mybir.dt.bfloat16
I32 = mybir.dt.int32
ALU = mybir.AluOpType
ACT = mybir.ActivationFunctionType
AX = mybir.AxisListType

P = 128
SEQ = 2048
TILES = SEQ // P
D_MODEL = 1024
KT = D_MODEL // P
HEAD = 64
DSA_HEADS = 8
NSA_HEADS = 8
GROUPS = 2
IDX_HEADS = 8
IDX_DIM = 32
TOPK = 256
WINDOW = 512
CMP_BLOCK = 32
CMP_STRIDE = 16
N_CMP = (SEQ - CMP_BLOCK) // CMP_STRIDE + 1
SLC_BLOCK = 64
N_SLC = SEQ // SLC_BLOCK
FFN = 2816
ALPHA = 2.0 ** 0.25
LN_EPS = 1e-5
SCALE = HEAD ** -0.5
MASKED = -1e30
FLOOR = -1e20

PARTS = (("dq", 512), ("nq", 512), ("dk", 64), ("ksl", 128), ("kwn", 128), ("kcm", 128),
         ("iq", 256), ("ik", 32), ("dv", 64), ("vsl", 128), ("vwn", 128), ("vcm", 128), ("iw", 8), ("ng", 24))
COL, _at = {}, 0
for _name, _n in PARTS:
    COL[_name] = _at
    _at += _n
IN_COLS = _at
R64 = COL["iq"] // HEAD
R32 = (COL["dv"] - COL["iq"]) // IDX_DIM
NCH = 5
CH = IN_COLS // NCH
MAGIC = 1.5 * 2.0 ** 23
TWO_PI = 2 * np.pi
PI_A = 6.28125
PI_B = float(np.float32(np.round((TWO_PI - PI_A) * 2 ** 20) / 2 ** 20))
PI_C = float(TWO_PI - PI_A - PI_B)
PI_MAX = float(np.nextafter(np.float32(np.pi), np.float32(0)))


def projection_phase(nc, x_t, w_in, b_in, pos, inv_freq, z):
    with ExitStack() as ctx:
        def sb(name, shape, dt=F32):
            return ctx.enter_context(nc.sbuf_tensor(name, shape, dt))

        def sem(name):
            return ctx.enter_context(nc.semaphore(name))

        HALF = IN_COLS // 2
        w_hi = sb("pw_hi", [P, KT, IN_COLS], F32R)
        w_lo = sb("pw_lo", [P, KT, IN_COLS], F32R)
        w_raw = sb("pw_raw", [P, 2, HALF])
        x_raw = sb("px_raw", [P, 2, KT, P])
        x_hi = sb("px_hi", [P, 2, KT, P], F32R)
        x_lo = sb("px_lo", [P, 2, KT, P], F32R)
        bias = sb("p_bias", [P, IN_COLS])
        zt = sb("p_z", [P, 2, IN_COLS])
        posi = sb("p_posi", [P, TILES], I32)
        posf = sb("p_posf", [P, TILES])
        freq = sb("p_freq", [P, 12])
        cos2 = sb("p_cos", [P, TILES, 2, 12])
        sin2 = sb("p_sin", [P, TILES, 2, 12])
        ra = sb("p_ra", [P, R64, 2, 8])
        rb = sb("p_rb", [P, R64, 2, 8])
        ra3 = sb("p_ra3", [P, R32, 2, 4])
        rb3 = sb("p_rb3", [P, R32, 2, 4])
        acc = [ctx.enter_context(nc.psum_tensor(f"p_acc{c}", [P, 512], F32)) for c in range(NCH)]
        def scratch(n):
            return zt[:, 0, n * 192:(n + 1) * 192].rearrange("p (t f) -> p t f", t=TILES)
        ang, kk, r1, r2 = (scratch(n) for n in range(4))

        small_in = sem("p_small_in")
        bias_in = sem("p_bias_in")
        w_in_ld = [sem(f"p_w_ld{b}") for b in range(2)]
        w_hi_done = sem("p_w_hi")
        w_lo_done = sem("p_w_lo")
        x_ld = [sem(f"p_x_ld{b}") for b in range(2)]
        x_hi_done = sem("p_x_hi")
        x_lo_done = sem("p_x_lo")
        acc_full = sem("p_acc_full")
        acc_free = sem("p_acc_free")
        trig = sem("p_trig")
        trig_done = sem("p_trig_done")
        v = sem("p_vec")
        z_ready = sem("p_z_ready")
        z_out = [sem(f"p_z_out{b}") for b in range(2)]

        block = ctx.enter_context(nc.Block())
        x_tiles = x_t.rearrange("(k p) n -> p k n", p=P)
        w_rows = w_in.rearrange("(k p) n -> k p n", p=P)
        z_tiles = z.rearrange("(t p) n -> t p n", p=P)
        NW = 2 * KT

        @block.sync
        def _(sp):
            def store(tile, u):
                sp.wait_ge(z_ready, tile + 1)
                sp.dma_start(z_tiles[bass.ds(tile, 1), :, :].rearrange("o p n -> (o p) n"), zt[:, u]).then_inc(z_out[u], 16)

            sp.dma_start(posi[:, :], pos).then_inc(small_in, 16)
            sp.dma_start(freq[:, :], inv_freq).then_inc(small_in, 16)
            sp.dma_start(x_raw[:, 0], x_tiles[:, :, 0:P]).then_inc(x_ld[0], 16)
            for c in range(NW):
                if c >= 2:
                    sp.wait_ge(w_lo_done, c - 1)
                sp.dma_start(w_raw[:, c % 2], w_rows[c // 2, :, (c % 2) * HALF:(c % 2 + 1) * HALF]).then_inc(w_in_ld[c % 2], 16)
            sp.dma_start(bias[:, :], b_in.broadcast_to([P, IN_COLS])).then_inc(bias_in, 16)
            sp.dma_start(x_raw[:, 1], x_tiles[:, :, P:2 * P]).then_inc(x_ld[1], 16)
            with sp.Fori(0, TILES // 2 - 1) as t:
                for u in range(2):
                    sp.wait_ge(x_lo_done, 2 * t + u + 1)
                    sp.dma_start(x_raw[:, u], x_tiles[:, :, bass.ds((2 * t + u + 2) * P, P)]).then_inc(x_ld[u], 16)
                    store(2 * t + u, u)
            for u in range(2):
                store(TILES - 2 + u, u)
            for u in range(2):
                sp.wait_ge(z_out[u], 16 * (TILES // 2 + 1))

        @block.scalar
        def _(act):
            act.wait_ge(trig, 1)
            act.activation(cos2[:, :, 0, :], r2, ACT.Sin).then_inc(trig_done, 1)
            act.activation(cos2[:, :, 1, :], r2, ACT.Sin).then_inc(trig_done, 1)
            act.activation(sin2[:, :, 0, :], r1, ACT.Sin, scale=-1.0).then_inc(trig_done, 1)
            act.activation(sin2[:, :, 1, :], r1, ACT.Sin).then_inc(trig_done, 1)
            def high(t, u):
                act.wait_ge(x_ld[u], (t + 1) * 16)
                act.wait_ge(acc_full, (2 * t + u + 1) * NCH)
                act.activation(x_hi[:, u], x_raw[:, u], ACT.Copy).then_inc(x_hi_done, 1)

            high(0, 0)
            for c in range(NW):
                act.wait_ge(w_in_ld[c % 2], 16 * (c // 2 + 1))
                act.activation(w_hi[:, c // 2, (c % 2) * HALF:(c % 2 + 1) * HALF], w_raw[:, c % 2], ACT.Copy).then_inc(w_hi_done, 1)
            high(0, 1)
            with act.Fori(1, TILES // 2) as t:
                for u in range(2):
                    high(t, u)

        @block.tensor
        def _(pe):
            pe.sem_inc(acc_full, 2 * NCH)

            def product(u, c, k, n, last):
                xs, ws = ((x_hi, w_hi), (x_hi, w_lo), (x_lo, w_hi))[n]
                mm = pe.matmul(acc[c][:, 0:CH], xs[:, u, k], ws[:, k, c * CH:(c + 1) * CH],
                               start=(k == 0 and n == 0), stop=last)
                if last:
                    mm.then_inc(acc_full, 1)

            def tile_products(tile, u):
                pe.wait_ge(x_lo_done, tile + 1)
                for c in range(NCH):
                    pe.wait_ge(acc_free, tile * NCH + c + 1)
                    for k in range(KT):
                        for n in range(3):
                            product(u, c, k, n, k == KT - 1 and n == 2)

            pe.wait_ge(x_lo_done, 1)
            pe.wait_ge(acc_free, NCH)
            for k in range(KT):
                pe.wait_ge(w_lo_done, 2 * (k + 1))
                for c in range(NCH):
                    for n in range(3):
                        product(0, c, k, n, k == KT - 1 and n == 2)
            tile_products(1, 1)
            with pe.Fori(1, TILES // 2) as t:
                for u in range(2):
                    tile_products(2 * t + u, u)

        @block.vector
        def _(dve):
            def wait_own(value):
                dve.wait_ge(v, value)

            dve.sem_inc(acc_free, NCH)
            dve.wait_ge(small_in, 32)
            dve.tensor_copy(posf[:, :], posi[:, :]).then_inc(v, 1)
            wait_own(1)
            fb = freq[:, :].unsqueeze(1).broadcast_to([P, TILES, 12])
            pb = posf[:, :].unsqueeze(2).broadcast_to([P, TILES, 12])
            dve.tensor_tensor(ang, pb, fb, ALU.mult).then_inc(v, 1)
            n = 2
            for r, shift in ((r1, 0.0), (r2, 0.25)):
                wait_own(n)
                dve.tensor_scalar(kk, ang, 1.0 / TWO_PI, shift, ALU.mult, ALU.add).then_inc(v, 1)
                wait_own(n + 1)
                dve.tensor_scalar(kk, kk, MAGIC, MAGIC, ALU.add, ALU.subtract).then_inc(v, 1)
                src = ang
                for m, part in enumerate((PI_A, PI_B, PI_C)):
                    wait_own(n + 2 + m)
                    dve.scalar_tensor_tensor(r, kk, -part, src, ALU.mult, ALU.add).then_inc(v, 1)
                    src = r
                n += 5
                if shift:
                    wait_own(n)
                    dve.tensor_scalar(r, r, float(np.float32(np.pi / 2)), None, ALU.add).then_inc(v, 1)
                    n += 1
                for op, turn in ((ALU.is_gt, -TWO_PI), (ALU.is_lt, TWO_PI)):
                    wait_own(n)
                    dve.tensor_scalar(kk, r, PI_MAX if turn < 0 else -PI_MAX, turn, op, ALU.mult).then_inc(v, 1)
                    wait_own(n + 1)
                    dve.tensor_tensor(r, r, kk, ALU.add).then_inc(v, 1)
                    n += 2
                wait_own(n)
                dve.tensor_scalar(r, r, PI_MAX, -PI_MAX, ALU.min, ALU.max).then_inc(v, 1)
                n += 1
            wait_own(n)
            dve.sem_inc(trig, 1)
            for u in range(2):
                dve.sem_inc(z_out[u], 16)

            def split(t, u):
                dve.wait_ge(x_hi_done, t + 1)
                dve.tensor_tensor(x_lo[:, u], x_raw[:, u], x_hi[:, u].bitcast(F32), ALU.subtract).then_inc(x_lo_done, 1)

            split(0, 0)
            for c in range(NW):
                dve.wait_ge(w_hi_done, c + 1)
                dve.tensor_tensor(w_lo[:, c // 2, (c % 2) * HALF:(c % 2 + 1) * HALF], w_raw[:, c % 2],
                                  w_hi[:, c // 2, (c % 2) * HALF:(c % 2 + 1) * HALF].bitcast(F32), ALU.subtract).then_inc(w_lo_done, 1)
            dve.wait_ge(trig_done, 4)
            dve.wait_ge(bias_in, 16)
            STEPS = 7

            def bias_and_rope(t, u, last):
                tile = 2 * t + u
                base = n + tile * STEPS
                if not last:
                    split(tile + 1, 1 - u)
                dve.wait_ge(z_out[u], 16 * (t + 1))
                for c in range(NCH):
                    dve.wait_ge(acc_full, (tile + 2) * NCH + c + 1)
                    dve.tensor_tensor(zt[:, u, c * CH:(c + 1) * CH], acc[c][:, 0:CH], bias[:, c * CH:(c + 1) * CH],
                                      ALU.add).then_inc(acc_free, 1)
                dve.wait_ge(acc_free, (tile + 2) * NCH)
                done = base
                for h, (lo, heads, dim, f, fo, a, b) in enumerate(((0, R64, HEAD, 8, 0, ra, rb),
                                                                  (COL["iq"], R32, IDX_DIM, 4, 8, ra3, rb3))):
                    zr = zt[:, u, lo:lo + heads * dim].rearrange("p (h d) -> p h d", h=heads)[:, :, 0:2 * f].rearrange(
                        "p h (a f) -> p h a f", a=2)
                    cs = cos2[:, bass.ds(tile, 1), :, fo:fo + f].rearrange("p o a f -> p (o a) f").unsqueeze(1).broadcast_to([P, heads, 2, f])
                    sn = sin2[:, bass.ds(tile, 1), :, fo:fo + f].rearrange("p o a f -> p (o a) f").unsqueeze(1).broadcast_to([P, heads, 2, f])
                    dve.tensor_tensor(a[:, :, :, :], zr, cs, ALU.mult).then_inc(v, 1)
                    dve.tensor_tensor(b[:, :, 0, :], zr[:, :, 1, :], sn[:, :, 0, :], ALU.mult).then_inc(v, 1)
                    dve.tensor_tensor(b[:, :, 1, :], zr[:, :, 0, :], sn[:, :, 1, :], ALU.mult).then_inc(v, 1)
                    dve.wait_ge(v, done + 3)
                    dve.tensor_tensor(zr, a[:, :, :, :], b[:, :, :, :], ALU.add).then_inc((v, z_ready)[h], 1)
                    done = done + 4

            with dve.Fori(0, TILES // 2 - 1) as t:
                for u in range(2):
                    bias_and_rope(t, u, False)
            bias_and_rope(TILES // 2 - 1, 0, False)
            bias_and_rope(TILES // 2 - 1, 1, True)


def compression_phase(nc, z, cmp_pos, cmp_w1, cmp_w2, ident_in, kc, vc):
    LC = CMP_BLOCK // 2
    LAST = CMP_STRIDE * (N_CMP - 1)
    with ExitStack() as ctx:
        def sb(name, shape, dt=F32):
            return ctx.enter_context(nc.sbuf_tensor(name, shape, dt))

        def sem(name):
            return ctx.enter_context(nc.semaphore(name))

        rows = sb("c_rows", [P, TILES, 4, 2, HEAD])
        pairs = sb("c_pairs", [P, 2, SEQ])
        w1 = sb("c_w1", [P, 2, LC, P])
        w2k = sb("c_w2k", [P, 2, HEAD])
        w2v = sb("c_w2v", [P, HEAD])
        pos = sb("c_pos", [P, 2, LC])
        ident = sb("c_ident", [P, P])
        posb = sb("c_posb", [P, 2])
        y = sb("c_y", [P, 4, N_CMP])
        u = sb("c_u", [P, 4, N_CMP])
        g = sb("c_g", [P, 4, N_CMP])
        hi_tmp = sb("c_hi", [P, 2, P], F32R)
        turned = [ctx.enter_context(nc.psum_tensor(f"c_turned{b}", [P, 512], F32)) for b in range(2)]
        hid = [ctx.enter_context(nc.psum_tensor(f"c_hid{h}", [P, 512], F32)) for h in range(4)]
        small = ctx.enter_context(nc.psum_tensor("c_small", [P, 512], F32))

        w_ld = sem("c_w_ld")
        rows_ld = [sem(f"c_rows_ld{h}") for h in range(4)]
        turned_full = sem("c_turned_full")
        upper_done = sem("c_upper_done")
        lower_done = sem("c_lower_done")
        hid_full = sem("c_hid_full")
        v = sem("c_vec")
        tanh_done = sem("c_tanh_done")
        small_full = sem("c_small_full")
        block = ctx.enter_context(nc.Block())
        z_rows = z.rearrange("(t p) n -> p t n", p=P)
        head_col = [COL["kcm"], COL["kcm"] + HEAD, COL["vcm"], COL["vcm"] + HEAD]

        @block.sync
        def _(sp):
            sp.dma_start(ident[:, :], ident_in).then_inc(w_ld, 16)
            for h in range(4):
                for twice in range(2):
                    sp.dma_start(rows[:, :, h, twice, :], z_rows[:, :, head_col[h]:head_col[h] + HEAD]).then_inc(rows_ld[h], 16)
            sp.dma_start(pos[:, :, :], cmp_pos).then_inc(w_ld, 16)

        @block.tensor
        def _(pe):
            pe.wait_ge(w_ld, 16 * 7)
            for b in range(2):
                for c in range(LC):
                    mm = pe.matmul(small[:, b:b + 1], w1[:, b, c], pos[:, b, c:c + 1], start=(c == 0), stop=(c == LC - 1))
            mm.then_inc(small_full, 1)
            for h in range(4):
                pe.wait_ge(rows_ld[h], 32)
                for q in range(4):
                    n = 4 * h + q
                    if n >= 2:
                        pe.wait_ge(upper_done, n - 1)
                        pe.wait_ge(lower_done, n - 1)
                    for t in range(4):
                        mm = pe.transpose(turned[n % 2][:, t * P:(t + 1) * P],
                                          rows[:, 4 * q + t, h].rearrange("p a d -> p (a d)"), ident[:, :])
                    mm.then_inc(turned_full, 1)
                pe.wait_ge(upper_done, 4 * (h + 1))
                pe.wait_ge(lower_done, 4 * (h + 1))
                for c in range(LC):
                    mm = pe.matmul(hid[h][:, 0:N_CMP], w1[:, h // 2, c], pairs[:, h % 2, 2 * c:2 * c + LAST + 1:CMP_STRIDE],
                                   start=(c == 0), stop=(c == LC - 1))
                mm.then_inc(hid_full, 1)
            pe.wait_ge(v, 12)
            for h in range(2):
                pe.matmul(small[:, h * P:h * P + N_CMP], w2k[:, :, :].rearrange("p a d -> p (a d)"), g[:, h, :],
                          start=True, stop=True)
            for h in range(2):
                mm = pe.matmul(small[0:N_CMP, (2 + h) * P:(2 + h) * P + HEAD], g[:, 2 + h, :], w2v[:, :], start=True, stop=True)
            mm.then_inc(small_full, 1)

        @block.scalar
        def _(act):
            for b in range(2):
                act.dma_start(w1[:, b], cmp_w1[b].rearrange("(c p) n -> p c n", p=P)).then_inc(w_ld, 16)
            for twice in range(2):
                act.dma_start(w2k[:, twice], cmp_w2[0]).then_inc(w_ld, 16)
            act.dma_start(w2v[:, :], cmp_w2[1]).then_inc(w_ld, 16)
            for n in range(16):
                h, q = divmod(n, 4)
                if q == 0 and h >= 2:
                    act.wait_ge(hid_full, h - 1)
                act.wait_ge(turned_full, n + 1)
                act.activation(pairs[0:HEAD, h % 2, 512 * q:512 * (q + 1)], turned[n % 2][0:HEAD, :], ACT.Copy).then_inc(upper_done, 1)
            act.wait_ge(v, 10)
            act.activation(u[:, :, :], u[:, :, :], ACT.Tanh, scale=float(np.sqrt(2 / np.pi))).then_inc(tanh_done, 1)

        @block.vector
        def _(dve):
            dve.memset(kc.bitcast(F32), 0.0).then_inc(v, 1)
            dve.memset(vc.bitcast(F32), 0.0).then_inc(v, 1)
            for n in range(16):
                h, q = divmod(n, 4)
                if q == 0 and h >= 2:
                    dve.wait_ge(hid_full, h - 1)
                dve.wait_ge(turned_full, n + 1)
                skip = 1 if q == 0 else 0
                dve.tensor_copy(pairs[HEAD:P, h % 2, 512 * q - 1 + skip:512 * (q + 1) - 1], turned[n % 2][HEAD:P, skip:512]).then_inc(lower_done, 1)
                if n == 0:
                    dve.wait_ge(small_full, 1)
                    dve.tensor_copy(posb[:, :], small[:, 0:2]).then_inc(v, 1)
            dve.wait_ge(v, 3)
            for h in range(4):
                dve.wait_ge(hid_full, h + 1)
                dve.tensor_scalar(y[:, h, :], hid[h][:, 0:N_CMP], posb[:, h // 2:h // 2 + 1], None, ALU.add).then_inc(v, 1)
            dve.wait_ge(v, 7)
            dve.tensor_tensor(u[:, :, :], y[:, :, :], y[:, :, :], ALU.mult).then_inc(v, 1)
            dve.wait_ge(v, 8)
            dve.tensor_scalar(u[:, :, :], u[:, :, :], 0.044715, 1.0, ALU.mult, ALU.add).then_inc(v, 1)
            dve.wait_ge(v, 9)
            dve.tensor_tensor(u[:, :, :], u[:, :, :], y[:, :, :], ALU.mult).then_inc(v, 1)
            dve.wait_ge(tanh_done, 1)
            dve.scalar_tensor_tensor(g[:, :, :], u[:, :, :], 1.0, y[:, :, :], ALU.add, ALU.mult).then_inc(v, 1)
            dve.wait_ge(v, 11)
            dve.tensor_scalar(g[:, :, :], g[:, :, :], 0.5, None, ALU.mult).then_inc(v, 1)
            dve.wait_ge(small_full, 2)
            keys = small[:, 0:2 * P].rearrange("p (h n) -> p h n", h=2)[:, :, 0:N_CMP]
            vals = small[0:N_CMP, 2 * P:4 * P].rearrange("p (h n) -> p h n", h=2)[:, :, 0:HEAD]
            dve.tensor_copy(kc[0:HEAD, :, 0:N_CMP], keys[0:HEAD]).then_inc(v, 1)
            dve.tensor_copy(hi_tmp[HEAD:P, :, 0:N_CMP], keys[HEAD:P]).then_inc(v, 1)
            dve.tensor_copy(vc[0:N_CMP, :, 0:HEAD], vals).then_inc(v, 1)
            dve.wait_ge(v, 15)
            dve.tensor_tensor(kc[HEAD:P, :, 0:N_CMP], keys[HEAD:P], hi_tmp[HEAD:P, :, 0:N_CMP].bitcast(F32), ALU.subtract).then_inc(v, 1)
            dve.tensor_tensor(vc[0:N_CMP, :, HEAD:P], vals, vc[0:N_CMP, :, 0:HEAD].bitcast(F32), ALU.subtract).then_inc(v, 1)


RING = 8
W_TILES = WINDOW // P + 1
CHUNK = 1024
NSTEP = 24
ZA = COL["dk"]
ZA_COLS = IN_COLS - ZA
PT_RING = 3
CONST = (("ident", P), ("diag", P), ("win", W_TILES * P), ("cmp", 248), ("keep", 62), ("add", 62), ("halve", NSTEP + 1))
CCOL, _at = {}, 0
for _name, _n in CONST:
    CCOL[_name] = _at
    _at += _n
CONST_COLS = _at


def attention_schedule():
    units = []
    for i in range(TILES):
        for h in range(NSA_HEADS):
            units.append(("C", i, h))
            if 2 <= i + 1 < TILES:
                units.append(("I", i + 1, h))
        for kind in "WSD":
            units += [(kind, i, h) for h in range(8)]
    return units


def key_tiles(kind, i):
    if kind == "C":
        return 0, 1
    if kind == "W":
        return max(0, i - W_TILES + 1), min(i + 1, W_TILES)
    return 0, i + 1


def attention_phase(nc, z, consts, kc, vc, o_mix):
    units = attention_schedule()
    N = len(units)
    where = {u: n for n, u in enumerate(units)}
    width = [P * key_tiles(k, i)[1] for k, i, h in units]
    chunks = [[(c, min(CHUNK, w - c)) for c in range(0, w, CHUNK)] for w in width]
    att = [n for n in range(N) if units[n][0] != "I"]
    a_of = {n: a for a, n in enumerate(att)}
    chunk0, mask0, relu0 = [0], [0], [0]
    for n in range(N):
        m = len(chunks[n])
        chunk0.append(chunk0[-1] + m)
        mask0.append(mask0[-1] + (m if n in a_of else 0))
        relu0.append(relu0[-1] + (0 if n in a_of else m))
    reader = [("mask", mask0[n] + c + 1) if n in a_of else ("relu", relu0[n] + c + 1)
              for n in range(N) for c in range(len(chunks[n]))]
    preps = [("A", 0), ("A", 1), ("N", 0)]
    pool_at, pe_at = {}, {}
    for i in range(TILES):
        preps.append(("D", i))
        pool_at.setdefault(where[("C", i, 0)], []).append(("D", i))
        pe_at.setdefault(where[("C", i, 2)], []).append(("D", i))
        if i + 1 < TILES:
            preps.append(("N", i + 1))
            pool_at.setdefault(where[("S", i, 6)], []).append(("N", i + 1))
            pe_at.setdefault(where[("D", i, 1)], []).append(("N", i + 1))
        if i + 2 < TILES:
            preps.append(("A", i + 2))
            pool_at.setdefault(where[("D", i, 2)], []).append(("A", i + 2))
            pe_at.setdefault(where[("D", i, 5)], []).append(("A", i + 2))
    prep_no = {p: m for m, p in enumerate(preps)}
    PREP_BLOCKS = {"A": 14, "N": 8, "D": 8}
    EVACS = {"A": (((0, 1, "dk"), (1, 2, "ksl"), (3, 1, "kwn0")), ((4, 1, "kwn1"), (5, 1, "ik"), (6, 2, "iq")), ((8, 4, "iq"),), ((12, 2, "iq"),)),
             "N": (((0, 4, "nq"),), ((4, 4, "nq"),)), "D": (((0, 4, "dq"),), ((4, 4, "dq"),))}
    groups, evac_no = [], {}
    n_evac = 0

    def add_prep(p):
        nonlocal n_evac
        for g, ops in enumerate(EVACS[p[0]]):
            n_evac += len(ops)
            evac_no[(p, g)] = n_evac
            groups.append(("prep", p, g))
    for p in preps[:3]:
        add_prep(p)
    att_group0 = {}
    n_att = 0
    for n in range(N):
        for p in pe_at.get(n, ()):
            add_prep(p)
        if n in a_of:
            att_group0[n] = n_att
            for g in range((width[n] // P + 3) // 4):
                groups.append(("att", n, g))
                n_att += 1
    group_no = {g: m for m, g in enumerate(groups)}
    last_group = {n: att_group0[n] + (width[n] // P + 3) // 4 for n in att}
    steps = {}
    for i in range(1, TILES - 1):
        for m, (kind, h) in enumerate([(k, h) for k in "WSD" for h in range(8)]):
            steps[where[(kind, i, h)]] = ((i - 1) * NSTEP + m, i + 1, m)
    act_part = {t: (t + 1) * P * 7 // 16 // 64 * 64 for t in range(TILES)}

    with ExitStack() as ctx:
        def sb(name, shape, dt=F32):
            return ctx.enter_context(nc.sbuf_tensor(name, shape, dt))

        def sem(name):
            return ctx.enter_context(nc.semaphore(name))

        def psum(name, cols):
            return ctx.enter_context(nc.psum_tensor(name, [P, cols], F32))

        cst = sb("a_const", [P, CONST_COLS])
        def const(name, lo, n):
            return cst[:, CCOL[name] + lo:CCOL[name] + lo + n]
        dk_t = sb("a_dk", [P, SEQ], F32R)
        ksl_t = sb("a_ksl", [P, GROUPS, SEQ], F32R)
        kwn_t = sb("a_kwn", [P, GROUPS, RING, P], F32R)
        ik_t = sb("a_ik", [P, SEQ], F32R)
        iq_t = sb("a_iq", [P, IDX_HEADS, P], F32R)
        dv = sb("a_dv", [P, TILES, 2, HEAD], F32R)
        vsl = sb("a_vsl", [P, GROUPS, TILES, 2, HEAD], F32R)
        vwn = sb("a_vwn", [P, GROUPS, RING, 2, HEAD], F32R)
        q_t = {"N": sb("a_nq", [P, 8, P], F32R), "D": sb("a_dq", [P, 8, P], F32R)}
        q_s = {"N": sb("a_nqs", [P, 8, P], F32R), "D": sb("a_dqs", [P, 8, P], F32R)}
        za = sb("a_za", [P, ZA_COLS])
        zq = {"N": sb("a_zn", [P, 512]), "D": sb("a_zd", [P, 512])}
        split = sb("a_split", [P, 14, P], F32R)
        scores = [sb(f"a_scores{b}", [P, SEQ]) for b in range(2)]
        p_hi = sb("a_p_hi", [P, PT_RING, 512], F32R)
        p_lo = sb("a_p_lo", [P, PT_RING, 512], F32R)
        index = [sb(f"a_index{b}", [P, SEQ]) for b in range(2)]
        relu = sb("a_relu", [P, 2, CHUNK])
        mask_d = sb("a_mask_d", [P, SEQ], BF16)
        mask_s = sb("a_mask_s", [P, GROUPS, SEQ], BF16)
        above = sb("a_above", [P, SEQ], BF16)
        atleast = sb("a_atleast", [P, SEQ], BF16)
        junk_a = sb("a_junk_a", [P, 896], BF16)
        junk_v = sb("a_junk_v", [P, 1152], BF16)
        oacc = sb("a_oacc", [P, 2, 2 * 512])
        fin = sb("a_fin", [P, 2, 2, 256])
        iw = sb("a_iw", [P, 2, IDX_HEADS])
        gate = sb("a_gate", [P, 2, 24])
        nmax = sb("a_nmax", [P, 4, 2])
        lsum = sb("a_lsum", [P, 2, 4])
        rsum = sb("a_rsum", [P, 2, 4])
        rgate = sb("a_rgate", [P, 2, 4])
        imp_c = sb("a_imp_c", [P, P + 1])
        imp = sb("a_imp", [P, 2, N_SLC])
        top8 = sb("a_top8", [P, 8])
        sel = sb("a_sel", [P, 2, N_SLC])
        tk = sb("a_tk", [P, 16])
        amax, thr, cnt_a, cnt_v, tmp1, tmp2, lo, hi, n_above, room = (tk[:, m:m + 1] for m in range(10))
        halves = sb("a_halves", [P, NSTEP + 1])

        ps_s = [psum(f"a_ps_s{b}", CHUNK) for b in range(2)]
        ps_t = [psum(f"a_ps_t{b}", 512) for b in range(2)]
        ps_o = [psum(f"a_ps_o{b}", 512) for b in range(2)]

        const_ld = sem("a_const_ld")
        za_ld = sem("a_za_ld")
        zq_ld = {k: sem(f"a_z{k}_ld") for k in "ND"}
        split_done = sem("a_split_done")
        prep_turned = sem("a_prep_turned")
        group_turned = sem("a_group_turned")
        evac_done = sem("a_evac_done")
        swap_done = {k: sem(f"a_swap{k}") for k in "ND"}
        qk_done = sem("a_qk_done")
        masked = sem("a_masked")
        exp_done = sem("a_exp_done")
        hi_done = sem("a_hi_done")
        lo_done = sem("a_lo_done")
        pv_done = sem("a_pv_done")
        relu_done = sem("a_relu_done")
        index_done = sem("a_index_done")
        search_set = sem("a_search_set")
        count_a = sem("a_count_a")
        count_v = sem("a_count_v")
        thr_moved = sem("a_thr_moved")
        above_done = sem("a_above_done")
        atleast_done = sem("a_atleast_done")
        kept_done = sem("a_kept_done")
        mask_d_done = sem("a_mask_d_done")
        sel_done = sem("a_sel_done")
        mask_s_done = sem("a_mask_s_done")
        gate_in = sem("a_gate_in")
        gate_exp = sem("a_gate_exp")
        gate_done = sem("a_gate_done")
        fin_done = sem("a_fin_done")
        acc_done = sem("a_acc_done")
        out_done = [sem(f"a_out{b}") for b in range(2)]
        vec = sem("a_vec")
        own = sem("a_pool_own")

        block = ctx.enter_context(nc.Block())
        z_tiles = z.rearrange("(t p) n -> t p n", p=P)
        o_tiles = o_mix.rearrange("(t p) n -> t p n", p=P)
        quad = {n: a_of[n] // 4 for n in att}

        def wait_reader(eng, s):
            if s >= 2:
                kind, value = reader[s - 2]
                eng.wait_ge(masked if kind == "mask" else relu_done, value)

        def qk_before(n):
            return chunk0[n + 1]

        @block.sync
        def _(sp):
            def load(p):
                kind, t = p
                if kind == "A":
                    if t >= 1:
                        sp.wait_ge(split_done, prep_no[("A", t - 1)] + 1)
                    sp.dma_start(za[:, :], z_tiles[t, :, ZA:IN_COLS]).then_inc(za_ld, 16)
                else:
                    if t >= 1:
                        sp.wait_ge(split_done, prep_no[(kind, t - 1)] + 1)
                    c = COL["nq" if kind == "N" else "dq"]
                    sp.dma_start(zq[kind][:, :], z_tiles[t, :, c:c + 512]).then_inc(zq_ld[kind], 16)

            def swap(p):
                kind, t = p
                sp.wait_ge(evac_done, evac_no[(p, 1)])
                for half in range(2):
                    sp.dma_start(q_s[kind][half * HEAD:(half + 1) * HEAD].bitcast(F32), q_t[kind][(1 - half) * HEAD:(2 - half) * HEAD].bitcast(F32)).then_inc(swap_done[kind], 16)

            sp.dma_start(cst[:, :], consts).then_inc(const_ld, 16)
            for p in (("A", 0), ("N", 0), ("D", 0), ("A", 1)):
                load(p)
            swap(("N", 0))
            load(("N", 1))
            load(("A", 2))
            for n in range(N):
                kind, i, h = units[n]
                for p in pe_at.get(n, ()):
                    if p[0] != "A":
                        swap(p)
                    nxt = (p[0], p[1] + 1)
                    if nxt in prep_no:
                        load(nxt)
                if (kind, h) == ("C", 6) and i >= 1:
                    sp.wait_ge(acc_done, 8 * i)
                    sp.dma_start(o_tiles[i - 1], oacc[:, (i - 1) % 2]).then_inc(out_done[(i - 1) % 2], 16)
            sp.wait_ge(acc_done, 8 * TILES)
            sp.dma_start(o_tiles[TILES - 1], oacc[:, (TILES - 1) % 2]).then_inc(out_done[(TILES - 1) % 2], 16)
            for b in range(2):
                sp.wait_ge(out_done[b], 16 * (TILES // 2))

        @block.gpsimd
        def _(pool):
            owned = [0]

            def mine(ins):
                ins.then_inc(own, 1)
                owned[0] += 1
                return owned[0]

            def copies(pairs, waits=True):
                for h_, l_, x_ in pairs:
                    last = mine(pool.tensor_copy(h_, x_))
                pool.wait_ge(own, last)
                for h_, l_, x_ in pairs:
                    last = mine(pool.tensor_tensor(l_, x_, h_.bitcast(F32), ALU.subtract))
                return last

            def prep(p):
                kind, t = p
                m = prep_no[p]
                if m >= 1:
                    pool.wait_ge(prep_turned, m)
                if kind != "A":
                    pool.wait_ge(zq_ld[kind], 16 * (t + 1))
                    x = zq[kind][:, :].rearrange("p (h d) -> p h d", h=8)
                    last = copies([(split[:, 0:8, 0:HEAD], split[:, 0:8, HEAD:P], x)])
                else:
                    pool.wait_ge(za_ld, 16 * (t + 1))
                    if t >= RING:
                        pool.wait_ge(pv_done, last_group[where[("W", t - RING + W_TILES - 1, 7)]])

                    def part(name, heads, dim):
                        c = COL[name] - ZA
                        return za[:, c:c + heads * dim].rearrange("p (h d) -> p h d", h=heads)
                    ikx = part("ik", 1, IDX_DIM).broadcast_to([P, 2, IDX_DIM])
                    iks = split[:, 5, :].rearrange("p (a b d) -> p a b d", a=2, b=2)
                    iqx = part("iq", 8, IDX_DIM).unsqueeze(2).broadcast_to([P, 8, 2, IDX_DIM])
                    iqs = split[:, 6:14, :].rearrange("p h (a d) -> p h a d", a=4)
                    last = copies([
                        (split[:, 0:5, 0:HEAD], split[:, 0:5, HEAD:P], part("dk", 5, HEAD)),
                        (iks[:, :, 0, :], iks[:, :, 1, :], ikx),
                        (iqs[:, :, 0:2, :], iqs[:, :, 2:4, :], iqx),
                        (dv[:, t, 0, :], dv[:, t, 1, :], part("dv", 1, HEAD).rearrange("p h d -> p (h d)")),
                        (vsl[:, :, t, 0, :], vsl[:, :, t, 1, :], part("vsl", 2, HEAD)),
                        (vwn[:, :, t % RING, 0, :], vwn[:, :, t % RING, 1, :], part("vwn", 2, HEAD)),
                    ])
                    if t >= 2:
                        if t >= 4:
                            pool.wait_ge(index_done, relu0[where[("I", t - 2, 7)] + 1])
                        pool.wait_ge(fin_done, 2 * quad_end("S", t - 2))
                    last = mine(pool.tensor_copy(iw[:, t % 2], za[:, COL["iw"] - ZA:COL["iw"] - ZA + 8]))
                    pool.tensor_copy(gate[:, t % 2], za[:, COL["ng"] - ZA:COL["ng"] - ZA + 24]).then_inc(gate_in, 1)
                    pool.wait_ge(gate_in, t + 1)
                pool.wait_ge(own, last)
                pool.sem_inc(split_done, 1)

            def quad_end(kind, i):
                return quad[where[(kind, i, 7)]] + 1

            def accumulate(n):
                kind, i, h = units[n]
                q = quad[n]
                pool.wait_ge(fin_done, 2 * (q + 1))
                col = 256 * (h // 4) + (0 if kind == "D" else 512)
                dst = oacc[:, i % 2, col:col + 256]
                if kind in "CD":
                    if i >= 2 and kind == "C" and h == 3:
                        pool.wait_ge(out_done[i % 2], 16 * (i // 2))
                    pool.tensor_tensor(dst, fin[:, q % 2, 0], fin[:, q % 2, 1], ALU.add).then_inc(acc_done, 1)
                else:
                    pool.wait_ge(acc_done, q)
                    last = mine(pool.tensor_tensor(dst, dst, fin[:, q % 2, 0], ALU.add))
                    pool.wait_ge(own, last)
                    pool.tensor_tensor(dst, dst, fin[:, q % 2, 1], ALU.add).then_inc(acc_done, 1)

            def atleast_mask(t):
                w = (t + 1) * P
                pool.wait_ge(above_done, t - 1)
                pool.tensor_scalar(atleast[:, 0:w], index[t % 2][:, 0:w], lo, None, ALU.is_ge).then_inc(atleast_done, 1)
                pool.tensor_scalar(room, n_above, -1.0, float(TOPK), ALU.mult, ALU.add).then_inc(atleast_done, 1)

            def final_mask(t):
                w = (t + 1) * P
                if t >= 1:
                    pool.wait_ge(masked, mask0[where[("D", t - 1, 7)] + 1])
                if t < 2:
                    if t == 1:
                        last = mine(pool.memset(mask_d[:, 0:P], 0.0))
                        pool.wait_ge(own, last)
                    pool.tensor_copy(mask_d[:, t * P:w], const("diag", 0, P)).then_inc(mask_d_done, 1)
                else:
                    pool.wait_ge(kept_done, t - 1)
                    last = mine(pool.tensor_tensor(above[:, 0:w], above[:, 0:w], atleast[:, 0:w], ALU.add))
                    pool.wait_ge(own, last)
                    pool.tensor_scalar(mask_d[:, 0:w], above[:, 0:w], 0.5, MASKED, ALU.is_lt, ALU.mult).then_inc(mask_d_done, 1)

            def block_mask(i, g):
                w = (i + 1) * P
                if i >= 1:
                    pool.wait_ge(masked, mask0[where[("S", i - 1, 4 * g + 3)] + 1])
                pool.wait_ge(sel_done, 2 * i + g + 1)
                if i >= 1:
                    last = mine(pool.tensor_copy(mask_s[:, g, 0:i * P].rearrange("p (j k) -> p j k", k=SLC_BLOCK),
                                                 sel[:, g, 0:2 * i].unsqueeze(2).broadcast_to([P, 2 * i, SLC_BLOCK])))
                    pool.wait_ge(own, last)
                pool.tensor_copy(mask_s[:, g, i * P:w], const("diag", 0, P)).then_inc(mask_s_done, 1)

            def move_threshold(s, t, m):
                pool.wait_ge(count_a, s + 1)
                pool.wait_ge(count_v, s + 1)
                last = mine(pool.tensor_scalar(tmp1, cnt_a, -0.5, cnt_v, ALU.mult, ALU.add))
                pool.wait_ge(own, last)
                last = mine(pool.tensor_scalar(tmp2, tmp1, TOPK - 0.25 - act_part[t] / 2, -0.5, ALU.is_ge, ALU.add))
                pool.wait_ge(own, last)
                pool.tensor_scalar(thr, tmp2, halves[:, m:m + 1], thr, ALU.mult, ALU.add).then_inc(thr_moved, 1)

            pool.wait_ge(const_ld, 16)
            for p in preps[:3]:
                prep(p)
            for n in range(N):
                kind, i, h = units[n]
                for p in pool_at.get(n, ()):
                    prep(p)
                if kind == "C":
                    if h == 1 and i >= 2:
                        atleast_mask(i)
                    if h == 4:
                        final_mask(i)
                if kind == "W" and h == 0:
                    block_mask(i, 0)
                if kind == "W" and h == 1:
                    block_mask(i, 1)
                if n in steps:
                    move_threshold(*steps[n])
                m = n - 1
                if m >= 0 and m in a_of and units[m][2] % 4 == 3:
                    accumulate(m)
            accumulate(N - 1)

        @block.tensor
        def _(pe):
            turned = [0]

            def bank_free(m):
                if m >= 2:
                    kind, x, g = groups[m - 2]
                    if kind == "prep":
                        pe.wait_ge(evac_done, evac_no[(x, g)])
                    else:
                        pe.wait_ge(lo_done, att_group0[x] + g + 1)

            def prep(p):
                pe.wait_ge(split_done, prep_no[p] + 1)
                for g in range(len(EVACS[p[0]])):
                    m = group_no[("prep", p, g)]
                    bank_free(m)
                    blocks = range(4 * g, min(4 * g + 4, PREP_BLOCKS[p[0]]))
                    for b in blocks:
                        mm = pe.transpose(ps_t[m % 2][:, (b % 4) * P:(b % 4 + 1) * P], split[:, b, :].bitcast(F32), const("ident", 0, P))
                    mm.then_inc(group_turned, 1)
                pe.wait_ge(group_turned, group_no[("prep", p, len(EVACS[p[0]]) - 1)] + 1)
                pe.sem_inc(prep_turned, 1)

            def keys(kind, h, i, b0, nb):
                g = h // 4
                if kind == "C":
                    return kc[:, g, :]
                if kind == "W":
                    return kwn_t[:, g, b0 % RING:b0 % RING + nb, :]
                if kind == "S":
                    return ksl_t[:, g, b0 * P:(b0 + nb) * P]
                if kind == "D":
                    return dk_t[:, b0 * P:(b0 + nb) * P]
                return ik_t[:, b0 * P:(b0 + nb) * P]

            def qk(n):
                kind, i, h = units[n]
                first, _ = key_tiles(kind, i)
                if h == 0 or kind in "I":
                    if kind == "I":
                        pe.wait_ge(evac_done, evac_no[(("A", i), 3)])
                    elif kind != "C":
                        pe.wait_ge(evac_done, evac_no[(("A", i), 3)])
                    if kind == "C":
                        pe.wait_ge(evac_done, evac_no[(("N", i), 1)])
                        pe.wait_ge(swap_done["N"], 32 * (i + 1))
                    if kind == "D":
                        pe.wait_ge(evac_done, evac_no[(("D", i), 1)])
                        pe.wait_ge(swap_done["D"], 32 * (i + 1))
                for c, (col, w) in enumerate(chunks[n]):
                    s = chunk0[n] + c
                    wait_reader(pe, s)
                    out = ps_s[s % 2]
                    b = 0
                    while b < w // P:
                        t0 = first + col // P + b
                        nb = min(4 - b % 4, w // P - b)
                        if kind == "W":
                            nb = min(nb, RING - t0 % RING)
                        rhs = keys(kind, h, i, t0, nb)
                        dst = out[:, b * P:(b + nb) * P]
                        if kind == "I":
                            mm = pe.matmul(dst, iq_t[:, h, :], rhs, start=True, stop=True)
                        else:
                            q = "D" if kind == "D" else "N"
                            pe.matmul(dst, q_t[q][:, h, :], rhs, start=True, stop=False)
                            mm = pe.matmul(dst, q_s[q][:, h, :], rhs, start=False, stop=True)
                        b += nb
                    mm.then_inc(qk_done, 1)

            def values(kind, g, t):
                if kind == "C":
                    return vc[:, g, :]
                if kind == "W":
                    return vwn[:, g, t % RING].rearrange("p a d -> p (a d)")
                if kind == "S":
                    return vsl[:, g, t].rearrange("p a d -> p (a d)")
                return dv[:, t].rearrange("p a d -> p (a d)")

            def pv(n, g):
                kind, i, h = units[n]
                j = att_group0[n] + g
                first, nb = key_tiles(kind, i)
                q = quad[n]
                if g == 0 and h % 4 == 0 and q >= 2:
                    pe.wait_ge(fin_done, 2 * (q - 1))
                pe.wait_ge(lo_done, j + 1)
                out = ps_o[q % 2][:, (h % 4) * P:(h % 4 + 1) * P]
                for b in range(4 * g, min(4 * g + 4, nb)):
                    cols = slice((b % 4) * P, (b % 4 + 1) * P)
                    v = values(kind, h // 4, first + b)
                    pe.matmul(out, p_hi[:, j % PT_RING, cols], v, start=(b == 0), stop=False)
                    mm = pe.matmul(out, p_lo[:, j % PT_RING, cols], v, start=False, stop=(b == nb - 1))
                mm.then_inc(pv_done, 1)

            pe.wait_ge(const_ld, 16)
            for p in preps[:3]:
                prep(p)
            qk(0)
            qk(1)
            for n in range(N):
                for p in pe_at.get(n, ()):
                    prep(p)
                ng = 0
                if n in a_of:
                    a = a_of[n]
                    nb = width[n] // P
                    ng = (nb + 3) // 4
                    pe.wait_ge(exp_done, a + 1)
                    for g in range(ng):
                        m = group_no[("att", n, g)]
                        bank_free(m)
                        for b in range(4 * g, min(4 * g + 4, nb)):
                            mm = pe.transpose(ps_t[m % 2][:, (b % 4) * P:(b % 4 + 1) * P],
                                              scores[a % 2][:, b * P:(b + 1) * P], const("ident", 0, P))
                        mm.then_inc(group_turned, 1)
                        if g >= 1:
                            pv(n, g - 1)
                if n + 2 < N:
                    qk(n + 2)
                if ng:
                    pv(n, ng - 1)

        @block.scalar
        def _(act):
            def prep(p):
                kind, t = p
                cols = slice(t * P, (t + 1) * P)
                if kind == "A" and t >= 3:
                    act.wait_ge(qk_done, qk_before(where[("I", t - 1, 7)]))
                if kind == "A" and t >= RING:
                    act.wait_ge(qk_done, qk_before(where[("W", t - RING + W_TILES - 1, 7)]))
                if kind != "A" and t >= 1:
                    act.wait_ge(qk_done, qk_before(where[("S" if kind == "N" else "D", t - 1, 7)]))
                    act.wait_ge(swap_done[kind], 32 * t)
                dest = {"dk": lambda b, nb: dk_t[:, cols], "ksl": lambda b, nb: ksl_t[:, :, cols],
                        "kwn0": lambda b, nb: kwn_t[:, 0, t % RING, :], "kwn1": lambda b, nb: kwn_t[:, 1, t % RING, :],
                        "ik": lambda b, nb: ik_t[:, cols], "iq": lambda b, nb: iq_t[:, b - 6:b - 6 + nb, :],
                        "nq": lambda b, nb: q_t["N"][:, b:b + nb, :], "dq": lambda b, nb: q_t["D"][:, b:b + nb, :]}
                for g, ops in enumerate(EVACS[kind]):
                    m = group_no[("prep", p, g)]
                    act.wait_ge(group_turned, m + 1)
                    for b, nb, name in ops:
                        src = ps_t[m % 2][:, (b % 4) * P:(b % 4 + nb) * P]
                        if nb > 1:
                            src = src.rearrange("p (b k) -> p b k", b=nb)
                        act.activation(dest[name](b, nb), src, ACT.Copy).then_inc(evac_done, 1)
                if kind == "A":
                    act.wait_ge(gate_in, t + 1)
                    act.activation(gate[:, t % 2], gate[:, t % 2], ACT.Exp, scale=-1.0).then_inc(gate_exp, 1)

            def head(n):
                kind, i, h = units[n]
                if kind == "I":
                    for c, (col, w) in enumerate(chunks[n]):
                        r = relu0[n] + c
                        act.wait_ge(qk_done, chunk0[n] + c + 1)
                        if r >= 2:
                            act.wait_ge(index_done, r - 1)
                        act.activation(relu[:, r % 2, 0:w], ps_s[(chunk0[n] + c) % 2][:, 0:w], ACT.Relu).then_inc(relu_done, 1)
                    return
                a, w = a_of[n], width[n]
                act.wait_ge(masked, mask0[n + 1])
                if h % 4 == 0 and quad[n] >= 2:
                    act.wait_ge(fin_done, 2 * (quad[n] - 1))
                act.activation(scores[a % 2][:, 0:w], scores[a % 2][:, 0:w], ACT.Exp, bias=nmax[:, a % 4, len(chunks[n]) - 1:len(chunks[n])],
                               scale=-1.0, accum_out=lsum[:, quad[n] % 2, h % 4:h % 4 + 1]).then_inc(exp_done, 1)

            for p in preps[:3]:
                prep(p)
            head(0)
            for n in range(N):
                for p in pe_at.get(n, ()):
                    prep(p)
                if n in a_of:
                    ng = (width[n] // P + 3) // 4
                    for g in range(ng):
                        j = att_group0[n] + g
                        m = group_no[("att", n, g)]
                        w = min(512, width[n] - 512 * g)
                        act.wait_ge(group_turned, m + 1)
                        if j >= PT_RING:
                            act.wait_ge(pv_done, j - PT_RING + 1)
                        act.activation(p_hi[:, j % PT_RING, 0:w], ps_t[m % 2][:, 0:w], ACT.Copy).then_inc(hi_done, 1)
                if n + 1 < N:
                    head(n + 1)
                if n in steps:
                    s, t, m = steps[n]
                    act.wait_ge(search_set, t - 1)
                    if m >= 1:
                        act.wait_ge(thr_moved, s)
                    act.activation(junk_a[:, 0:act_part[t]], index[t % 2][:, 0:act_part[t]], ACT.Sign, bias=thr, scale=-1.0,
                                   accum_out=cnt_a).then_inc(count_a, 1)

        @block.vector
        def _(dve):
            owned = [0]

            def mine(ins):
                ins.then_inc(vec, 1)
                owned[0] += 1

            def settle():
                dve.wait_ge(vec, owned[0])

            def low(n, g):
                j = att_group0[n] + g
                m = group_no[("att", n, g)]
                w = min(512, width[n] - 512 * g)
                dve.wait_ge(hi_done, j + 1)
                dve.tensor_tensor(p_lo[:, j % PT_RING, 0:w], ps_t[m % 2][:, 0:w], p_hi[:, j % PT_RING, 0:w].bitcast(F32),
                                  ALU.subtract).then_inc(lo_done, 1)

            def mask(n, c):
                kind, i, h = units[n]
                a = a_of[n]
                col, w = chunks[n][c]
                s = chunk0[n] + c
                if c == 0:
                    if a >= 2:
                        last = att[a - 2]
                        dve.wait_ge(group_turned, group_no[("att", last, (width[last] // P + 3) // 4 - 1)] + 1)
                    if kind == "S" and h % 4 == 0:
                        dve.wait_ge(mask_s_done, 2 * i + h // 4 + 1)
                    if kind == "D" and h == 0:
                        dve.wait_ge(mask_d_done, i + 1)
                    if a >= 4:
                        dve.wait_ge(exp_done, a - 3)
                dve.wait_ge(qk_done, s + 1)
                m = {"C": lambda: const("cmp", 120 - 8 * i, P),
                     "W": lambda: const("win", W_TILES * P - w, w),
                     "S": lambda: mask_s[:, h // 4, col:col + w],
                     "D": lambda: mask_d[:, col:col + w]}[kind]()
                if c:
                    dve.wait_ge(masked, mask0[n] + c)
                start = nmax[:, a % 4, c - 1:c] if c else (1e20 if kind == "C" else 3e38)
                dve.tensor_tensor_reduce(scores[a % 2][:, col:col + w], ps_s[s % 2][:, 0:w], m, -SCALE, start, ALU.add, ALU.min,
                                         nmax[:, a % 4, c:c + 1]).then_inc(masked, 1)

            def index_unit(n):
                kind, t, h = units[n]
                for c, (col, w) in enumerate(chunks[n]):
                    r = relu0[n] + c
                    dve.wait_ge(relu_done, r + 1)
                    dst = index[t % 2][:, col:col + w]
                    weight = iw[:, t % 2, h:h + 1]
                    if h == 0:
                        if t >= 4 and c == 0:
                            dve.wait_ge(kept_done, t - 3)
                        dve.tensor_scalar(dst, relu[:, r % 2, 0:w], weight, None, ALU.mult).then_inc(index_done, 1)
                    else:
                        dve.wait_ge(index_done, r - len(chunks[n]) + 1)
                        dve.scalar_tensor_tensor(dst, relu[:, r % 2, 0:w], weight, dst, ALU.mult, ALU.add).then_inc(index_done, 1)

            def set_search(n):
                kind, t, h = units[n]
                w = (t + 1) * P
                x = index[t % 2]
                dve.wait_ge(index_done, relu0[n + 1])
                mine(dve.tensor_reduce(amax, x[:, 0:w], AX.X, ALU.max, apply_absolute_value=True))
                settle()
                mine(dve.tensor_tensor(x[:, t * P:w], x[:, t * P:w], const("diag", 0, P), ALU.add))
                mine(dve.tensor_scalar(amax.bitcast(I32), amax.bitcast(I32), 0x7F800000, None, ALU.bitwise_and))
                mine(dve.memset(thr, 0.0))
                settle()
                dve.tensor_scalar(halves[:, :], const("halve", 0, NSTEP + 1), amax, None, ALU.mult).then_inc(search_set, 1)

            def count(s, t, m):
                dve.wait_ge(search_set, t - 1)
                if m >= 1:
                    dve.wait_ge(thr_moved, s)
                a, w = act_part[t], (t + 1) * P
                dve.tensor_scalar(junk_v[:, 0:w - a], index[t % 2][:, a:w], thr, None, ALU.is_ge, ALU.add, accum_out=cnt_v).then_inc(count_v, 1)

            def above_mask(t):
                w = (t + 1) * P
                dve.wait_ge(thr_moved, (t - 1) * NSTEP)
                mine(dve.tensor_tensor(hi, thr, halves[:, NSTEP:NSTEP + 1], ALU.add))
                mine(dve.tensor_tensor(lo, thr, halves[:, NSTEP:NSTEP + 1], ALU.subtract))
                settle()
                if t >= 3:
                    dve.wait_ge(mask_d_done, t)
                dve.tensor_scalar(above[:, 0:w], index[t % 2][:, 0:w], hi, None, ALU.is_gt, ALU.add, accum_out=n_above).then_inc(above_done, 1)

            def kept_mask(t):
                w = (t + 1) * P
                dve.wait_ge(atleast_done, 2 * (t - 1))
                x = index[t % 2][:, 0:w]
                mine(dve.tensor_tensor_scan(x, atleast[:, 0:w], above[:, 0:w], 0.0, ALU.add, ALU.subtract))
                settle()
                dve.scalar_tensor_tensor(atleast[:, 0:w], x, room, atleast[:, 0:w], ALU.is_le, ALU.mult).then_inc(kept_done, 1)

            def importance(n):
                kind, i, h = units[n]
                a, q = a_of[n], quad[n]
                dve.wait_ge(exp_done, a + 1)
                r = rsum[:, q % 2, h % 4:h % 4 + 1]
                mine(dve.tensor_scalar(r, lsum[:, q % 2, h % 4:h % 4 + 1], 1e-30, None, ALU.max))
                settle()
                mine(dve.reciprocal(r, r))
                settle()
                pr = scores[a % 2][:, 0:P]
                if h % 4 == 0:
                    mine(dve.tensor_scalar(imp_c[:, 1:P + 1], pr, r, None, ALU.mult))
                else:
                    mine(dve.scalar_tensor_tensor(imp_c[:, 1:P + 1], pr, r, imp_c[:, 1:P + 1], ALU.mult, ALU.add))
                settle()

            def select(i, g):
                x, y = imp[:, 0, :], imp[:, 1, :]
                mine(dve.tensor_reduce(x, imp_c[:, 1:P + 1].rearrange("p (j c) -> p j c", c=4), AX.X, ALU.add))
                settle()
                mine(dve.tensor_tensor(x, x, imp_c[:, 0:P:4], ALU.add))
                settle()
                mine(dve.tensor_tensor(x, x, const("keep", 30 - 2 * i, N_SLC), ALU.mult))
                settle()
                mine(dve.tensor_tensor(x, x, const("add", 30 - 2 * i, N_SLC), ALU.add))
                settle()
                mine(dve.memset(x[:, 0:1], 1.0e4))
                settle()
                mine(dve.max(top8[:, :], x))
                settle()
                mine(dve.match_replace(y, top8[:, :], x, -5.0))
                settle()
                if i >= 1:
                    dve.wait_ge(mask_s_done, 2 * i)
                dve.tensor_scalar(sel[:, g, :], y, -4.0, MASKED, ALU.is_gt, ALU.mult).then_inc(sel_done, 1)

            def finish(n):
                kind, i, h = units[n]
                q = quad[n]
                h0 = h - 3
                dve.wait_ge(exp_done, a_of[n] + 1)
                r = rsum[:, q % 2, :]
                if kind != "C":
                    mine(dve.reciprocal(r, lsum[:, q % 2, :]))
                    settle()
                if kind != "D":
                    if kind == "C" and h == 3:
                        dve.wait_ge(gate_done, i + 1)
                    b = "CSW".index(kind)
                    mine(dve.tensor_tensor(rgate[:, q % 2, :], r, gate[:, i % 2, 3 * h0 + b:3 * h0 + b + 10:3], ALU.mult))
                    settle()
                    r = rgate[:, q % 2, :]
                dve.wait_ge(pv_done, last_group[n])
                if q >= 2:
                    dve.wait_ge(acc_done, q - 1)
                o = ps_o[q % 2][:, :].rearrange("p (h a d) -> p h a d", h=4, a=2)
                for part in range(2):
                    dve.tensor_tensor(fin[:, q % 2, part].rearrange("p (h d) -> p h d", h=4), o[:, :, part, :],
                                      r.unsqueeze(2).broadcast_to([P, 4, HEAD]), ALU.mult).then_inc(fin_done, 1)

            def gates(t):
                dve.wait_ge(gate_exp, t + 1)
                mine(dve.tensor_scalar(gate[:, t % 2], gate[:, t % 2], 1.0, None, ALU.add))
                settle()
                dve.reciprocal(gate[:, t % 2], gate[:, t % 2]).then_inc(gate_done, 1)

            mine(dve.memset(imp_c[:, 0:1], 0.0))
            settle()
            dve.wait_ge(const_ld, 16)
            gates(0)
            gates(1)
            for c in range(len(chunks[0])):
                mask(0, c)
            for n in range(N):
                kind, i, h = units[n]
                ng = (width[n] // P + 3) // 4 if n in a_of else 0
                todo = list(range(len(chunks[n + 1]))) if n + 1 in a_of else []
                for g in range(ng):
                    low(n, g)
                    if todo and g % 2 == 0:
                        mask(n + 1, todo.pop(0))
                for c in todo:
                    mask(n + 1, c)
                if n + 1 < N and n + 1 not in a_of:
                    index_unit(n + 1)
                    if units[n + 1][2] == IDX_HEADS - 1:
                        set_search(n + 1)
                if kind == "C":
                    importance(n)
                    if h % 4 == 3:
                        select(i, h // 4)
                    if i >= 2 and h == 0:
                        above_mask(i)
                    if i >= 2 and h == 3:
                        kept_mask(i)
                for p in pe_at.get(n, ()):
                    if p[0] == "A":
                        gates(p[1])
                m = n - 1
                if m >= 0 and m in a_of and units[m][2] % 4 == 3:
                    finish(m)
                if n in steps:
                    count(*steps[n])
            finish(N - 1)


def constants():
    q = np.arange(P)[:, None]
    out = {"ident": np.eye(P)}
    out["diag"] = np.where(np.arange(P)[None] > q, MASKED, 0.0)
    d = q - (np.arange(W_TILES * P)[None] - WINDOW)
    out["win"] = np.where((d >= 0) & (d < WINDOW), 0.0, MASKED)
    c = np.arange(248)[None] - 120
    out["cmp"] = np.where(CMP_STRIDE * c + CMP_BLOCK - 1 <= q, 0.0, MASKED)
    j = np.arange(62)[None] - 30
    cur = q // SLC_BLOCK
    forced = (j == cur) | (j == cur - 1)
    out["keep"] = np.where((j > cur) | forced, 0.0, 1.0)
    out["add"] = np.where(forced, 1.0e4, np.where(j > cur, -1.0, 0.0))
    out["halve"] = np.broadcast_to(2.0 ** (1.0 - np.arange(NSTEP + 1)), (P, NSTEP + 1))
    return np.ascontiguousarray(np.concatenate([out[n] for n, _ in CONST], axis=1).astype(np.float32))


def mixing_phase(nc, x, o_mix, gain, w_out, ln_g, ln_b, ident_in, h, h_t):
    HALF = D_MODEL // 2
    with ExitStack() as ctx:
        def sb(name, shape, dt=F32):
            return ctx.enter_context(nc.sbuf_tensor(name, shape, dt))

        def sem(name):
            return ctx.enter_context(nc.semaphore(name))

        def psum(name, cols):
            return ctx.enter_context(nc.psum_tensor(name, [P, cols], F32))

        w_hi = sb("m_w_hi", [P, KT, D_MODEL], F32R)
        w_lo = sb("m_w_lo", [P, KT, D_MODEL], F32R)
        w_raw = sb("m_w_raw", [P, 2, D_MODEL])
        ident = sb("m_ident", [P, P])
        gain_b = sb("m_gain", [P, D_MODEL])
        g_b = sb("m_ln_g", [P, D_MODEL])
        b_b = sb("m_ln_b", [P, D_MODEL])
        o_in = sb("m_o_in", [P, 2, D_MODEL])
        on = sb("m_on", [P, 2, D_MODEL])
        junk = sb("m_junk", [P, HALF])
        ot_hi = sb("m_ot_hi", [P, 2, KT, P], F32R)
        ot_lo = sb("m_ot_lo", [P, 2, KT, P], F32R)
        x_in = sb("m_x_in", [P, 2, D_MODEL])
        hp = sb("m_hp", [P, 2, D_MODEL])
        hn = sb("m_hn", [P, 2, D_MODEL])
        ho = sb("m_ho", [P, 2, D_MODEL])
        ht = sb("m_ht", [P, 2, KT, P])
        ssq = sb("m_ssq", [P, 2, 2])
        rinv = sb("m_rinv", [P, 2, 2])
        stats = sb("m_stats", [P, 2, 6])
        aggr = sb("m_aggr", [P, 2, 2])
        rstd = sb("m_rstd", [P, 2, 1])
        nmr = sb("m_nmr", [P, 2, 1])
        power = sb("m_power", [P, 2])
        eps = sb("m_eps", [P, 2])
        minus = sb("m_minus", [P, 1])
        t_o = psum("m_t_o", D_MODEL)
        ys = [psum(f"m_y{b}", D_MODEL) for b in range(2)]
        t_h = psum("m_t_h", D_MODEL)

        small_ld = sem("m_small_ld")
        w_ld = [sem(f"m_w_ld{b}") for b in range(2)]
        w_hi_done = sem("m_w_hi_done")
        w_lo_done = sem("m_w_lo_done")
        o_ld = [sem(f"m_o_ld{b}") for b in range(2)]
        x_ld = [sem(f"m_x_ld{b}") for b in range(2)]
        squared = sem("m_squared")
        rinv_done = sem("m_rinv_done")
        scaled = sem("m_scaled")
        o_turned = sem("m_o_turned")
        hi_done = sem("m_hi_done")
        lo_done = sem("m_lo_done")
        y_full = sem("m_y_full")
        added = sem("m_added")
        aggr_done = sem("m_aggr_done")
        rstd_done = sem("m_rstd_done")
        normed = sem("m_normed")
        gained = sem("m_gained")
        h_done = sem("m_h_done")
        h_turned = sem("m_h_turned")
        ht_done = sem("m_ht_done")
        h_out = [sem(f"m_h_out{b}") for b in range(2)]
        ht_out = [sem(f"m_ht_out{b}") for b in range(2)]
        own = sem("m_pool_own")
        fixed_set = sem("m_fixed_set")
        vec = sem("m_vec")
        block = ctx.enter_context(nc.Block())

        x_tiles = x.rearrange("(t p) n -> t p n", p=P)
        o_tiles = o_mix.rearrange("(t p) n -> t p n", p=P)
        h_tiles = h.rearrange("(t p) n -> t p n", p=P)
        ht_cols = h_t.rearrange("(k p) n -> p k n", p=P)
        w_rows = w_out.rearrange("(k p) n -> k p n", p=P)

        def tile_of(ap, t):
            return ap[bass.ds(t, 1), :, :].rearrange("o p n -> (o p) n")

        def reached(eng, s, value):
            if not isinstance(value, int) or value > 0:
                eng.wait_ge(s, value)

        def run_steps(eng, step):
            for t in range(3):
                step(t, t % 2, True, True)
            with eng.Fori(0, (TILES - 6) // 2) as i:
                for d in range(2):
                    step(2 * i + 3 + d, (3 + d) % 2, True, True)
            for t in range(TILES - 3, TILES):
                step(t, t % 2, t + 2 < TILES, t + 1 < TILES)

        @block.sync
        def _(sp):
            def load_o(t, u):
                reached(sp, scaled, 2 * (t - 1))
                sp.dma_start(o_in[:, u], tile_of(o_tiles, t)).then_inc(o_ld[u], 16)

            def load_x(t, u):
                reached(sp, added, t - 1)
                sp.dma_start(x_in[:, u], tile_of(x_tiles, t)).then_inc(x_ld[u], 16)

            def store(t, u):
                sp.wait_ge(h_done, t + 1)
                sp.dma_start(tile_of(h_tiles, t), ho[:, u]).then_inc(h_out[u], 16)
                sp.wait_ge(ht_done, 2 * (t + 1))
                sp.dma_start(ht_cols[:, :, bass.ds(t * P, P)], ht[:, u]).then_inc(ht_out[u], 16)

            for dst, src in ((ident, ident_in), (gain_b, gain.broadcast_to([P, D_MODEL])),
                             (g_b, ln_g.broadcast_to([P, D_MODEL])), (b_b, ln_b.broadcast_to([P, D_MODEL]))):
                sp.dma_start(dst[:, :], src).then_inc(small_ld, 16)
            for t in range(2):
                load_o(t, t)
            for k in range(KT):
                if k >= 2:
                    sp.wait_ge(w_lo_done, k - 1)
                sp.dma_start(w_raw[:, k % 2], w_rows[k]).then_inc(w_ld[k % 2], 16)
            for t in range(2):
                load_x(t, t)

            def step(t, u, two, one):
                if two:
                    load_o(t + 2, u)
                    load_x(t + 2, u)
                if not isinstance(t, int) or t >= 1:
                    store(t - 1, 1 - u)

            run_steps(sp, step)
            store(TILES - 1, (TILES - 1) % 2)
            for b in range(2):
                sp.wait_ge(h_out[b], 16 * (TILES // 2))
                sp.wait_ge(ht_out[b], 16 * (TILES // 2))

        @block.gpsimd
        def _(pool):
            for c, value in ((power, -0.5), (eps, LN_EPS), (minus, -1.0)):
                pool.memset(c[:, :], value).then_inc(fixed_set, 1)

            def root_ln(t, u):
                pool.wait_ge(aggr_done, t + 1)
                reached(pool, normed, t - 1)
                pool.tensor_tensor(rstd[:, u], aggr[:, u, 1:2], eps[:, 0:1], ALU.add).then_inc(rstd_done, 1)
                pool.tensor_tensor(nmr[:, u], aggr[:, u, 0:1], minus[:, :], ALU.mult).then_inc(rstd_done, 1)
                pool.wait_ge(rstd_done, 4 * t + 2)
                pool.tensor_tensor(rstd[:, u], rstd[:, u], power[:, 0:1], ALU.pow).then_inc(rstd_done, 1)
                pool.wait_ge(rstd_done, 4 * t + 3)
                pool.tensor_tensor(nmr[:, u], nmr[:, u], rstd[:, u], ALU.mult).then_inc(rstd_done, 1)

            def add_b(t, u):
                pool.wait_ge(gained, t + 1)
                if not isinstance(t, int) or t >= 2:
                    pool.wait_ge(h_out[u], (t - u) * 8)
                    pool.wait_ge(h_turned, 2 * (t - 1))
                pool.tensor_tensor(ho[:, u], hn[:, u], b_b[:, :], ALU.add).then_inc(h_done, 1)

            pool.wait_ge(fixed_set, 3)
            for t in range(2):
                pool.wait_ge(squared, 2 * (t + 1))
                pool.tensor_tensor(rinv[:, t], ssq[:, t], eps[:, :], ALU.add).then_inc(own, 1)
                pool.wait_ge(own, t + 1)
                pool.tensor_tensor(rinv[:, t], rinv[:, t], power[:, :], ALU.pow).then_inc(rinv_done, 1)

            def step(t, u, two, one):
                if two:
                    pool.wait_ge(squared, 2 * (t + 3))
                    pool.wait_ge(scaled, 2 * (t + 1))
                    pool.tensor_tensor(rinv[:, u], ssq[:, u], eps[:, :], ALU.add).then_inc(own, 1)
                    pool.wait_ge(own, t + 3)
                    pool.tensor_tensor(rinv[:, u], rinv[:, u], power[:, :], ALU.pow).then_inc(rinv_done, 1)
                root_ln(t, u)
                add_b(t, u)

            run_steps(pool, step)

        @block.tensor
        def _(pe):
            def turn_o(t, u):
                pe.wait_ge(scaled, 2 * (t + 1))
                reached(pe, lo_done, 2 * t)
                for half in range(2):
                    for k in range(4 * half, 4 * half + 4):
                        mm = pe.transpose(t_o[:, k * P:(k + 1) * P], on[:, u, k * P:(k + 1) * P], ident[:, :])
                    mm.then_inc(o_turned, 1)

            def project(t, u):
                pe.wait_ge(lo_done, 2 * (t + 1))
                reached(pe, added, t - 1)
                for half in range(2):
                    for k in range(KT):
                        for n, (a, w) in enumerate(((ot_hi, w_hi), (ot_hi, w_lo), (ot_lo, w_hi))):
                            mm = pe.matmul(ys[u][:, half * HALF:(half + 1) * HALF], a[:, u, k], w[:, k, half * HALF:(half + 1) * HALF],
                                           start=(k == 0 and n == 0), stop=(k == KT - 1 and n == 2))
                mm.then_inc(y_full, 1)

            def turn_h(t, u):
                pe.wait_ge(h_done, t + 1)
                reached(pe, ht_done, 2 * t)
                for half in range(2):
                    for k in range(4 * half, 4 * half + 4):
                        mm = pe.transpose(t_h[:, k * P:(k + 1) * P], ho[:, u, k * P:(k + 1) * P], ident[:, :])
                    mm.then_inc(h_turned, 1)

            pe.wait_ge(small_ld, 64)
            turn_o(0, 0)
            pe.wait_ge(w_lo_done, KT)

            def step(t, u, two, one):
                if one:
                    turn_o(t + 1, 1 - u)
                project(t, u)
                if not isinstance(t, int) or t >= 1:
                    turn_h(t - 1, 1 - u)

            run_steps(pe, step)
            turn_h(TILES - 1, (TILES - 1) % 2)

        @block.scalar
        def _(act):
            def square(t, u):
                act.wait_ge(o_ld[u], (t - u + 2) * 8)
                reached(act, rinv_done, t - 1)
                for half in range(2):
                    if not isinstance(t, int) or 2 * t + half >= 1:
                        act.wait_ge(squared, 2 * t + half)
                    act.activation(junk[:, :], o_in[:, u, half * HALF:(half + 1) * HALF], ACT.Square, scale=HALF ** -0.5,
                                   accum_out=ssq[:, u, half:half + 1]).then_inc(squared, 1)

            def high(t, u):
                reached(act, y_full, t - 1)
                for half in range(2):
                    act.wait_ge(o_turned, 2 * t + half + 1)
                    act.activation(ot_hi[:, u, 4 * half:4 * half + 4], t_o[:, half * HALF:(half + 1) * HALF].rearrange("p (k n) -> p k n", k=4),
                                   ACT.Copy).then_inc(hi_done, 1)

            def norm(t, u):
                act.wait_ge(rstd_done, 4 * (t + 1))
                act.wait_ge(added, t + 1)
                reached(act, gained, t - 1)
                act.activation(hp[:, u], hp[:, u], ACT.Identity, bias=nmr[:, u], scale=rstd[:, u]).then_inc(normed, 1)

            def copy_h(t, u):
                if not isinstance(t, int) or t >= 2:
                    act.wait_ge(ht_out[u], (t - u) * 8)
                for half in range(2):
                    act.wait_ge(h_turned, 2 * t + half + 1)
                    act.activation(ht[:, u, 4 * half:4 * half + 4], t_h[:, half * HALF:(half + 1) * HALF].rearrange("p (k n) -> p k n", k=4),
                                   ACT.Copy).then_inc(ht_done, 1)

            square(0, 0)
            square(1, 1)
            high(0, 0)
            for k in range(KT):
                act.wait_ge(w_ld[k % 2], 16 * (k // 2 + 1))
                act.activation(w_hi[:, k], w_raw[:, k % 2], ACT.Copy).then_inc(w_hi_done, 1)

            def step(t, u, two, one):
                if two:
                    square(t + 2, u)
                if one:
                    high(t + 1, 1 - u)
                norm(t, u)
                if not isinstance(t, int) or t >= 1:
                    copy_h(t - 1, 1 - u)

            run_steps(act, step)
            copy_h(TILES - 1, (TILES - 1) % 2)

        @block.vector
        def _(dve):
            def scale(t, u):
                dve.wait_ge(rinv_done, t + 1)
                reached(dve, o_turned, 2 * (t - 1))
                for half in range(2):
                    c = slice(half * HALF, (half + 1) * HALF)
                    dve.scalar_tensor_tensor(on[:, u, c], o_in[:, u, c], rinv[:, u, half:half + 1], gain_b[:, c], ALU.mult, ALU.mult).then_inc(scaled, 1)

            def low(t, u):
                for half in range(2):
                    dve.wait_ge(hi_done, 2 * t + half + 1)
                    dve.tensor_tensor(ot_lo[:, u, 4 * half:4 * half + 4], t_o[:, half * HALF:(half + 1) * HALF].rearrange("p (k n) -> p k n", k=4),
                                      ot_hi[:, u, 4 * half:4 * half + 4].bitcast(F32), ALU.subtract).then_inc(lo_done, 1)

            def add_x(t, u):
                dve.wait_ge(y_full, t + 1)
                dve.wait_ge(x_ld[u], (t - u + 2) * 8)
                reached(dve, gained, t - 1)
                dve.scalar_tensor_tensor(hp[:, u], x_in[:, u], ALPHA, ys[u][:, :], ALU.mult, ALU.add).then_inc(added, 1)
                dve.wait_ge(added, t + 1)
                reached(dve, aggr_done, t)
                reached(dve, rstd_done, 4 * (t - 1))
                for half in range(2):
                    dve.bn_stats(stats[:, half], hp[:, u, half * HALF:(half + 1) * HALF]).then_inc(vec, 1)
                dve.wait_ge(small_ld, 64)
                dve.wait_ge(vec, 2 * (t + 1))
                dve.bn_aggr(aggr[:, u], stats[:, :, :].rearrange("p a s -> p (a s)")).then_inc(aggr_done, 1)

            def gains(t, u):
                dve.wait_ge(normed, t + 1)
                reached(dve, h_done, t - 1)
                dve.tensor_tensor(hn[:, u], hp[:, u], g_b[:, :], ALU.mult).then_inc(gained, 1)

            dve.wait_ge(small_ld, 64)
            scale(0, 0)
            scale(1, 1)
            low(0, 0)
            for k in range(KT):
                dve.wait_ge(w_hi_done, k + 1)
                dve.tensor_tensor(w_lo[:, k], w_raw[:, k % 2], w_hi[:, k].bitcast(F32), ALU.subtract).then_inc(w_lo_done, 1)

            def step(t, u, two, one):
                if two:
                    scale(t + 2, u)
                if one:
                    low(t + 1, 1 - u)
                add_x(t, u)
                gains(t, u)

            run_steps(dve, step)


GROUP = 512
N_GROUPS = SEQ // GROUP
FT = FFN // P
DOWN = FT // 2


def ffn_phase(nc, h, h_t, w_gate, w_up, w_down, ln_g, ln_b, out):
    NB = GROUP // P
    HALF = D_MODEL // 2
    W_PER = 2 * FT + 2 * DOWN
    NX = KT * GROUP // D_MODEL
    X_AFTER = {2: 0, 6: 1, 13: 2, 17: 3}
    S_PER = W_PER + NX

    def raw_of_down(d, last):
        return d if last else d + sum(1 for k in X_AFTER if k < d)

    with ExitStack() as ctx:
        def sb(name, shape, dt=F32):
            return ctx.enter_context(nc.sbuf_tensor(name, shape, dt))

        def sem(name):
            return ctx.enter_context(nc.semaphore(name))

        def psum(name, cols):
            return ctx.enter_context(nc.psum_tensor(name, [P, cols], F32))

        raw = sb("f_raw", [P, 2, D_MODEL])
        w_hi = sb("f_w_hi", [P, 2, D_MODEL], F32R)
        w_lo = sb("f_w_lo", [P, 2, D_MODEL], F32R)
        x_hi = sb("f_x_hi", [P, KT, GROUP], F32R)
        x_lo = sb("f_x_lo", [P, KT, GROUP], F32R)
        silu = sb("f_silu", [P, 2, GROUP])
        prod = sb("f_prod", [P, 2, GROUP])
        g_hi = sb("f_g_hi", [P, FT, GROUP], F32R)
        g_lo = sb("f_g_lo", [P, FT, GROUP], F32R)
        y = sb("f_y", [P, NB, D_MODEL])
        g_b = sb("f_ln_g", [P, D_MODEL])
        b_b = sb("f_ln_b", [P, D_MODEL])
        stats = sb("f_stats", [P, 2, 6])
        aggr = sb("f_aggr", [P, NB, 2])
        rstd = sb("f_rstd", [P, NB])
        nmr = sb("f_nmr", [P, NB])
        power = sb("f_power", [P, 1])
        eps = sb("f_eps", [P, 1])
        minus = sb("f_minus", [P, 1])
        mark = sb("f_mark", [P, 1])
        gate_ps = [psum(f"f_gate{b}", GROUP) for b in range(2)]
        up_ps = [psum(f"f_up{b}", GROUP) for b in range(2)]
        acc = [psum(f"f_acc{b}", HALF) for b in range(NB)]

        small_ld = sem("f_small_ld")
        raw_ld = [sem(f"f_raw_ld{b}") for b in range(2)]
        y_ld = sem("f_y_ld")
        hi_done = sem("f_hi_done")
        lo_done = sem("f_lo_done")
        used = sem("f_used")
        silu_done = sem("f_silu_done")
        prod_done = sem("f_prod_done")
        g_hi_done = sem("f_g_hi_done")
        g_lo_done = sem("f_g_lo_done")
        added = sem("f_added")
        stats_done = sem("f_stats_done")
        aggr_done = sem("f_aggr_done")
        rstd_done = sem("f_rstd_done")
        normed = sem("f_normed")
        gained = sem("f_gained")
        y_done = sem("f_y_done")
        y_out = sem("f_y_out")
        fixed_set = sem("f_fixed_set")
        marked = sem("f_marked")
        block = ctx.enter_context(nc.Block())

        gate_cols = w_gate.rearrange("(k p) n -> p k n", p=P)
        up_cols = w_up.rearrange("(k p) n -> p k n", p=P)
        down_rows = w_down.rearrange("(f p) n -> p f n", p=P)
        xt_rows = h_t.rearrange("(k p) n -> p k n", p=P)
        h_rows = h.rearrange("(g t p) n -> g p t n", p=P, t=NB)
        out_rows = out.rearrange("(g t p) n -> g p t n", p=P, t=NB)

        def over_groups(eng, body):
            body(0, True, False)
            with eng.Fori(1, N_GROUPS - 1) as g:
                body(g, False, False)
            body(N_GROUPS - 1, False, True)

        @block.sync
        def _(sp):
            def load(s, parity, src, shape=None):
                if not isinstance(s, int) or s >= 2:
                    sp.wait_ge(lo_done, s - 1)
                dst = raw[:, parity]
                if shape:
                    dst = dst.rearrange("p (a n) -> p a n", a=shape)
                sp.dma_start(dst, src).then_inc(raw_ld[parity], 16)

            def load_x(s, parity, g, n):
                load(s, parity, xt_rows[:, 2 * n:2 * n + 2, bass.ds(g * GROUP, GROUP)], 2)

            for dst, src in ((g_b, ln_g.broadcast_to([P, D_MODEL])), (b_b, ln_b.broadcast_to([P, D_MODEL]))):
                sp.dma_start(dst[:, :], src).then_inc(small_ld, 16)
            for n in range(NX):
                load_x(n, n % 2, 0, n)

            def store(g):
                sp.wait_ge(y_done, NB * (g + 1))
                sp.dma_start(out_rows[bass.ds(g, 1), :, :, :].rearrange("o p t n -> (o p) t n"), y[:, :, :]).then_inc(y_out, 16)

            def body(g, first, last):
                s0 = NX + g * S_PER
                with sp.Fori(0, FT) as f:
                    for m, cols in enumerate((gate_cols, up_cols)):
                        load(s0 + 2 * f + m, m, cols[:, :, bass.ds(f * P, P)], KT)
                if not first:
                    store(g - 1)
                    sp.wait_ge(y_out, 16 * g)
                sp.dma_start(y[:, :, :], h_rows[bass.ds(g, 1), :, :, :].rearrange("o p t n -> (o p) t n")).then_inc(y_ld, 16)
                for d in range(2 * DOWN):
                    s = raw_of_down(d, last)
                    half, b = divmod(d, DOWN)
                    load(s0 + 2 * FT + s, s % 2, down_rows[:, 2 * b:2 * b + 2, half * HALF:(half + 1) * HALF], 2)
                    if d in X_AFTER and not last:
                        load_x(s0 + 2 * FT + s + 1, (s + 1) % 2, g + 1, X_AFTER[d])

            over_groups(sp, body)
            store(N_GROUPS - 1)
            sp.wait_ge(y_out, 16 * N_GROUPS)

        def down_splits(split, split_x, g, last, after):
            for d in range(2 * DOWN):
                e = d + 2
                if e - 1 in X_AFTER and not last:
                    split_x(NX + g * S_PER + 2 * FT + raw_of_down(e, last) - 1, (raw_of_down(e, last) - 1) % 2, X_AFTER[e - 1], g)
                if e < 2 * DOWN:
                    split(NX + g * S_PER + 2 * FT + raw_of_down(e, last), raw_of_down(e, last) % 2, g * W_PER + 2 * FT + e, e % 2)
                elif not last:
                    m = e - 2 * DOWN
                    split(NX + (g + 1) * S_PER + m, m, (g + 1) * W_PER + m, m)
                after(d)

        def raw_landed(eng, s, parity):
            eng.wait_ge(raw_ld[parity], (s - parity + 2) * 8)

        @block.gpsimd
        def _(pool):
            for c, value in ((power, -0.5), (eps, LN_EPS), (minus, -1.0)):
                pool.memset(c[:, :], value).then_inc(fixed_set, 1)
            pool.wait_ge(fixed_set, 3)
            pool.wait_ge(small_ld, 32)

            def body(g, first, last):
                n0 = g * NB
                for t in range(NB):
                    pool.wait_ge(aggr_done, n0 + t + 1)
                    pool.tensor_tensor(rstd[:, t:t + 1], aggr[:, t, 1:2], eps[:, :], ALU.add).then_inc(rstd_done, 1)
                    pool.tensor_tensor(nmr[:, t:t + 1], aggr[:, t, 0:1], minus[:, :], ALU.mult).then_inc(rstd_done, 1)
                    pool.wait_ge(rstd_done, 4 * (n0 + t) + 2)
                    pool.tensor_tensor(rstd[:, t:t + 1], rstd[:, t:t + 1], power[:, :], ALU.pow).then_inc(rstd_done, 1)
                    pool.wait_ge(rstd_done, 4 * (n0 + t) + 3)
                    pool.tensor_tensor(nmr[:, t:t + 1], nmr[:, t:t + 1], rstd[:, t:t + 1], ALU.mult).then_inc(rstd_done, 1)
                for t in range(NB):
                    pool.wait_ge(gained, n0 + t + 1)
                    pool.tensor_tensor(y[:, t], y[:, t], b_b[:, :], ALU.add).then_inc(y_done, 1)

            over_groups(pool, body)

        @block.tensor
        def _(pe):
            def product(out, a, w, start, stop):
                return pe.matmul(out, a, w, start=start, stop=stop)

            def body(g, first, last):
                s0, w0 = NX + g * S_PER, g * W_PER

                def gate_up(f, q, wait_bank):
                    for m, ps in enumerate((gate_ps, up_ps)):
                        pe.wait_ge(lo_done, s0 + 2 * f + m + 1)
                        if wait_bank:
                            pe.wait_ge(prod_done, g * FT + f - 1)
                        for k in range(KT):
                            cols = slice(k * P, (k + 1) * P)
                            for n, (w, x) in enumerate(((w_hi, x_hi), (w_hi, x_lo), (w_lo, x_hi))):
                                mm = product(ps[q][:, :], w[:, m, cols], x[:, k], k == 0 and n == 0, k == KT - 1 and n == 2)
                        mm.then_inc(used, 1)

                gate_up(0, 0, not first)
                gate_up(1, 1, not first)
                with pe.Fori(1, FT // 2) as f2:
                    for q in range(2):
                        gate_up(2 * f2 + q, q, True)
                for d in range(2 * DOWN):
                    half, b = divmod(d, DOWN)
                    pe.wait_ge(lo_done, s0 + 2 * FT + raw_of_down(d, last) + 1)
                    if half == 0:
                        pe.wait_ge(g_lo_done, g * FT + 2 * b + 2)
                    for j in range(2):
                        f = 2 * b + j
                        for t in range(NB):
                            if b == 0 and j == 0 and not (first and half == 0):
                                pe.wait_ge(added, NB * (2 * g + half - 1) + t + 1)
                            cols = slice(t * P, (t + 1) * P)
                            for n, (x, w) in enumerate(((g_hi, w_hi), (g_hi, w_lo), (g_lo, w_hi))):
                                mm = product(acc[t][:, :], x[:, f, cols], w[:, d % 2, j * HALF:(j + 1) * HALF],
                                             f == 0 and n == 0, f == FT - 1 and n == 2)
                    mm.then_inc(used, 1)

            over_groups(pe, body)

        @block.scalar
        def _(act):
            def high(s, parity, w, slot):
                raw_landed(act, s, parity)
                if not isinstance(w, int) or w >= 2:
                    act.wait_ge(used, w - 1)
                act.activation(w_hi[:, slot], raw[:, parity], ACT.Copy).then_inc(hi_done, 1)

            def high_x(s, parity, n, g):
                raw_landed(act, s, parity)
                if g is not None:
                    act.wait_ge(used, g * W_PER + 2 * FT)
                act.activation(x_hi[:, 2 * n:2 * n + 2], raw[:, parity].rearrange("p (a n) -> p a n", a=2), ACT.Copy).then_inc(hi_done, 1)

            for n in range(NX):
                high_x(n, n % 2, n, None)
            for m in range(2):
                high(NX + m, m, m, m)

            def body(g, first, last):
                s0, w0 = NX + g * S_PER, g * W_PER

                def tile(f, q, wait):
                    high(s0 + 2 * f + 2, 0, w0 + 2 * f + 2, 0)
                    act.wait_ge(used, w0 + 2 * f + 1)
                    if wait:
                        act.wait_ge(prod_done, g * FT + f - 1)
                    act.activation(silu[:, q], gate_ps[q][:, :], ACT.Silu).then_inc(silu_done, 1)
                    high(s0 + 2 * f + 3, 1, w0 + 2 * f + 3, 1)
                    act.wait_ge(prod_done, g * FT + f + 1)
                    act.activation(g_hi[:, bass.ds(f, 1)].rearrange("p o n -> p (o n)"), prod[:, q], ACT.Copy).then_inc(g_hi_done, 1)

                tile(0, 0, not first)
                tile(1, 1, not first)
                with act.Fori(1, FT // 2) as f2:
                    for q in range(2):
                        tile(2 * f2 + q, q, True)
                down_splits(high, high_x, g, last, lambda d: None)
                for t in range(NB):
                    act.wait_ge(rstd_done, 4 * (g * NB + t + 1))
                    act.activation(y[:, t], y[:, t], ACT.Identity, bias=nmr[:, t:t + 1], scale=rstd[:, t:t + 1]).then_inc(normed, 1)

            over_groups(act, body)

        @block.vector
        def _(dve):
            def low(s, parity, w, slot):
                dve.wait_ge(hi_done, s + 1)
                dve.tensor_tensor(w_lo[:, slot], raw[:, parity], w_hi[:, slot].bitcast(F32), ALU.subtract).then_inc(lo_done, 1)

            def low_x(s, parity, n, g):
                dve.wait_ge(hi_done, s + 1)
                dve.tensor_tensor(x_lo[:, 2 * n:2 * n + 2], raw[:, parity].rearrange("p (a n) -> p a n", a=2),
                                  x_hi[:, 2 * n:2 * n + 2].bitcast(F32), ALU.subtract).then_inc(lo_done, 1)

            dve.wait_ge(small_ld, 32)
            for n in range(NX):
                low_x(n, n % 2, n, None)
            for m in range(2):
                low(NX + m, m, m, m)

            def body(g, first, last):
                s0, w0 = NX + g * S_PER, g * W_PER

                def tile(f, q, wait):
                    low(s0 + 2 * f + 2, 0, w0 + 2 * f + 2, 0)
                    low(s0 + 2 * f + 3, 1, w0 + 2 * f + 3, 1)
                    dve.wait_ge(silu_done, g * FT + f + 1)
                    dve.wait_ge(used, w0 + 2 * f + 2)
                    if wait:
                        dve.wait_ge(g_lo_done, g * FT + f - 1)
                    dve.tensor_tensor(prod[:, q], silu[:, q], up_ps[q][:, :], ALU.mult).then_inc(prod_done, 1)
                    dve.wait_ge(g_hi_done, g * FT + f + 1)
                    cols = bass.ds(f, 1)
                    dve.tensor_tensor(g_lo[:, cols].rearrange("p o n -> p (o n)"), prod[:, q],
                                      g_hi[:, cols].rearrange("p o n -> p (o n)").bitcast(F32), ALU.subtract).then_inc(g_lo_done, 1)

                def after(d):
                    if (d + 1) % DOWN == 0:
                        half = d // DOWN
                        cols = slice(half * HALF, (half + 1) * HALF)
                        dve.wait_ge(used, w0 + 2 * FT + d + 1)
                        dve.wait_ge(y_ld, 16 * (g + 1))
                        for t in range(NB):
                            dve.scalar_tensor_tensor(y[:, t, cols], y[:, t, cols], ALPHA, acc[t][:, :], ALU.mult, ALU.add).then_inc(added, 1)

                tile(0, 0, not first)
                tile(1, 1, not first)
                with dve.Fori(1, FT // 2) as f2:
                    for q in range(2):
                        tile(2 * f2 + q, q, True)
                down_splits(low, low_x, g, last, after)
                n0 = g * NB
                for t in range(NB):
                    dve.wait_ge(added, 2 * n0 + NB + t + 1)
                    if t or not first:
                        dve.wait_ge(aggr_done, n0 + t)
                    for half in range(2):
                        dve.bn_stats(stats[:, half], y[:, t, half * HALF:(half + 1) * HALF]).then_inc(stats_done, 1)
                    if t == 0 and not first:
                        dve.wait_ge(rstd_done, 4 * n0)
                    dve.wait_ge(stats_done, 2 * (n0 + t + 1))
                    if t or not first:
                        dve.wait_ge(marked, n0 + t)
                    dve.tensor_tensor(mark[:, :], g_b[:, 0:1], b_b[:, 0:1], ALU.add).then_inc(marked, 1)
                    dve.bn_aggr(aggr[:, t], stats[:, :, :].rearrange("p a s -> p (a s)")).then_inc(aggr_done, 1)
                for t in range(NB):
                    dve.wait_ge(normed, n0 + t + 1)
                    dve.tensor_tensor(y[:, t], y[:, t], g_b[:, :], ALU.mult).then_inc(gained, 1)

            over_groups(dve, body)


def layer(nc, ap, out):
    def scratch(name, rows, cols):
        return nc.dram_tensor(name, (rows, cols), F32, kind="Internal").ap()

    z = scratch("z_scratch", SEQ, IN_COLS)
    o_mix = scratch("o_scratch", SEQ, D_MODEL)
    h = scratch("h_scratch", SEQ, D_MODEL)
    h_t = scratch("ht_scratch", D_MODEL, SEQ)
    ident = ap["consts"][:, CCOL["ident"]:CCOL["ident"] + P]
    projection_phase(nc, ap["x_t"], ap["w_in"], ap["b_in"], ap["pos"], ap["freq"], z)
    with ExitStack() as ctx:
        kc = ctx.enter_context(nc.sbuf_tensor("kc", [P, GROUPS, P], F32R))
        vc = ctx.enter_context(nc.sbuf_tensor("vc", [P, GROUPS, 2 * HEAD], F32R))
        compression_phase(nc, z, ap["cmp_pos"], ap["cmp_w1"], ap["cmp_w2"], ident, kc[:, :, :], vc[:, :, :])
        attention_phase(nc, z, ap["consts"], kc[:, :, :], vc[:, :, :], o_mix)
    mixing_phase(nc, ap["x"], o_mix, ap["gain"], ap["w_out"], ap["ln1_g"], ap["ln1_b"], ident, h, h_t)
    ffn_phase(nc, h, h_t, ap["w_gate"], ap["w_up"], ap["w_down"], ap["ln2_g"], ap["ln2_b"], out)


def kernel(x, positions, w_in, b_in, cmp_pos, cmp_w1, cmp_w2, mix_gain, w_out,
           ln1_g, ln1_b, w_gate, w_up, w_down, ln2_g, ln2_b):
    import concourse.bacc as _bacc
    from concourse.bass_utils import run_bass_kernel_spmd as _run

    own = (("dq", 512), ("dk", 64), ("dv", 64), ("iq", 256), ("iw", 8), ("ik", 32), ("nq", 512), ("kcm", 128),
           ("vcm", 128), ("ksl", 128), ("vsl", 128), ("kwn", 128), ("vwn", 128), ("ng", 24))
    start, at = {}, 0
    for name, n in own:
        start[name] = at
        at += n
    order = np.concatenate([np.arange(start[name], start[name] + n) for name, n in PARTS])
    freq = np.concatenate([500000.0 ** (-np.arange(8) / 8), 500000.0 ** (-np.arange(4) / 4)]).astype(np.float32)
    arrays = {
        "x": np.asarray(x)[0],
        "x_t": np.asarray(x)[0].T,
        "pos": np.asarray(positions)[0].reshape(TILES, P).T,
        "freq": np.broadcast_to(freq, (P, 12)),
        "w_in": np.asarray(w_in)[0][:, order],
        "b_in": np.asarray(b_in)[:, order],
        "cmp_pos": np.asarray(cmp_pos)[0].reshape(2, CMP_BLOCK // 2, P).transpose(2, 0, 1),
        "cmp_w1": np.asarray(cmp_w1)[0],
        "cmp_w2": np.asarray(cmp_w2)[0],
        "gain": np.asarray(mix_gain),
        "w_out": np.asarray(w_out)[0],
        "ln1_g": np.asarray(ln1_g), "ln1_b": np.asarray(ln1_b),
        "w_gate": np.asarray(w_gate)[0], "w_up": np.asarray(w_up)[0], "w_down": np.asarray(w_down)[0],
        "ln2_g": np.asarray(ln2_g), "ln2_b": np.asarray(ln2_b),
        "consts": constants(),
    }
    arrays = {f"in_{k}": np.ascontiguousarray(a) for k, a in arrays.items()}
    nc = _bacc.Bacc("TRN2", target_bir_lowering=False, num_devices=1)
    ap = {k[3:]: nc.dram_tensor(k, a.shape, mybir.dt.from_np(a.dtype), kind="ExternalInput").ap() for k, a in arrays.items()}
    out = nc.dram_tensor("out", (SEQ, D_MODEL), F32, kind="ExternalOutput").ap()
    layer(nc, ap, out)
    r = _run(nc, [arrays], core_ids=[0])
    return np.asarray(r.results[0]["out"]).reshape(1, SEQ, D_MODEL)
```

```python
from contextlib import ExitStack

import numpy as np

import concourse.bass as bass
from concourse import mybir

F32 = mybir.dt.float32
F32R = mybir.dt.float32r
BF16 = mybir.dt.bfloat16
I32 = mybir.dt.int32
ALU = mybir.AluOpType
ACT = mybir.ActivationFunctionType
AX = mybir.AxisListType

P = 128
SEQ = 2048
TILES = SEQ // P
D_MODEL = 1024
KT = D_MODEL // P
HEAD = 64
DSA_HEADS = 8
NSA_HEADS = 8
GROUPS = 2
IDX_HEADS = 8
IDX_DIM = 32
TOPK = 256
WINDOW = 512
CMP_BLOCK = 32
CMP_STRIDE = 16
N_CMP = (SEQ - CMP_BLOCK) // CMP_STRIDE + 1
SLC_BLOCK = 64
N_SLC = SEQ // SLC_BLOCK
FFN = 2816
ALPHA = 2.0 ** 0.25
LN_EPS = 1e-5
SCALE = HEAD ** -0.5
MASKED = -1e30

PARTS = (("dq", 512), ("nq", 512), ("dk", 64), ("ksl", 128), ("kwn", 128), ("kcm", 128),
         ("iq", 256), ("ik", 32), ("dv", 64), ("vsl", 128), ("vwn", 128), ("vcm", 128), ("iw", 8), ("ng", 24))
COL, _at = {}, 0
for _name, _n in PARTS:
    COL[_name] = _at
    _at += _n
IN_COLS = _at
R64 = COL["iq"] // HEAD
R32 = (COL["dv"] - COL["iq"]) // IDX_DIM
NCH = 5
CH = IN_COLS // NCH
MAGIC = 1.5 * 2.0 ** 23
TWO_PI = 2 * np.pi
PI_A = 6.28125
PI_B = float(np.float32(np.round((TWO_PI - PI_A) * 2 ** 20) / 2 ** 20))
PI_C = float(TWO_PI - PI_A - PI_B)
PI_MAX = float(np.nextafter(np.float32(np.pi), np.float32(0)))


def projection_phase(nc, x_t, w_in, b_in, pos, inv_freq, z):
    with ExitStack() as ctx:
        def sb(name, shape, dt=F32):
            return ctx.enter_context(nc.sbuf_tensor(name, shape, dt))

        def sem(name):
            return ctx.enter_context(nc.semaphore(name))

        HALF = IN_COLS // 2
        w_hi = sb("pw_hi", [P, KT, IN_COLS], F32R)
        w_lo = sb("pw_lo", [P, KT, IN_COLS], F32R)
        w_raw = sb("pw_raw", [P, 2, HALF])
        x_raw = sb("px_raw", [P, 2, KT, P])
        x_hi = sb("px_hi", [P, 2, KT, P], F32R)
        x_lo = sb("px_lo", [P, 2, KT, P], F32R)
        bias = sb("p_bias", [P, IN_COLS])
        zt = sb("p_z", [P, 2, IN_COLS])
        posi = sb("p_posi", [P, TILES], I32)
        posf = sb("p_posf", [P, TILES])
        freq = sb("p_freq", [P, 12])
        cos2 = sb("p_cos", [P, TILES, 2, 12])
        sin2 = sb("p_sin", [P, TILES, 2, 12])
        ra = sb("p_ra", [P, R64, 2, 8])
        rb = sb("p_rb", [P, R64, 2, 8])
        ra3 = sb("p_ra3", [P, R32, 2, 4])
        rb3 = sb("p_rb3", [P, R32, 2, 4])
        acc = [ctx.enter_context(nc.psum_tensor(f"p_acc{c}", [P, 512], F32)) for c in range(NCH)]
        def scratch(n):
            return zt[:, 0, n * 192:(n + 1) * 192].rearrange("p (t f) -> p t f", t=TILES)
        ang, kk, r1, r2 = (scratch(n) for n in range(4))

        small_in = sem("p_small_in")
        bias_in = sem("p_bias_in")
        w_in_ld = [sem(f"p_w_ld{b}") for b in range(2)]
        w_hi_done = sem("p_w_hi")
        w_lo_done = sem("p_w_lo")
        x_ld = [sem(f"p_x_ld{b}") for b in range(2)]
        x_hi_done = sem("p_x_hi")
        x_lo_done = sem("p_x_lo")
        acc_full = sem("p_acc_full")
        acc_free = sem("p_acc_free")
        trig = sem("p_trig")
        trig_done = sem("p_trig_done")
        v = sem("p_vec")
        z_ready = sem("p_z_ready")
        z_out = [sem(f"p_z_out{b}") for b in range(2)]

        block = ctx.enter_context(nc.Block())
        x_tiles = x_t.rearrange("(k p) n -> p k n", p=P)
        w_rows = w_in.rearrange("(k p) n -> k p n", p=P)
        z_tiles = z.rearrange("(t p) n -> t p n", p=P)
        NW = 2 * KT

        @block.sync
        def _(sp):
            def store(tile, u):
                sp.wait_ge(z_ready, tile + 1)
                sp.dma_start(z_tiles[bass.ds(tile, 1), :, :].rearrange("o p n -> (o p) n"), zt[:, u]).then_inc(z_out[u], 16)

            sp.dma_start(posi[:, :], pos).then_inc(small_in, 16)
            sp.dma_start(freq[:, :], inv_freq).then_inc(small_in, 16)
            sp.dma_start(x_raw[:, 0], x_tiles[:, :, 0:P]).then_inc(x_ld[0], 16)
            for c in range(NW):
                if c >= 2:
                    sp.wait_ge(w_lo_done, c - 1)
                sp.dma_start(w_raw[:, c % 2], w_rows[c // 2, :, (c % 2) * HALF:(c % 2 + 1) * HALF]).then_inc(w_in_ld[c % 2], 16)
            sp.dma_start(bias[:, :], b_in.broadcast_to([P, IN_COLS])).then_inc(bias_in, 16)
            sp.dma_start(x_raw[:, 1], x_tiles[:, :, P:2 * P]).then_inc(x_ld[1], 16)
            with sp.Fori(0, TILES // 2 - 1) as t:
                for u in range(2):
                    sp.wait_ge(x_lo_done, 2 * t + u + 1)
                    sp.dma_start(x_raw[:, u], x_tiles[:, :, bass.ds((2 * t + u + 2) * P, P)]).then_inc(x_ld[u], 16)
                    store(2 * t + u, u)
            for u in range(2):
                store(TILES - 2 + u, u)
            for u in range(2):
                sp.wait_ge(z_out[u], 16 * (TILES // 2 + 1))

        @block.scalar
        def _(act):
            act.wait_ge(trig, 1)
            act.activation(cos2[:, :, 0, :], r2, ACT.Sin).then_inc(trig_done, 1)
            act.activation(cos2[:, :, 1, :], r2, ACT.Sin).then_inc(trig_done, 1)
            act.activation(sin2[:, :, 0, :], r1, ACT.Sin, scale=-1.0).then_inc(trig_done, 1)
            act.activation(sin2[:, :, 1, :], r1, ACT.Sin).then_inc(trig_done, 1)

            def high(t, u):
                act.wait_ge(x_ld[u], (t + 1) * 16)
                act.wait_ge(acc_full, (2 * t + u + 1) * NCH)
                act.activation(x_hi[:, u], x_raw[:, u], ACT.Copy).then_inc(x_hi_done, 1)

            high(0, 0)
            for c in range(NW):
                act.wait_ge(w_in_ld[c % 2], 16 * (c // 2 + 1))
                act.activation(w_hi[:, c // 2, (c % 2) * HALF:(c % 2 + 1) * HALF], w_raw[:, c % 2], ACT.Copy).then_inc(w_hi_done, 1)
            high(0, 1)
            with act.Fori(1, TILES // 2) as t:
                for u in range(2):
                    high(t, u)

        @block.tensor
        def _(pe):
            pe.sem_inc(acc_full, 2 * NCH)

            def product(u, c, k, n, last):
                xs, ws = ((x_hi, w_hi), (x_hi, w_lo), (x_lo, w_hi))[n]
                mm = pe.matmul(acc[c][:, 0:CH], xs[:, u, k], ws[:, k, c * CH:(c + 1) * CH],
                               start=(k == 0 and n == 0), stop=last)
                if last:
                    mm.then_inc(acc_full, 1)

            def tile_products(tile, u):
                pe.wait_ge(x_lo_done, tile + 1)
                for c in range(NCH):
                    pe.wait_ge(acc_free, tile * NCH + c + 1)
                    for k in range(KT):
                        for n in range(3):
                            product(u, c, k, n, k == KT - 1 and n == 2)

            pe.wait_ge(x_lo_done, 1)
            pe.wait_ge(acc_free, NCH)
            for k in range(KT):
                pe.wait_ge(w_lo_done, 2 * (k + 1))
                for c in range(NCH):
                    for n in range(3):
                        product(0, c, k, n, k == KT - 1 and n == 2)
            tile_products(1, 1)
            with pe.Fori(1, TILES // 2) as t:
                for u in range(2):
                    tile_products(2 * t + u, u)

        @block.vector
        def _(dve):
            def wait_own(value):
                dve.wait_ge(v, value)

            dve.sem_inc(acc_free, NCH)
            dve.wait_ge(small_in, 32)
            dve.tensor_copy(posf[:, :], posi[:, :]).then_inc(v, 1)
            wait_own(1)
            fb = freq[:, :].unsqueeze(1).broadcast_to([P, TILES, 12])
            pb = posf[:, :].unsqueeze(2).broadcast_to([P, TILES, 12])
            dve.tensor_tensor(ang, pb, fb, ALU.mult).then_inc(v, 1)
            n = 2
            for r, shift in ((r1, 0.0), (r2, 0.25)):
                wait_own(n)
                dve.tensor_scalar(kk, ang, 1.0 / TWO_PI, shift, ALU.mult, ALU.add).then_inc(v, 1)
                wait_own(n + 1)
                dve.tensor_scalar(kk, kk, MAGIC, MAGIC, ALU.add, ALU.subtract).then_inc(v, 1)
                src = ang
                for m, part in enumerate((PI_A, PI_B, PI_C)):
                    wait_own(n + 2 + m)
                    dve.scalar_tensor_tensor(r, kk, -part, src, ALU.mult, ALU.add).then_inc(v, 1)
                    src = r
                n += 5
                if shift:
                    wait_own(n)
                    dve.tensor_scalar(r, r, float(np.float32(np.pi / 2)), None, ALU.add).then_inc(v, 1)
                    n += 1
                for op, turn in ((ALU.is_gt, -TWO_PI), (ALU.is_lt, TWO_PI)):
                    wait_own(n)
                    dve.tensor_scalar(kk, r, PI_MAX if turn < 0 else -PI_MAX, turn, op, ALU.mult).then_inc(v, 1)
                    wait_own(n + 1)
                    dve.tensor_tensor(r, r, kk, ALU.add).then_inc(v, 1)
                    n += 2
                wait_own(n)
                dve.tensor_scalar(r, r, PI_MAX, -PI_MAX, ALU.min, ALU.max).then_inc(v, 1)
                n += 1
            wait_own(n)
            dve.sem_inc(trig, 1)
            for u in range(2):
                dve.sem_inc(z_out[u], 16)

            def split(t, u):
                dve.wait_ge(x_hi_done, t + 1)
                dve.tensor_tensor(x_lo[:, u], x_raw[:, u], x_hi[:, u].bitcast(F32), ALU.subtract).then_inc(x_lo_done, 1)

            split(0, 0)
            for c in range(NW):
                dve.wait_ge(w_hi_done, c + 1)
                dve.tensor_tensor(w_lo[:, c // 2, (c % 2) * HALF:(c % 2 + 1) * HALF], w_raw[:, c % 2],
                                  w_hi[:, c // 2, (c % 2) * HALF:(c % 2 + 1) * HALF].bitcast(F32), ALU.subtract).then_inc(w_lo_done, 1)
            dve.wait_ge(trig_done, 4)
            dve.wait_ge(bias_in, 16)
            STEPS = 7

            def bias_and_rope(t, u, last):
                tile = 2 * t + u
                base = n + tile * STEPS
                if not last:
                    split(tile + 1, 1 - u)
                dve.wait_ge(z_out[u], 16 * (t + 1))
                for c in range(NCH):
                    dve.wait_ge(acc_full, (tile + 2) * NCH + c + 1)
                    dve.tensor_tensor(zt[:, u, c * CH:(c + 1) * CH], acc[c][:, 0:CH], bias[:, c * CH:(c + 1) * CH],
                                      ALU.add).then_inc(acc_free, 1)
                dve.wait_ge(acc_free, (tile + 2) * NCH)
                done = base
                for h, (lo, heads, dim, f, fo, a, b) in enumerate(((0, R64, HEAD, 8, 0, ra, rb),
                                                                  (COL["iq"], R32, IDX_DIM, 4, 8, ra3, rb3))):
                    zr = zt[:, u, lo:lo + heads * dim].rearrange("p (h d) -> p h d", h=heads)[:, :, 0:2 * f].rearrange(
                        "p h (a f) -> p h a f", a=2)
                    cs = cos2[:, bass.ds(tile, 1), :, fo:fo + f].rearrange("p o a f -> p (o a) f").unsqueeze(1).broadcast_to([P, heads, 2, f])
                    sn = sin2[:, bass.ds(tile, 1), :, fo:fo + f].rearrange("p o a f -> p (o a) f").unsqueeze(1).broadcast_to([P, heads, 2, f])
                    dve.tensor_tensor(a[:, :, :, :], zr, cs, ALU.mult).then_inc(v, 1)
                    dve.tensor_tensor(b[:, :, 0, :], zr[:, :, 1, :], sn[:, :, 0, :], ALU.mult).then_inc(v, 1)
                    dve.tensor_tensor(b[:, :, 1, :], zr[:, :, 0, :], sn[:, :, 1, :], ALU.mult).then_inc(v, 1)
                    dve.wait_ge(v, done + 3)
                    dve.tensor_tensor(zr, a[:, :, :, :], b[:, :, :, :], ALU.add).then_inc((v, z_ready)[h], 1)
                    done = done + 4

            with dve.Fori(0, TILES // 2 - 1) as t:
                for u in range(2):
                    bias_and_rope(t, u, False)
            bias_and_rope(TILES // 2 - 1, 0, False)
            bias_and_rope(TILES // 2 - 1, 1, True)


def compression_phase(nc, z, cmp_pos, cmp_w1, cmp_w2, ident_in, kc, vc):
    LC = CMP_BLOCK // 2
    LAST = CMP_STRIDE * (N_CMP - 1)
    with ExitStack() as ctx:
        def sb(name, shape, dt=F32):
            return ctx.enter_context(nc.sbuf_tensor(name, shape, dt))

        def sem(name):
            return ctx.enter_context(nc.semaphore(name))

        rows = sb("c_rows", [P, TILES, 4, 2, HEAD])
        pairs = sb("c_pairs", [P, 2, SEQ])
        w1 = sb("c_w1", [P, 2, LC, P])
        w2k = sb("c_w2k", [P, 2, HEAD])
        w2v = sb("c_w2v", [P, HEAD])
        pos = sb("c_pos", [P, 2, LC])
        ident = sb("c_ident", [P, P])
        posb = sb("c_posb", [P, 2])
        y = sb("c_y", [P, 4, N_CMP])
        u = sb("c_u", [P, 4, N_CMP])
        g = sb("c_g", [P, 4, N_CMP])
        hi_tmp = sb("c_hi", [P, 2, P], F32R)
        turned = [ctx.enter_context(nc.psum_tensor(f"c_turned{b}", [P, 512], F32)) for b in range(2)]
        hid = [ctx.enter_context(nc.psum_tensor(f"c_hid{h}", [P, 512], F32)) for h in range(4)]
        small = ctx.enter_context(nc.psum_tensor("c_small", [P, 512], F32))

        ident_ld = sem("c_ident_ld")
        w_ld = sem("c_w_ld")
        rows_ld = [sem(f"c_rows_ld{h}") for h in range(4)]
        twice_done = sem("c_twice_done")
        turned_full = sem("c_turned_full")
        upper_done = sem("c_upper_done")
        lower_done = sem("c_lower_done")
        hid_full = sem("c_hid_full")
        v = sem("c_vec")
        tanh_done = sem("c_tanh_done")
        small_full = sem("c_small_full")
        block = ctx.enter_context(nc.Block())
        z_rows = z.rearrange("(t p) n -> p t n", p=P)
        head_col = [COL["kcm"], COL["kcm"] + HEAD, COL["vcm"], COL["vcm"] + HEAD]

        @block.sync
        def _(sp):
            sp.dma_start(ident[:, :], ident_in).then_inc(ident_ld, 16)
            for h in range(4):
                sp.dma_start(rows[:, :, h, 0, :], z_rows[:, :, head_col[h]:head_col[h] + HEAD]).then_inc(rows_ld[h], 16)
            sp.dma_start(pos[:, :, :], cmp_pos).then_inc(w_ld, 16)

        @block.gpsimd
        def _(pool):
            for h in range(4):
                pool.wait_ge(rows_ld[h], 16)
                pool.tensor_copy(rows[:, :, h, 1, :], rows[:, :, h, 0, :]).then_inc(twice_done, 1)

        @block.tensor
        def _(pe):
            pe.wait_ge(ident_ld, 16)
            for h in range(4):
                pe.wait_ge(twice_done, h + 1)
                for q in range(4):
                    n = 4 * h + q
                    if n >= 2:
                        pe.wait_ge(upper_done, n - 1)
                        pe.wait_ge(lower_done, n - 1)
                    for t in range(4):
                        mm = pe.transpose(turned[n % 2][:, t * P:(t + 1) * P],
                                          rows[:, 4 * q + t, h].rearrange("p a d -> p (a d)"), ident[:, :])
                    mm.then_inc(turned_full, 1)
                if h == 0:
                    pe.wait_ge(w_ld, 16 * 6)
                    for b in range(2):
                        for c in range(LC):
                            mm = pe.matmul(small[:, b:b + 1], w1[:, b, c], pos[:, b, c:c + 1], start=(c == 0), stop=(c == LC - 1))
                    mm.then_inc(small_full, 1)
                pe.wait_ge(upper_done, 4 * (h + 1))
                pe.wait_ge(lower_done, 4 * (h + 1))
                for c in range(LC):
                    mm = pe.matmul(hid[h][:, 0:N_CMP], w1[:, h // 2, c], pairs[:, h % 2, 2 * c:2 * c + LAST + 1:CMP_STRIDE],
                                   start=(c == 0), stop=(c == LC - 1))
                mm.then_inc(hid_full, 1)
            pe.wait_ge(v, 12)
            for h in range(2):
                pe.matmul(small[:, h * P:h * P + N_CMP], w2k[:, :, :].rearrange("p a d -> p (a d)"), g[:, h, :],
                          start=True, stop=True)
            for h in range(2):
                mm = pe.matmul(small[0:N_CMP, (2 + h) * P:(2 + h) * P + HEAD], g[:, 2 + h, :], w2v[:, :], start=True, stop=True)
            mm.then_inc(small_full, 1)

        @block.scalar
        def _(act):
            for b in range(2):
                act.dma_start(w1[:, b], cmp_w1[b].rearrange("(c p) n -> p c n", p=P)).then_inc(w_ld, 16)
            for twice in range(2):
                act.dma_start(w2k[:, twice], cmp_w2[0]).then_inc(w_ld, 16)
            act.dma_start(w2v[:, :], cmp_w2[1]).then_inc(w_ld, 16)
            for n in range(16):
                h, q = divmod(n, 4)
                if q == 0 and h >= 2:
                    act.wait_ge(hid_full, h - 1)
                act.wait_ge(turned_full, n + 1)
                act.activation(pairs[0:HEAD, h % 2, 512 * q:512 * (q + 1)], turned[n % 2][0:HEAD, :], ACT.Copy).then_inc(upper_done, 1)
            act.wait_ge(v, 10)
            act.activation(u[:, :, :], u[:, :, :], ACT.Tanh, scale=float(np.sqrt(2 / np.pi))).then_inc(tanh_done, 1)

        @block.vector
        def _(dve):
            dve.memset(kc.bitcast(F32), 0.0).then_inc(v, 1)
            dve.memset(vc, 0.0).then_inc(v, 1)
            for n in range(16):
                h, q = divmod(n, 4)
                if q == 0 and h >= 2:
                    dve.wait_ge(hid_full, h - 1)
                dve.wait_ge(turned_full, n + 1)
                skip = 1 if q == 0 else 0
                dve.tensor_copy(pairs[HEAD:P, h % 2, 512 * q - 1 + skip:512 * (q + 1) - 1], turned[n % 2][HEAD:P, skip:512]).then_inc(lower_done, 1)
                if n == 4:
                    dve.wait_ge(small_full, 1)
                    dve.tensor_copy(posb[:, :], small[:, 0:2]).then_inc(v, 1)
            dve.wait_ge(v, 3)
            for h in range(4):
                dve.wait_ge(hid_full, h + 1)
                dve.tensor_scalar(y[:, h, :], hid[h][:, 0:N_CMP], posb[:, h // 2:h // 2 + 1], None, ALU.add).then_inc(v, 1)
            dve.wait_ge(v, 7)
            dve.tensor_tensor(u[:, :, :], y[:, :, :], y[:, :, :], ALU.mult).then_inc(v, 1)
            dve.wait_ge(v, 8)
            dve.tensor_scalar(u[:, :, :], u[:, :, :], 0.044715, 1.0, ALU.mult, ALU.add).then_inc(v, 1)
            dve.wait_ge(v, 9)
            dve.tensor_tensor(u[:, :, :], u[:, :, :], y[:, :, :], ALU.mult).then_inc(v, 1)
            dve.wait_ge(tanh_done, 1)
            dve.scalar_tensor_tensor(g[:, :, :], u[:, :, :], 1.0, y[:, :, :], ALU.add, ALU.mult).then_inc(v, 1)
            dve.wait_ge(v, 11)
            dve.tensor_scalar(g[:, :, :], g[:, :, :], 0.5, None, ALU.mult).then_inc(v, 1)
            dve.wait_ge(small_full, 2)
            keys = small[:, 0:2 * P].rearrange("p (h n) -> p h n", h=2)[:, :, 0:N_CMP]
            vals = small[0:N_CMP, 2 * P:4 * P].rearrange("p (h n) -> p h n", h=2)[:, :, 0:HEAD]
            dve.tensor_copy(kc[0:HEAD, :, 0:N_CMP], keys[0:HEAD]).then_inc(v, 1)
            dve.tensor_copy(hi_tmp[HEAD:P, :, 0:N_CMP], keys[HEAD:P]).then_inc(v, 1)
            dve.tensor_copy(vc[0:N_CMP], vals).then_inc(v, 1)
            dve.wait_ge(v, 15)
            dve.tensor_tensor(kc[HEAD:P, :, 0:N_CMP], keys[HEAD:P], hi_tmp[HEAD:P, :, 0:N_CMP].bitcast(F32), ALU.subtract).then_inc(v, 1)


RING = 7
W_TILES = WINDOW // P + 1
CHUNK = 512
BANKS_S = 4
NSTEP = 24
ZA = COL["dk"]
ZA_COLS = IN_COLS - ZA
PT_RING = 4
RELU_RING = 8
LONG_UNIT = 12 * P
MOVE_FIRST = 3
INDEX_AFTER = (("W", 1), ("W", 4), ("W", 6), ("S", 1), ("S", 3), ("S", 5), ("S", 7), ("D", 1))
PV_LAG = 2
CONST = (("ident", P), ("diag", P), ("win", W_TILES * P), ("cmp", 248), ("keep", 62), ("add", 62), ("halve", NSTEP + 1))
CCOL, _at = {}, 0
for _name, _n in CONST:
    CCOL[_name] = _at
    _at += _n
CONST_COLS = _at


def attention_schedule():
    units = []
    for i in range(TILES):
        for kind in "CWSD":
            for h in range(8):
                units.append((kind, i, h))
                if (kind, h) in INDEX_AFTER and i + 2 < TILES:
                    units.append(("I", i + 2, INDEX_AFTER.index((kind, h))))
    return units


def key_tiles(kind, i):
    if kind == "C":
        return 0, 1
    if kind == "W":
        return max(0, i - W_TILES + 1), min(i + 1, W_TILES)
    return 0, i + 1


def attention_phase(nc, z, consts, kc, vc, o_mix):
    units = attention_schedule()
    N = len(units)
    where = {u: n for n, u in enumerate(units)}
    width = [P * key_tiles(k, i)[1] for k, i, h in units]
    chunks = [[(c, min(CHUNK, w - c)) for c in range(0, w, CHUNK)] for w in width]
    att = [n for n in range(N) if units[n][0] != "I"]
    a_of = {n: a for a, n in enumerate(att)}

    def index_after(a):
        return [n for n in range(att[a] + 1, att[a + 1])] if a + 1 < len(att) else []
    chunk0, mask0, relu0 = [0], [0], [0]
    for n in range(N):
        m = len(chunks[n])
        chunk0.append(chunk0[-1] + m)
        mask0.append(mask0[-1] + (m if n in a_of else 0))
        relu0.append(relu0[-1] + (0 if n in a_of else m))
    reader = [("mask", mask0[n] + c + 1) if n in a_of else ("relu", relu0[n] + c + 1)
              for n in range(N) for c in range(len(chunks[n]))]
    PIECES = {"A": (("dk", "ik"), ("iq",), ("gates",)), "N": (("q",),), "D": (("q",),)}
    preps = [("A", 0), ("A", 1), ("A", 2), ("N", 0)]
    pool_at, pe_at = {}, {}

    def place(at, p, units_of):
        for m, u in enumerate(units_of):
            at.setdefault(where[u], []).append((p, m))
    for i in range(TILES):
        preps.append(("D", i))
        place(pool_at, ("D", i), [("C", i, 0)])
        place(pe_at, ("D", i), [("C", i, 2), ("C", i, 3)])
        if i + 1 < TILES:
            preps.append(("N", i + 1))
            place(pool_at, ("N", i + 1), [("S", i, 4)])
            place(pe_at, ("N", i + 1), [("S", i, 6), ("S", i, 7)])
        if i + 3 < TILES:
            preps.append(("A", i + 3))
            place(pool_at, ("A", i + 3), [("D", i, h) for h in (0, 1, 1)])
            place(pe_at, ("A", i + 3), [("D", i, h) for h in (4, 5, 6, 7)])
    prep_no = {p: m for m, p in enumerate(preps)}
    PREP_BLOCKS = {"A": 14, "N": 8, "D": 8}
    EVACS = {"A": (((0, 1, "dk"), (1, 2, "ksl"), (3, 1, "kwn0")), ((4, 1, "kwn1"), (5, 1, "ik"), (6, 2, "iq")), ((8, 4, "iq"),), ((12, 2, "iq"),)),
             "N": (((0, 4, "nq"),), ((4, 4, "nq"),)), "D": (((0, 4, "dq"),), ((4, 4, "dq"),))}
    groups, evac_no = [], {}
    n_evac = 0

    def add_group(p, g):
        nonlocal n_evac
        n_evac += len(EVACS[p[0]][g])
        evac_no[(p, g)] = n_evac
        groups.append(("prep", p, g))
    for p in preps[:4]:
        for g in range(len(EVACS[p[0]])):
            add_group(p, g)
    att_group0 = {}
    n_att = 0
    for n in range(N):
        for p, g in pe_at.get(n, ()):
            add_group(p, g)
        if n in a_of:
            att_group0[n] = n_att
            for g in range((width[n] // P + 3) // 4):
                groups.append(("att", n, g))
                n_att += 1
    group_no = {g: m for m, g in enumerate(groups)}
    last_group = {n: att_group0[n] + (width[n] // P + 3) // 4 for n in att}
    finish_at, behind = {}, []
    for n in att:
        for g in range((width[n] // P + 3) // 4):
            behind.append((n, g))
            if len(behind) > PV_LAG:
                m, g_m = behind.pop(0)
                if units[m][2] % 4 == 3 and g_m == (width[m] // P + 3) // 4 - 1:
                    finish_at[att[a_of[n] + 1]] = m
    steps = {}
    for i in range(1, TILES - 1):
        for m, (kind, h) in enumerate([(k, h) for k in "WSD" for h in range(8)]):
            steps[where[(kind, i, h)]] = ((i - 1) * NSTEP + m, i + 1, m)
    act_part = {t: (t + 1) * P * 9 // 16 // 64 * 64 for t in range(TILES)}

    with ExitStack() as ctx:
        def sb(name, shape, dt=F32):
            return ctx.enter_context(nc.sbuf_tensor(name, shape, dt))

        def sem(name):
            return ctx.enter_context(nc.semaphore(name))

        def psum(name, cols):
            return ctx.enter_context(nc.psum_tensor(name, [P, cols], F32))

        cst = sb("a_const", [P, CONST_COLS])
        def const(name, lo, n):
            return cst[:, CCOL[name] + lo:CCOL[name] + lo + n]
        dk_t = sb("a_dk", [P, SEQ], F32R)
        ksl_t = sb("a_ksl", [P, GROUPS, SEQ], F32R)
        kwn_t = sb("a_kwn", [P, GROUPS, RING, P], F32R)
        ik_t = sb("a_ik", [P, SEQ], F32R)
        iq_t = sb("a_iq", [P, IDX_HEADS, P], F32R)
        dv = sb("a_dv", [P, TILES, HEAD])
        vsl = sb("a_vsl", [P, TILES, GROUPS, HEAD])
        vwn = sb("a_vwn", [P, TILES, GROUPS, HEAD])
        q_t = {"N": sb("a_nq", [P, 8, P], F32R), "D": sb("a_dq", [P, 8, P], F32R)}
        q_s = {"N": sb("a_nqs", [P, 8, P], F32R), "D": sb("a_dqs", [P, 8, P], F32R)}
        za = sb("a_za", [P, ZA_COLS])
        zq = {"N": sb("a_zn", [P, 512]), "D": sb("a_zd", [P, 512])}
        split = sb("a_split", [P, 14, P], F32R)
        scores = [sb(f"a_scores{b}", [P, SEQ]) for b in range(3)]
        p_t = sb("a_p_t", [P, PT_RING, 512])
        index = [sb(f"a_index{b}", [P, SEQ]) for b in range(2)]
        relu = sb("a_relu", [P, RELU_RING, CHUNK])
        mask_d = sb("a_mask_d", [P, SEQ], BF16)
        mask_s = sb("a_mask_s", [P, GROUPS, SEQ], BF16)
        above = sb("a_above", [P, SEQ], BF16)
        atleast = sb("a_atleast", [P, SEQ], BF16)
        junk_a, junk_v = atleast, above
        oacc = sb("a_oacc", [P, 2 * 512])
        fin = sb("a_fin", [P, 2, 256])
        iw = sb("a_iw", [P, 4, IDX_HEADS])
        gate = sb("a_gate", [P, 4, 24])
        nmax = sb("a_nmax", [P, 4, SEQ // CHUNK])
        lsum = sb("a_lsum", [P, 2, 4])
        rsum = sb("a_rsum", [P, 2, 4])
        rgate = sb("a_rgate", [P, 2, 4])
        imp_c = sb("a_imp_c", [P, P + 1])
        imp = sb("a_imp", [P, 2, N_SLC])
        top8 = sb("a_top8", [P, 8])
        sel = sb("a_sel", [P, 2, N_SLC])
        tk = sb("a_tk", [P, 16])
        amax, thr, cnt_a, cnt_v, tmp1, tmp2, lo, hi, n_above, room = (tk[:, m:m + 1] for m in range(10))
        halves = sb("a_halves", [P, NSTEP + 1])

        ps_s = [psum(f"a_ps_s{b}", CHUNK) for b in range(BANKS_S)]
        ps_t = [psum(f"a_ps_t{b}", 512) for b in range(2)]
        ps_o = [psum(f"a_ps_o{b}", 4 * HEAD) for b in range(2)]

        const_ld = sem("a_const_ld")
        za_ld = sem("a_za_ld")
        v_ld = sem("a_v_ld")
        zq_ld = {k: sem(f"a_z{k}_ld") for k in "ND"}
        split_done = sem("a_split_done")
        prep_turned = sem("a_prep_turned")
        group_turned = sem("a_group_turned")
        evac_done = sem("a_evac_done")
        swap_done = {k: sem(f"a_swap{k}") for k in "ND"}
        qk_done = sem("a_qk_done")
        masked = sem("a_masked")
        exp_done = sem("a_exp_done")
        copied = sem("a_copied")
        pv_done = sem("a_pv_done")
        relu_done = sem("a_relu_done")
        index_done = sem("a_index_done")
        search_set = sem("a_search_set")
        count_a = sem("a_count_a")
        count_v = sem("a_count_v")
        thr_moved = sem("a_thr_moved")
        above_done = sem("a_above_done")
        atleast_done = sem("a_atleast_done")
        kept_done = sem("a_kept_done")
        mask_d_done = sem("a_mask_d_done")
        sel_done = sem("a_sel_done")
        mask_s_done = sem("a_mask_s_done")
        gate_in = sem("a_gate_in")
        gate_exp = sem("a_gate_exp")
        gate_done = sem("a_gate_done")
        fin_done = sem("a_fin_done")
        acc_done = sem("a_acc_done")
        out_done = {k: sem(f"a_out{k}") for k in "ND"}
        vec = sem("a_vec")
        own = sem("a_pool_own")

        block = ctx.enter_context(nc.Block())
        z_tiles = z.rearrange("(t p) n -> t p n", p=P)
        z_cols = z.rearrange("(t p) n -> p t n", p=P)
        o_tiles = o_mix.rearrange("(t p) n -> t p n", p=P)
        quad = {n: a_of[n] // 4 for n in att}

        def wait_reader(eng, s):
            if s >= BANKS_S:
                kind, value = reader[s - BANKS_S]
                eng.wait_ge(masked if kind == "mask" else relu_done, value)

        def qk_before(n):
            return chunk0[n + 1]

        @block.sync
        def _(sp):
            def load(p):
                kind, t = p
                if kind == "A":
                    if t >= 1:
                        sp.wait_ge(split_done, prep_no[("A", t - 1)] + 1)
                        sp.wait_ge(gate_in, 2 * t)
                    sp.dma_start(za[:, :], z_tiles[t, :, ZA:IN_COLS]).then_inc(za_ld, 16)
                else:
                    if t >= 1:
                        sp.wait_ge(split_done, prep_no[(kind, t - 1)] + 1)
                    c = COL["nq" if kind == "N" else "dq"]
                    sp.dma_start(zq[kind][:, :], z_tiles[t, :, c:c + 512]).then_inc(zq_ld[kind], 16)

            def swap(p):
                kind, t = p
                sp.wait_ge(evac_done, evac_no[(p, 1)])
                for half in range(2):
                    sp.dma_start(q_s[kind][half * HEAD:(half + 1) * HEAD].bitcast(F32), q_t[kind][(1 - half) * HEAD:(2 - half) * HEAD].bitcast(F32)).then_inc(swap_done[kind], 16)

            sp.dma_start(cst[:, :], consts).then_inc(const_ld, 16)
            for p in (("A", 0), ("N", 0), ("D", 0)):
                load(p)
            for dst, name, heads in ((dv, "dv", 1), (vsl, "vsl", GROUPS), (vwn, "vwn", GROUPS)):
                dst = dst[:, :, :] if heads == 1 else dst[:, :, :, :].rearrange("p t g d -> p t (g d)")
                sp.dma_start(dst, z_cols[:, :, COL[name]:COL[name] + heads * HEAD]).then_inc(v_ld, 16)
            load(("A", 1))
            load(("A", 2))
            swap(("N", 0))
            load(("N", 1))
            load(("A", 3))
            for n in range(N):
                kind, i, h = units[n]
                for p, g in pe_at.get(n, ()):
                    if g == len(EVACS[p[0]]) - 1:
                        if p[0] != "A":
                            swap(p)
                        nxt = (p[0], p[1] + 1)
                        if nxt in prep_no:
                            load(nxt)
                if (kind, h) == ("D", 3):
                    sp.wait_ge(acc_done, 8 * i + 6)
                    sp.dma_start(o_tiles[i, :, 512:1024], oacc[:, 512:1024]).then_inc(out_done["N"], 16)
                if (kind, h) == ("C", 6) and i >= 1:
                    sp.wait_ge(acc_done, 8 * i)
                    sp.dma_start(o_tiles[i - 1, :, 0:512], oacc[:, 0:512]).then_inc(out_done["D"], 16)
            sp.wait_ge(acc_done, 8 * TILES)
            sp.dma_start(o_tiles[TILES - 1, :, 0:512], oacc[:, 0:512]).then_inc(out_done["D"], 16)
            for kind in "ND":
                sp.wait_ge(out_done[kind], 16 * TILES)

        @block.gpsimd
        def _(pool):
            owned = [0]

            def mine(ins):
                ins.then_inc(own, 1)
                owned[0] += 1
                return owned[0]

            def copies(pairs, waits=True):
                for h_, l_, x_ in pairs:
                    last = mine(pool.tensor_copy(h_, x_))
                pool.wait_ge(own, last)
                for h_, l_, x_ in pairs:
                    last = mine(pool.tensor_tensor(l_, x_, h_.bitcast(F32), ALU.subtract))
                return last

            def prep(p, piece):
                kind, t = p
                m = prep_no[p]
                names = PIECES[kind][piece]
                if piece == 0 and m >= 1:
                    pool.wait_ge(prep_turned, m)
                if kind != "A":
                    pool.wait_ge(zq_ld[kind], 16 * (t + 1))
                    x = zq[kind][:, :].rearrange("p (h d) -> p h d", h=8)
                    last = copies([(split[:, 0:8, 0:HEAD], split[:, 0:8, HEAD:P], x)])
                    pool.wait_ge(own, last)
                    pool.sem_inc(split_done, 1)
                    return

                def part(name, heads, dim):
                    c = COL[name] - ZA
                    return za[:, c:c + heads * dim].rearrange("p (h d) -> p h d", h=heads)
                pool.wait_ge(za_ld, 16 * (t + 1))
                if "dk" in names:
                    ikx = part("ik", 1, IDX_DIM).broadcast_to([P, 2, IDX_DIM])
                    iks = split[:, 5, :].rearrange("p (a b d) -> p a b d", a=2, b=2)
                    copies([(split[:, 0:5, 0:HEAD], split[:, 0:5, HEAD:P], part("dk", 5, HEAD)),
                            (iks[:, :, 0, :], iks[:, :, 1, :], ikx)])
                if "iq" in names:
                    iqx = part("iq", 8, IDX_DIM).unsqueeze(2).broadcast_to([P, 8, 2, IDX_DIM])
                    iqs = split[:, 6:14, :].rearrange("p h (a d) -> p h a d", a=4)
                    last = copies([(iqs[:, :, 0:2, :], iqs[:, :, 2:4, :], iqx)])
                    pool.wait_ge(own, last)
                    pool.sem_inc(split_done, 1)
                if "gates" in names:
                    if t >= 4:
                        if t >= 6:
                            pool.wait_ge(index_done, relu0[where[("I", t - 4, 7)] + 1])
                        pool.wait_ge(fin_done, quad_end("S", t - 4))
                    pool.tensor_copy(iw[:, t % 4], za[:, COL["iw"] - ZA:COL["iw"] - ZA + 8]).then_inc(gate_in, 1)
                    pool.tensor_copy(gate[:, t % 4], za[:, COL["ng"] - ZA:COL["ng"] - ZA + 24]).then_inc(gate_in, 1)

            def quad_end(kind, i):
                return quad[where[(kind, i, 7)]] + 1

            def accumulate(n):
                kind, i, h = units[n]
                q = quad[n]
                pool.wait_ge(fin_done, q + 1)
                col = 256 * (h // 4) + (0 if kind == "D" else 512)
                dst = oacc[:, col:col + 256]
                if kind in "CD":
                    if i >= 1 and h == 3:
                        pool.wait_ge(out_done["N" if kind == "C" else "D"], 16 * i)
                    pool.tensor_copy(dst, fin[:, q % 2]).then_inc(acc_done, 1)
                else:
                    pool.wait_ge(acc_done, q)
                    pool.tensor_tensor(dst, dst, fin[:, q % 2], ALU.add).then_inc(acc_done, 1)

            def atleast_mask(t):
                w = (t + 1) * P
                pool.wait_ge(above_done, t - 1)
                pool.tensor_scalar(atleast[:, 0:w], index[t % 2][:, 0:w], lo, None, ALU.is_ge).then_inc(atleast_done, 1)
                pool.tensor_scalar(room, n_above, -1.0, float(TOPK), ALU.mult, ALU.add).then_inc(atleast_done, 1)

            def final_mask(t):
                w = (t + 1) * P
                if t >= 1:
                    pool.wait_ge(masked, mask0[where[("D", t - 1, 7)] + 1])
                if t < 2:
                    if t == 1:
                        last = mine(pool.memset(mask_d[:, 0:P], 0.0))
                        pool.wait_ge(own, last)
                    pool.tensor_copy(mask_d[:, t * P:w], const("diag", 0, P)).then_inc(mask_d_done, 1)
                else:
                    pool.wait_ge(kept_done, t - 1)
                    last = mine(pool.tensor_tensor(above[:, 0:w], above[:, 0:w], atleast[:, 0:w], ALU.add))
                    pool.wait_ge(own, last)
                    pool.tensor_scalar(mask_d[:, 0:w], above[:, 0:w], 0.5, MASKED, ALU.is_lt, ALU.mult).then_inc(mask_d_done, 1)

            def block_mask(i, g):
                w = (i + 1) * P
                if i >= 1:
                    pool.wait_ge(masked, mask0[where[("S", i - 1, 4 * g + 3)] + 1])
                pool.wait_ge(sel_done, 2 * i + g + 1)
                if i >= 1:
                    last = mine(pool.tensor_copy(mask_s[:, g, 0:i * P].rearrange("p (j k) -> p j k", k=SLC_BLOCK),
                                                 sel[:, g, 0:2 * i].unsqueeze(2).broadcast_to([P, 2 * i, SLC_BLOCK])))
                    pool.wait_ge(own, last)
                pool.tensor_copy(mask_s[:, g, i * P:w], const("diag", 0, P)).then_inc(mask_s_done, 1)

            pool.wait_ge(const_ld, 16)
            for p in preps[:4]:
                for piece in range(len(PIECES[p[0]])):
                    prep(p, piece)
            for n in att:
                kind, i, h = units[n]
                if kind == "C":
                    if h == 1 and i >= 2:
                        atleast_mask(i)
                    if h == 4:
                        final_mask(i)
                if kind == "W" and h == 0:
                    block_mask(i, 0)
                if kind == "W" and h == 1:
                    block_mask(i, 1)
                if n in finish_at:
                    accumulate(finish_at[n])
                for job in pool_at.get(n, ()):
                    prep(*job)
            accumulate(N - 1)

        @block.tensor
        def _(pe):
            turned = [0]

            def taken(j):
                pe.wait_ge(copied, j + 1)

            def bank_free(m):
                if m >= 2:
                    kind, x, g = groups[m - 2]
                    if kind == "prep":
                        pe.wait_ge(evac_done, evac_no[(x, g)])
                    else:
                        taken(att_group0[x] + g)

            def prep(p, g):
                pe.wait_ge(split_done, prep_no[p] + 1)
                m = group_no[("prep", p, g)]
                bank_free(m)
                for b in range(4 * g, min(4 * g + 4, PREP_BLOCKS[p[0]])):
                    mm = pe.transpose(ps_t[m % 2][:, (b % 4) * P:(b % 4 + 1) * P], split[:, b, :].bitcast(F32), const("ident", 0, P))
                mm.then_inc(group_turned, 1)
                if g == len(EVACS[p[0]]) - 1:
                    pe.wait_ge(group_turned, m + 1)
                    pe.sem_inc(prep_turned, 1)

            def keys(kind, h, i, b0, nb):
                g = h // 4
                if kind == "C":
                    return kc[:, g, :]
                if kind == "W":
                    return kwn_t[:, g, b0 % RING:b0 % RING + nb, :]
                if kind == "S":
                    return ksl_t[:, g, b0 * P:(b0 + nb) * P]
                if kind == "D":
                    return dk_t[:, b0 * P:(b0 + nb) * P]
                return ik_t[:, b0 * P:(b0 + nb) * P]

            def qk(n, c):
                kind, i, h = units[n]
                first, _ = key_tiles(kind, i)
                if c == 0 and (h == 0 or kind == "I"):
                    if kind == "I":
                        pe.wait_ge(evac_done, evac_no[(("A", i), 3)])
                    elif kind != "C":
                        pe.wait_ge(evac_done, evac_no[(("A", i), 3)])
                    if kind == "C":
                        pe.wait_ge(evac_done, evac_no[(("N", i), 1)])
                        pe.wait_ge(swap_done["N"], 32 * (i + 1))
                    if kind == "D":
                        pe.wait_ge(evac_done, evac_no[(("D", i), 1)])
                        pe.wait_ge(swap_done["D"], 32 * (i + 1))
                col, w = chunks[n][c]
                s = chunk0[n] + c
                wait_reader(pe, s)
                out = ps_s[s % BANKS_S]
                b = 0
                while b < w // P:
                    t0 = first + col // P + b
                    nb = min(4 - b % 4, w // P - b)
                    if kind == "W":
                        nb = min(nb, RING - t0 % RING)
                    rhs = keys(kind, h, i, t0, nb)
                    dst = out[:, b * P:(b + nb) * P]
                    if kind == "I":
                        mm = pe.matmul(dst, iq_t[:, h, :], rhs, start=True, stop=True)
                    else:
                        q = "D" if kind == "D" else "N"
                        pe.matmul(dst, q_t[q][:, h, :], rhs, start=True, stop=False)
                        mm = pe.matmul(dst, q_s[q][:, h, :], rhs, start=False, stop=True)
                    b += nb
                mm.then_inc(qk_done, 1)

            def values(kind, g, t):
                if kind == "C":
                    return vc[:, g, :]
                return dv[:, t] if kind == "D" else (vwn if kind == "W" else vsl)[:, t, g]

            def pv(n, g):
                kind, i, h = units[n]
                j = att_group0[n] + g
                first, nb = key_tiles(kind, i)
                q = quad[n]
                if g == 0 and h % 4 == 0 and q >= 2:
                    pe.wait_ge(fin_done, q - 1)
                if j == att_group0[where[("W", 0, 0)]]:
                    pe.wait_ge(v_ld, 48)
                taken(j)
                out = ps_o[q % 2][:, (h % 4) * HEAD:(h % 4 + 1) * HEAD]
                for b in range(4 * g, min(4 * g + 4, nb)):
                    mm = pe.matmul(out, p_t[:, j % PT_RING, (b % 4) * P:(b % 4 + 1) * P], values(kind, h // 4, first + b),
                                   start=(b == 0), stop=(b == nb - 1))
                mm.then_inc(pv_done, 1)

            pe.wait_ge(const_ld, 16)
            for p in preps[:4]:
                for g in range(len(EVACS[p[0]])):
                    prep(p, g)
            ahead = [(n, c) for n in range(N) for c in range(len(chunks[n]))]

            def ahead_of(a):
                if a + 2 >= len(att):
                    return chunk0[N]
                if index_after(a + 2):
                    return chunk0[att[a + 3]]
                return min(chunk0[att[a + 2]] + BANKS_S, chunk0[att[a + 3] + 1] if a + 3 < len(att) else chunk0[N])

            issued = ahead_of(-1)
            for s in range(issued):
                qk(*ahead[s])
            behind = []
            for a, n in enumerate(att):
                for job in pe_at.get(n, ()):
                    prep(*job)
                nb = width[n] // P
                ng = (nb + 3) // 4
                inner = min(ahead_of(a), chunk0[att[a + 2] + 1]) if index_after(a + 2) else ahead_of(a)
                pe.wait_ge(exp_done, a + 1)
                for g in range(ng):
                    m = group_no[("att", n, g)]
                    bank_free(m)
                    for b in range(4 * g, min(4 * g + 4, nb)):
                        mm = pe.transpose(ps_t[m % 2][:, (b % 4) * P:(b % 4 + 1) * P],
                                          scores[a % 3][:, b * P:(b + 1) * P], const("ident", 0, P))
                    mm.then_inc(group_turned, 1)
                    for s in range(issued, issued + max(0, inner - issued) // (ng - g)):
                        qk(*ahead[s])
                        issued += 1
                    behind.append((n, g))
                    if len(behind) > PV_LAG:
                        pv(*behind.pop(0))
                while issued < ahead_of(a):
                    qk(*ahead[issued])
                    issued += 1
            for job in behind:
                pv(*job)

        @block.scalar
        def _(act):
            def prep(p, g):
                kind, t = p
                cols = slice(t * P, (t + 1) * P)
                if kind == "A" and t >= 3:
                    act.wait_ge(qk_done, qk_before(where[("I", t - 1, 7)]))
                if kind == "A" and t >= RING:
                    act.wait_ge(qk_done, qk_before(where[("W", t - RING + W_TILES - 1, 7)]))
                if kind != "A" and t >= 1:
                    act.wait_ge(qk_done, qk_before(where[("S" if kind == "N" else "D", t - 1, 7)]))
                    act.wait_ge(swap_done[kind], 32 * t)
                dest = {"dk": lambda b, nb: dk_t[:, cols], "ksl": lambda b, nb: ksl_t[:, :, cols],
                        "kwn0": lambda b, nb: kwn_t[:, 0, t % RING, :], "kwn1": lambda b, nb: kwn_t[:, 1, t % RING, :],
                        "ik": lambda b, nb: ik_t[:, cols], "iq": lambda b, nb: iq_t[:, b - 6:b - 6 + nb, :],
                        "nq": lambda b, nb: q_t["N"][:, b:b + nb, :], "dq": lambda b, nb: q_t["D"][:, b:b + nb, :]}
                m = group_no[("prep", p, g)]
                act.wait_ge(group_turned, m + 1)
                for b, nb, name in EVACS[kind][g]:
                    src = ps_t[m % 2][:, (b % 4) * P:(b % 4 + nb) * P]
                    if nb > 1:
                        src = src.rearrange("p (b k) -> p b k", b=nb)
                    act.activation(dest[name](b, nb), src, ACT.Copy).then_inc(evac_done, 1)
                if kind == "A" and g == len(EVACS[kind]) - 1:
                    act.wait_ge(gate_in, 2 * (t + 1))
                    act.activation(gate[:, t % 4], gate[:, t % 4], ACT.Exp, scale=-1.0).then_inc(gate_exp, 1)

            def relus(n):
                for c, (col, w) in enumerate(chunks[n]):
                    r = relu0[n] + c
                    act.wait_ge(qk_done, chunk0[n] + c + 1)
                    if r >= RELU_RING:
                        act.wait_ge(index_done, r - RELU_RING + 1)
                    act.activation(relu[:, r % RELU_RING, 0:w], ps_s[(chunk0[n] + c) % BANKS_S][:, 0:w], ACT.Relu).then_inc(relu_done, 1)

            def exps(n):
                kind, i, h = units[n]
                a, w = a_of[n], width[n]
                act.wait_ge(masked, mask0[n + 1])
                if h % 4 == 0 and quad[n] >= 2:
                    act.wait_ge(fin_done, quad[n] - 1)
                act.activation(scores[a % 3][:, 0:w], scores[a % 3][:, 0:w], ACT.Exp, bias=nmax[:, a % 4, len(chunks[n]) - 1:len(chunks[n])],
                               scale=-1.0, accum_out=lsum[:, quad[n] % 2, h % 4:h % 4 + 1]).then_inc(exp_done, 1)

            def count(s, t, m):
                act.wait_ge(search_set, t - 1)
                act.wait_ge(mask_d_done, t)
                if m >= 1:
                    act.wait_ge(thr_moved, s)
                act.activation(junk_a[:, 0:act_part[t]], index[t % 2][:, 0:act_part[t]], ACT.Sign, bias=thr, scale=-1.0,
                               accum_out=cnt_a).then_inc(count_a, 1)

            for p in preps[:4]:
                for g in range(len(EVACS[p[0]])):
                    prep(p, g)
            exps(0)
            for a, n in enumerate(att):
                for job in pe_at.get(n, ()):
                    prep(*job)
                for g in range((width[n] // P + 3) // 4):
                    j = att_group0[n] + g
                    m = group_no[("att", n, g)]
                    w = min(512, width[n] - 512 * g)
                    act.wait_ge(group_turned, m + 1)
                    if j >= PT_RING:
                        act.wait_ge(pv_done, j - PT_RING + 1)
                    act.activation(p_t[:, j % PT_RING, 0:w], ps_t[m % 2][:, 0:w], ACT.Copy).then_inc(copied, 1)
                    if g == (1 if width[n] > LONG_UNIT else 0) and a + 1 < len(att):
                        exps(att[a + 1])
                for m in index_after(a + 2):
                    relus(m)
                if n in steps:
                    count(*steps[n])

        @block.vector
        def _(dve):
            owned = [0]

            def mine(ins):
                ins.then_inc(vec, 1)
                owned[0] += 1

            def settle():
                dve.wait_ge(vec, owned[0])

            def mask(n, c):
                kind, i, h = units[n]
                a = a_of[n]
                col, w = chunks[n][c]
                s = chunk0[n] + c
                if c == 0:
                    if a >= 3:
                        last = att[a - 3]
                        dve.wait_ge(group_turned, group_no[("att", last, (width[last] // P + 3) // 4 - 1)] + 1)
                    if kind == "S" and h % 4 == 0:
                        dve.wait_ge(mask_s_done, 2 * i + h // 4 + 1)
                    if kind == "D" and h == 0:
                        dve.wait_ge(mask_d_done, i + 1)
                    if a >= 4:
                        dve.wait_ge(exp_done, a - 3)
                dve.wait_ge(qk_done, s + 1)
                m = {"C": lambda: const("cmp", 120 - 8 * i, P),
                     "W": lambda: const("win", W_TILES * P - width[n] + col, w),
                     "S": lambda: mask_s[:, h // 4, col:col + w],
                     "D": lambda: mask_d[:, col:col + w]}[kind]()
                if c:
                    dve.wait_ge(masked, mask0[n] + c)
                start = nmax[:, a % 4, c - 1:c] if c else (1e20 if kind == "C" else 3e38)
                dve.tensor_tensor_reduce(scores[a % 3][:, col:col + w], ps_s[s % BANKS_S][:, 0:w], m, -SCALE, start, ALU.add, ALU.min,
                                         nmax[:, a % 4, c:c + 1]).then_inc(masked, 1)

            def index_unit(n):
                kind, t, h = units[n]
                for c, (col, w) in enumerate(chunks[n]):
                    r = relu0[n] + c
                    dve.wait_ge(relu_done, r + 1)
                    dst = index[t % 2][:, col:col + w]
                    weight = iw[:, t % 4, h:h + 1]
                    if h == 0:
                        if t >= 4 and c == 0:
                            dve.wait_ge(kept_done, t - 3)
                        dve.tensor_scalar(dst, relu[:, r % RELU_RING, 0:w], weight, None, ALU.mult).then_inc(index_done, 1)
                    else:
                        dve.wait_ge(index_done, r - len(chunks[n]) + 1)
                        dve.scalar_tensor_tensor(dst, relu[:, r % RELU_RING, 0:w], weight, dst, ALU.mult, ALU.add).then_inc(index_done, 1)

            def set_search(t):
                w = (t + 1) * P
                x = index[t % 2]
                dve.wait_ge(index_done, relu0[where[("I", t, 7)] + 1])
                mine(dve.tensor_reduce(amax, x[:, 0:w], AX.X, ALU.max, apply_absolute_value=True))
                settle()
                mine(dve.tensor_tensor(x[:, t * P:w], x[:, t * P:w], const("diag", 0, P), ALU.add))
                mine(dve.tensor_scalar(amax.bitcast(I32), amax.bitcast(I32), 0x7F800000, None, ALU.bitwise_and))
                mine(dve.memset(thr, 0.0))
                settle()
                dve.tensor_scalar(halves[:, :], const("halve", 0, NSTEP + 1), amax, None, ALU.mult).then_inc(search_set, 1)

            counted = []

            def move_threshold():
                if not counted:
                    return
                s, t, m = counted.pop()
                dve.wait_ge(count_a, s + 1)
                mine(dve.tensor_scalar(tmp1, cnt_a, 0.5, TOPK - 0.25 - act_part[t] / 2, ALU.mult, ALU.add))
                mine(dve.tensor_tensor(thr, thr, halves[:, m + 1:m + 2], ALU.subtract))
                dve.wait_ge(count_v, s + 1)
                settle()
                mine(dve.scalar_tensor_tensor(tmp2, cnt_v, tmp1, halves[:, m:m + 1], ALU.is_ge, ALU.mult))
                settle()
                dve.tensor_tensor(thr, thr, tmp2, ALU.add).then_inc(thr_moved, 1)

            def count(s, t, m):
                move_threshold()
                dve.wait_ge(search_set, t - 1)
                dve.wait_ge(mask_d_done, t)
                if m >= 1:
                    dve.wait_ge(thr_moved, s)
                counted.append((s, t, m))
                a, w = act_part[t], (t + 1) * P
                dve.tensor_scalar(junk_v[:, 0:w - a], index[t % 2][:, a:w], thr, None, ALU.is_ge, ALU.add, accum_out=cnt_v).then_inc(count_v, 1)

            def above_mask(t):
                w = (t + 1) * P
                dve.wait_ge(thr_moved, (t - 1) * NSTEP)
                mine(dve.tensor_tensor(hi, thr, halves[:, NSTEP:NSTEP + 1], ALU.add))
                mine(dve.tensor_tensor(lo, thr, halves[:, NSTEP:NSTEP + 1], ALU.subtract))
                settle()
                if t >= 3:
                    dve.wait_ge(mask_d_done, t)
                dve.tensor_scalar(above[:, 0:w], index[t % 2][:, 0:w], hi, None, ALU.is_gt, ALU.add, accum_out=n_above).then_inc(above_done, 1)

            def kept_mask(t):
                w = (t + 1) * P
                dve.wait_ge(atleast_done, 2 * (t - 1))
                x = index[t % 2][:, 0:w]
                mine(dve.tensor_tensor_scan(x, atleast[:, 0:w], above[:, 0:w], 0.0, ALU.add, ALU.subtract))
                settle()
                dve.scalar_tensor_tensor(atleast[:, 0:w], x, room, atleast[:, 0:w], ALU.is_le, ALU.mult).then_inc(kept_done, 1)

            def importance(n):
                kind, i, h = units[n]
                a, q = a_of[n], quad[n]
                dve.wait_ge(exp_done, a + 1)
                r = rsum[:, q % 2, h % 4:h % 4 + 1]
                mine(dve.tensor_scalar(r, lsum[:, q % 2, h % 4:h % 4 + 1], 1e-30, None, ALU.max))
                settle()
                mine(dve.reciprocal(r, r))
                settle()
                pr = scores[a % 3][:, 0:P]
                if h % 4 == 0:
                    mine(dve.tensor_scalar(imp_c[:, 1:P + 1], pr, r, None, ALU.mult))
                else:
                    mine(dve.scalar_tensor_tensor(imp_c[:, 1:P + 1], pr, r, imp_c[:, 1:P + 1], ALU.mult, ALU.add))
                settle()

            def select(i, g):
                x, y = imp[:, 0, :], imp[:, 1, :]
                mine(dve.tensor_reduce(x, imp_c[:, 1:P + 1].rearrange("p (j c) -> p j c", c=4), AX.X, ALU.add))
                settle()
                mine(dve.tensor_tensor(x, x, imp_c[:, 0:P:4], ALU.add))
                settle()
                mine(dve.tensor_tensor(x, x, const("keep", 30 - 2 * i, N_SLC), ALU.mult))
                settle()
                mine(dve.tensor_tensor(x, x, const("add", 30 - 2 * i, N_SLC), ALU.add))
                settle()
                mine(dve.memset(x[:, 0:1], 1.0e4))
                settle()
                mine(dve.max(top8[:, :], x))
                settle()
                mine(dve.match_replace(y, top8[:, :], x, -5.0))
                settle()
                if i >= 1:
                    dve.wait_ge(mask_s_done, 2 * i)
                dve.tensor_scalar(sel[:, g, :], y, -4.0, MASKED, ALU.is_gt, ALU.mult).then_inc(sel_done, 1)

            def finish(n):
                kind, i, h = units[n]
                q = quad[n]
                h0 = h - 3
                dve.wait_ge(exp_done, a_of[n] + 1)
                r = rsum[:, q % 2, :]
                if kind != "C":
                    mine(dve.reciprocal(r, lsum[:, q % 2, :]))
                    settle()
                if kind != "D":
                    if kind == "C" and h == 3:
                        dve.wait_ge(gate_done, i + 1)
                    b = "CSW".index(kind)
                    mine(dve.tensor_tensor(rgate[:, q % 2, :], r, gate[:, i % 4, 3 * h0 + b:3 * h0 + b + 10:3], ALU.mult))
                    settle()
                    r = rgate[:, q % 2, :]
                dve.wait_ge(pv_done, last_group[n])
                if q >= 2:
                    dve.wait_ge(acc_done, q - 1)
                dve.tensor_tensor(fin[:, q % 2].rearrange("p (h d) -> p h d", h=4), ps_o[q % 2][:, :].rearrange("p (h d) -> p h d", h=4),
                                  r.unsqueeze(2).broadcast_to([P, 4, HEAD]), ALU.mult).then_inc(fin_done, 1)

            def gates(t):
                dve.wait_ge(gate_exp, t + 1)
                mine(dve.tensor_scalar(gate[:, t % 4], gate[:, t % 4], 1.0, None, ALU.add))
                settle()
                dve.reciprocal(gate[:, t % 4], gate[:, t % 4]).then_inc(gate_done, 1)

            mine(dve.memset(imp_c[:, 0:1], 0.0))
            settle()
            dve.wait_ge(const_ld, 16)
            for t in range(3):
                gates(t)
            for n in range(2):
                for c in range(len(chunks[n])):
                    mask(n, c)
            for a, n in enumerate(att):
                kind, i, h = units[n]
                if i < MOVE_FIRST:
                    move_threshold()
                for c in range(len(chunks[att[a + 2]]) if a + 2 < len(att) else 0):
                    mask(att[a + 2], c)
                    if c == 0:
                        move_threshold()
                if a + 2 >= len(att):
                    move_threshold()
                for m in index_after(a + 1):
                    index_unit(m)
                if kind == "C":
                    importance(n)
                    if h % 4 == 3:
                        select(i, h // 4)
                    if i >= 2 and h == 0:
                        above_mask(i)
                    if i >= 2 and h == 3:
                        kept_mask(i)
                    if i >= 1 and h == 4 and i + 1 < TILES:
                        set_search(i + 1)
                for p, g in pe_at.get(n, ()):
                    if p[0] == "A" and g == len(EVACS["A"]) - 1:
                        gates(p[1])
                if n in finish_at:
                    finish(finish_at[n])
                if n in steps:
                    count(*steps[n])
            finish(N - 1)


def constants():
    q = np.arange(P)[:, None]
    out = {"ident": np.eye(P)}
    out["diag"] = np.where(np.arange(P)[None] > q, MASKED, 0.0)
    d = q - (np.arange(W_TILES * P)[None] - WINDOW)
    out["win"] = np.where((d >= 0) & (d < WINDOW), 0.0, MASKED)
    c = np.arange(248)[None] - 120
    out["cmp"] = np.where(CMP_STRIDE * c + CMP_BLOCK - 1 <= q, 0.0, MASKED)
    j = np.arange(62)[None] - 30
    cur = q // SLC_BLOCK
    forced = (j == cur) | (j == cur - 1)
    out["keep"] = np.where((j > cur) | forced, 0.0, 1.0)
    out["add"] = np.where(forced, 1.0e4, np.where(j > cur, -1.0, 0.0))
    out["halve"] = np.broadcast_to(2.0 ** (1.0 - np.arange(NSTEP + 1)), (P, NSTEP + 1))
    return np.ascontiguousarray(np.concatenate([out[n] for n, _ in CONST], axis=1).astype(np.float32))


def mixing_phase(nc, x, o_mix, gain, w_out, ln_g, ln_b, ident_in, h, h_t):
    HALF = D_MODEL // 2
    with ExitStack() as ctx:
        def sb(name, shape, dt=F32):
            return ctx.enter_context(nc.sbuf_tensor(name, shape, dt))

        def sem(name):
            return ctx.enter_context(nc.semaphore(name))

        def psum(name, cols):
            return ctx.enter_context(nc.psum_tensor(name, [P, cols], F32))

        w_hi = sb("m_w_hi", [P, KT, D_MODEL], F32R)
        w_lo = sb("m_w_lo", [P, KT, D_MODEL], F32R)
        w_raw = sb("m_w_raw", [P, 2, D_MODEL])
        ident = sb("m_ident", [P, P])
        gain_b = sb("m_gain", [P, D_MODEL])
        g_b = sb("m_ln_g", [P, D_MODEL])
        b_b = sb("m_ln_b", [P, D_MODEL])
        o_in = sb("m_o_in", [P, 2, D_MODEL])
        on = sb("m_on", [P, 2, D_MODEL])
        junk = sb("m_junk", [P, HALF])
        ot_hi = sb("m_ot_hi", [P, 2, KT, P], F32R)
        ot_lo = sb("m_ot_lo", [P, 2, KT, P], F32R)
        x_in = sb("m_x_in", [P, 2, D_MODEL])
        hp = sb("m_hp", [P, 2, D_MODEL])
        hn = sb("m_hn", [P, 2, D_MODEL])
        ho = sb("m_ho", [P, 2, D_MODEL])
        ht = sb("m_ht", [P, 2, KT, P])
        ssq = sb("m_ssq", [P, 2, 2])
        rinv = sb("m_rinv", [P, 2, 2])
        stats = sb("m_stats", [P, 2, 6])
        aggr = sb("m_aggr", [P, 2, 2])
        rstd = sb("m_rstd", [P, 2, 1])
        nmr = sb("m_nmr", [P, 2, 1])
        power = sb("m_power", [P, 2])
        eps = sb("m_eps", [P, 2])
        minus = sb("m_minus", [P, 1])
        t_o = psum("m_t_o", D_MODEL)
        ys = [psum(f"m_y{b}", D_MODEL) for b in range(2)]
        t_h = psum("m_t_h", D_MODEL)

        small_ld = sem("m_small_ld")
        w_ld = [sem(f"m_w_ld{b}") for b in range(2)]
        w_hi_done = sem("m_w_hi_done")
        w_lo_done = sem("m_w_lo_done")
        o_ld = [sem(f"m_o_ld{b}") for b in range(2)]
        x_ld = [sem(f"m_x_ld{b}") for b in range(2)]
        squared = sem("m_squared")
        rinv_done = sem("m_rinv_done")
        scaled = sem("m_scaled")
        o_turned = sem("m_o_turned")
        hi_done = sem("m_hi_done")
        lo_done = sem("m_lo_done")
        y_full = sem("m_y_full")
        added = sem("m_added")
        aggr_done = sem("m_aggr_done")
        rstd_done = sem("m_rstd_done")
        normed = sem("m_normed")
        gained = sem("m_gained")
        h_done = sem("m_h_done")
        h_turned = sem("m_h_turned")
        ht_done = sem("m_ht_done")
        h_out = [sem(f"m_h_out{b}") for b in range(2)]
        ht_out = [sem(f"m_ht_out{b}") for b in range(2)]
        own = sem("m_pool_own")
        fixed_set = sem("m_fixed_set")
        vec = sem("m_vec")
        block = ctx.enter_context(nc.Block())

        x_tiles = x.rearrange("(t p) n -> t p n", p=P)
        o_tiles = o_mix.rearrange("(t p) n -> t p n", p=P)
        h_tiles = h.rearrange("(t p) n -> t p n", p=P)
        ht_cols = h_t.rearrange("(k p) n -> p k n", p=P)
        w_rows = w_out.rearrange("(k p) n -> k p n", p=P)

        def tile_of(ap, t):
            return ap[bass.ds(t, 1), :, :].rearrange("o p n -> (o p) n")

        def reached(eng, s, value):
            if not isinstance(value, int) or value > 0:
                eng.wait_ge(s, value)

        def run_steps(eng, step):
            for t in range(3):
                step(t, t % 2, True, True)
            with eng.Fori(0, (TILES - 6) // 2) as i:
                for d in range(2):
                    step(2 * i + 3 + d, (3 + d) % 2, True, True)
            for t in range(TILES - 3, TILES):
                step(t, t % 2, t + 2 < TILES, t + 1 < TILES)

        @block.sync
        def _(sp):
            def load_o(t, u):
                reached(sp, scaled, 2 * (t - 1))
                sp.dma_start(o_in[:, u], tile_of(o_tiles, t)).then_inc(o_ld[u], 16)

            def load_x(t, u):
                reached(sp, added, t - 1)
                sp.dma_start(x_in[:, u], tile_of(x_tiles, t)).then_inc(x_ld[u], 16)

            def store(t, u):
                sp.wait_ge(h_done, t + 1)
                sp.dma_start(tile_of(h_tiles, t), ho[:, u]).then_inc(h_out[u], 16)
                sp.wait_ge(ht_done, 2 * (t + 1))
                sp.dma_start(ht_cols[:, :, bass.ds(t * P, P)], ht[:, u]).then_inc(ht_out[u], 16)

            for dst, src in ((ident, ident_in), (gain_b, gain.broadcast_to([P, D_MODEL])),
                             (g_b, ln_g.broadcast_to([P, D_MODEL])), (b_b, ln_b.broadcast_to([P, D_MODEL]))):
                sp.dma_start(dst[:, :], src).then_inc(small_ld, 16)
            for t in range(2):
                load_o(t, t)
            for k in range(KT):
                if k >= 2:
                    sp.wait_ge(w_lo_done, k - 1)
                sp.dma_start(w_raw[:, k % 2], w_rows[k]).then_inc(w_ld[k % 2], 16)
            for t in range(2):
                load_x(t, t)

            load_o(2, 0)

            def step(t, u, two, one):
                if not isinstance(t, int) or t + 3 < TILES:
                    load_o(t + 3, 1 - u)
                if two:
                    load_x(t + 2, u)
                if not isinstance(t, int) or t >= 1:
                    store(t - 1, 1 - u)

            run_steps(sp, step)
            store(TILES - 1, (TILES - 1) % 2)
            for b in range(2):
                sp.wait_ge(h_out[b], 16 * (TILES // 2))
                sp.wait_ge(ht_out[b], 16 * (TILES // 2))

        @block.gpsimd
        def _(pool):
            for c, value in ((power, -0.5), (eps, LN_EPS), (minus, -1.0)):
                pool.memset(c[:, :], value).then_inc(fixed_set, 1)

            def root_ln(t, u):
                pool.wait_ge(aggr_done, t + 1)
                reached(pool, normed, t - 1)
                pool.tensor_tensor(rstd[:, u], aggr[:, u, 1:2], eps[:, 0:1], ALU.add).then_inc(rstd_done, 1)
                pool.tensor_tensor(nmr[:, u], aggr[:, u, 0:1], minus[:, :], ALU.mult).then_inc(rstd_done, 1)
                pool.wait_ge(rstd_done, 4 * t + 2)
                pool.tensor_tensor(rstd[:, u], rstd[:, u], power[:, 0:1], ALU.pow).then_inc(rstd_done, 1)
                pool.wait_ge(rstd_done, 4 * t + 3)
                pool.tensor_tensor(nmr[:, u], nmr[:, u], rstd[:, u], ALU.mult).then_inc(rstd_done, 1)

            def add_b(t, u):
                pool.wait_ge(gained, t + 1)
                if not isinstance(t, int) or t >= 2:
                    pool.wait_ge(h_out[u], (t - u) * 8)
                    pool.wait_ge(h_turned, 2 * (t - 1))
                pool.tensor_tensor(ho[:, u], hn[:, u], b_b[:, :], ALU.add).then_inc(h_done, 1)

            pool.wait_ge(fixed_set, 3)
            for t in range(2):
                pool.wait_ge(squared, 2 * (t + 1))
                pool.tensor_tensor(rinv[:, t], ssq[:, t], eps[:, :], ALU.add).then_inc(own, 1)
                pool.wait_ge(own, t + 1)
                pool.tensor_tensor(rinv[:, t], rinv[:, t], power[:, :], ALU.pow).then_inc(rinv_done, 1)

            def step(t, u, two, one):
                if two:
                    pool.wait_ge(squared, 2 * (t + 3))
                    pool.wait_ge(scaled, 2 * (t + 1))
                    pool.tensor_tensor(rinv[:, u], ssq[:, u], eps[:, :], ALU.add).then_inc(own, 1)
                    pool.wait_ge(own, t + 3)
                    pool.tensor_tensor(rinv[:, u], rinv[:, u], power[:, :], ALU.pow).then_inc(rinv_done, 1)
                root_ln(t, u)
                add_b(t, u)

            run_steps(pool, step)

        @block.tensor
        def _(pe):
            def turn_o(t, u):
                pe.wait_ge(scaled, 2 * (t + 1))
                reached(pe, lo_done, 2 * t)
                for half in range(2):
                    for k in range(4 * half, 4 * half + 4):
                        mm = pe.transpose(t_o[:, k * P:(k + 1) * P], on[:, u, k * P:(k + 1) * P], ident[:, :])
                    mm.then_inc(o_turned, 1)

            def project(t, u):
                pe.wait_ge(lo_done, 2 * (t + 1))
                reached(pe, added, t - 1)
                for half in range(2):
                    for k in range(KT):
                        for n, (a, w) in enumerate(((ot_hi, w_hi), (ot_hi, w_lo), (ot_lo, w_hi))):
                            mm = pe.matmul(ys[u][:, half * HALF:(half + 1) * HALF], a[:, u, k], w[:, k, half * HALF:(half + 1) * HALF],
                                           start=(k == 0 and n == 0), stop=(k == KT - 1 and n == 2))
                mm.then_inc(y_full, 1)

            def follow_weights():
                pe.wait_ge(lo_done, 2)
                for k in range(KT):
                    pe.wait_ge(w_lo_done, k + 1)
                    for half in range(2):
                        cols = slice(half * HALF, (half + 1) * HALF)
                        for n, (a, w) in enumerate(((ot_hi, w_hi), (ot_hi, w_lo), (ot_lo, w_hi))):
                            mm = pe.matmul(ys[0][:, cols], a[:, 0, k], w[:, k, cols], start=(k == 0 and n == 0), stop=(k == KT - 1 and n == 2))
                mm.then_inc(y_full, 1)

            def turn_h(t, u):
                pe.wait_ge(h_done, t + 1)
                reached(pe, ht_done, 2 * t)
                for half in range(2):
                    for k in range(4 * half, 4 * half + 4):
                        mm = pe.transpose(t_h[:, k * P:(k + 1) * P], ho[:, u, k * P:(k + 1) * P], ident[:, :])
                    mm.then_inc(h_turned, 1)

            pe.wait_ge(small_ld, 64)
            turn_o(0, 0)

            def step(t, u, two, one):
                if isinstance(t, int) and t == 0:
                    follow_weights()
                    turn_o(1, 1)
                else:
                    if one:
                        turn_o(t + 1, 1 - u)
                    project(t, u)
                if not isinstance(t, int) or t >= 1:
                    turn_h(t - 1, 1 - u)

            run_steps(pe, step)
            turn_h(TILES - 1, (TILES - 1) % 2)

        @block.scalar
        def _(act):
            def square(t, u):
                act.wait_ge(o_ld[u], (t - u + 2) * 8)
                reached(act, rinv_done, t - 1)
                for half in range(2):
                    if not isinstance(t, int) or 2 * t + half >= 1:
                        act.wait_ge(squared, 2 * t + half)
                    act.activation(junk[:, :], o_in[:, u, half * HALF:(half + 1) * HALF], ACT.Square, scale=HALF ** -0.5,
                                   accum_out=ssq[:, u, half:half + 1]).then_inc(squared, 1)

            def high(t, u):
                reached(act, y_full, t - 1)
                for half in range(2):
                    act.wait_ge(o_turned, 2 * t + half + 1)
                    act.activation(ot_hi[:, u, 4 * half:4 * half + 4], t_o[:, half * HALF:(half + 1) * HALF].rearrange("p (k n) -> p k n", k=4),
                                   ACT.Copy).then_inc(hi_done, 1)

            def norm(t, u):
                act.wait_ge(rstd_done, 4 * (t + 1))
                act.wait_ge(added, t + 1)
                reached(act, gained, t - 1)
                act.activation(hp[:, u], hp[:, u], ACT.Identity, bias=nmr[:, u], scale=rstd[:, u]).then_inc(normed, 1)

            def copy_h(t, u):
                if not isinstance(t, int) or t >= 2:
                    act.wait_ge(ht_out[u], (t - u) * 8)
                for half in range(2):
                    act.wait_ge(h_turned, 2 * t + half + 1)
                    act.activation(ht[:, u, 4 * half:4 * half + 4], t_h[:, half * HALF:(half + 1) * HALF].rearrange("p (k n) -> p k n", k=4),
                                   ACT.Copy).then_inc(ht_done, 1)

            square(0, 0)
            square(1, 1)
            high(0, 0)
            for k in range(KT):
                act.wait_ge(w_ld[k % 2], 16 * (k // 2 + 1))
                act.activation(w_hi[:, k], w_raw[:, k % 2], ACT.Copy).then_inc(w_hi_done, 1)

            def step(t, u, two, one):
                if two:
                    square(t + 2, u)
                if one:
                    high(t + 1, 1 - u)
                norm(t, u)
                if not isinstance(t, int) or t >= 1:
                    copy_h(t - 1, 1 - u)

            run_steps(act, step)
            copy_h(TILES - 1, (TILES - 1) % 2)

        @block.vector
        def _(dve):
            def scale(t, u):
                dve.wait_ge(rinv_done, t + 1)
                reached(dve, o_turned, 2 * (t - 1))
                for half in range(2):
                    c = slice(half * HALF, (half + 1) * HALF)
                    dve.scalar_tensor_tensor(on[:, u, c], o_in[:, u, c], rinv[:, u, half:half + 1], gain_b[:, c], ALU.mult, ALU.mult).then_inc(scaled, 1)

            def low(t, u):
                for half in range(2):
                    dve.wait_ge(hi_done, 2 * t + half + 1)
                    dve.tensor_tensor(ot_lo[:, u, 4 * half:4 * half + 4], t_o[:, half * HALF:(half + 1) * HALF].rearrange("p (k n) -> p k n", k=4),
                                      ot_hi[:, u, 4 * half:4 * half + 4].bitcast(F32), ALU.subtract).then_inc(lo_done, 1)

            def add_x(t, u):
                dve.wait_ge(y_full, t + 1)
                dve.wait_ge(x_ld[u], (t - u + 2) * 8)
                reached(dve, gained, t - 1)
                dve.scalar_tensor_tensor(hp[:, u], x_in[:, u], ALPHA, ys[u][:, :], ALU.mult, ALU.add).then_inc(added, 1)
                dve.wait_ge(added, t + 1)
                reached(dve, aggr_done, t)
                reached(dve, rstd_done, 4 * (t - 1))
                for half in range(2):
                    dve.bn_stats(stats[:, half], hp[:, u, half * HALF:(half + 1) * HALF]).then_inc(vec, 1)
                dve.wait_ge(small_ld, 64)
                dve.wait_ge(vec, 2 * (t + 1))
                dve.bn_aggr(aggr[:, u], stats[:, :, :].rearrange("p a s -> p (a s)")).then_inc(aggr_done, 1)

            def gains(t, u):
                dve.wait_ge(normed, t + 1)
                reached(dve, h_done, t - 1)
                dve.tensor_tensor(hn[:, u], hp[:, u], g_b[:, :], ALU.mult).then_inc(gained, 1)

            dve.wait_ge(small_ld, 64)
            scale(0, 0)
            scale(1, 1)
            low(0, 0)
            for k in range(KT):
                dve.wait_ge(w_hi_done, k + 1)
                dve.tensor_tensor(w_lo[:, k], w_raw[:, k % 2], w_hi[:, k].bitcast(F32), ALU.subtract).then_inc(w_lo_done, 1)

            def step(t, u, two, one):
                if two:
                    scale(t + 2, u)
                if one:
                    low(t + 1, 1 - u)
                add_x(t, u)
                gains(t, u)

            run_steps(dve, step)


GROUP = 512
N_GROUPS = SEQ // GROUP
FT = FFN // P
DOWN = FT // 2


def ffn_phase(nc, h, h_t, w_gate, w_up, w_down, ln_g, ln_b, out):
    NB = GROUP // P
    HALF = D_MODEL // 2
    W_PER = 2 * FT + 2 * DOWN
    NX = KT * GROUP // D_MODEL
    X_AFTER = {2: 0, 6: 1, 13: 2, 17: 3}
    S_PER = W_PER + NX

    def raw_of_down(d, last):
        return d if last else d + sum(1 for k in X_AFTER if k < d)

    with ExitStack() as ctx:
        def sb(name, shape, dt=F32):
            return ctx.enter_context(nc.sbuf_tensor(name, shape, dt))

        def sem(name):
            return ctx.enter_context(nc.semaphore(name))

        def psum(name, cols):
            return ctx.enter_context(nc.psum_tensor(name, [P, cols], F32))

        raw = sb("f_raw", [P, 2, D_MODEL])
        w_hi = sb("f_w_hi", [P, 2, D_MODEL], F32R)
        w_lo = sb("f_w_lo", [P, 2, D_MODEL], F32R)
        x_hi = sb("f_x_hi", [P, KT, GROUP], F32R)
        x_lo = sb("f_x_lo", [P, KT, GROUP], F32R)
        silu = sb("f_silu", [P, 2, GROUP])
        prod = sb("f_prod", [P, 2, GROUP])
        g_hi = sb("f_g_hi", [P, FT, GROUP], F32R)
        g_lo = sb("f_g_lo", [P, FT, GROUP], F32R)
        y = sb("f_y", [P, NB, D_MODEL])
        g_b = sb("f_ln_g", [P, D_MODEL])
        b_b = sb("f_ln_b", [P, D_MODEL])
        stats = sb("f_stats", [P, 2, 6])
        aggr = sb("f_aggr", [P, NB, 2])
        rstd = sb("f_rstd", [P, NB])
        nmr = sb("f_nmr", [P, NB])
        power = sb("f_power", [P, 1])
        eps = sb("f_eps", [P, 1])
        minus = sb("f_minus", [P, 1])
        mark = sb("f_mark", [P, 1])
        gate_ps = [psum(f"f_gate{b}", GROUP) for b in range(2)]
        up_ps = [psum(f"f_up{b}", GROUP) for b in range(2)]
        acc = [psum(f"f_acc{b}", HALF) for b in range(NB)]

        small_ld = sem("f_small_ld")
        raw_ld = [sem(f"f_raw_ld{b}") for b in range(2)]
        y_ld = sem("f_y_ld")
        hi_done = sem("f_hi_done")
        lo_done = sem("f_lo_done")
        used = sem("f_used")
        silu_done = sem("f_silu_done")
        prod_done = sem("f_prod_done")
        g_hi_done = sem("f_g_hi_done")
        g_lo_done = sem("f_g_lo_done")
        added = sem("f_added")
        stats_done = sem("f_stats_done")
        aggr_done = sem("f_aggr_done")
        rstd_done = sem("f_rstd_done")
        normed = sem("f_normed")
        gained = sem("f_gained")
        y_done = sem("f_y_done")
        y_out = sem("f_y_out")
        fixed_set = sem("f_fixed_set")
        marked = sem("f_marked")
        block = ctx.enter_context(nc.Block())

        gate_cols = w_gate.rearrange("(k p) n -> p k n", p=P)
        up_cols = w_up.rearrange("(k p) n -> p k n", p=P)
        down_rows = w_down.rearrange("(f p) n -> p f n", p=P)
        xt_rows = h_t.rearrange("(k p) n -> p k n", p=P)
        h_rows = h.rearrange("(g t p) n -> g p t n", p=P, t=NB)
        out_rows = out.rearrange("(g t p) n -> g p t n", p=P, t=NB)

        def over_groups(eng, body):
            body(0, True, False)
            body(1, False, False)
            with eng.Fori(2, N_GROUPS - 1) as g:
                body(g, False, False)
            body(N_GROUPS - 1, False, True)

        @block.sync
        def _(sp):
            def load(s, parity, src, shape=None):
                if not isinstance(s, int) or s >= 2:
                    sp.wait_ge(lo_done, s - 1)
                dst = raw[:, parity]
                if shape:
                    dst = dst.rearrange("p (a n) -> p a n", a=shape)
                sp.dma_start(dst, src).then_inc(raw_ld[parity], 16)

            def load_x(s, parity, g, n):
                load(s, parity, xt_rows[:, 2 * n:2 * n + 2, bass.ds(g * GROUP, GROUP)], 2)

            for dst, src in ((g_b, ln_g.broadcast_to([P, D_MODEL])), (b_b, ln_b.broadcast_to([P, D_MODEL]))):
                sp.dma_start(dst[:, :], src).then_inc(small_ld, 16)
            for n in range(NX):
                load_x(n, n % 2, 0, n)

            def store(g):
                sp.wait_ge(y_done, NB * (g + 1))
                sp.dma_start(out_rows[bass.ds(g, 1), :, :, :].rearrange("o p t n -> (o p) t n"), y[:, :, :]).then_inc(y_out, 16)

            def body(g, first, last):
                s0 = NX + g * S_PER
                with sp.Fori(0, FT) as f:
                    for m, cols in enumerate((gate_cols, up_cols)):
                        load(s0 + 2 * f + m, m, cols[:, :, bass.ds(f * P, P)], KT)
                if not first:
                    store(g - 1)
                    sp.wait_ge(y_out, 16 * g)
                sp.dma_start(y[:, :, :], h_rows[bass.ds(g, 1), :, :, :].rearrange("o p t n -> (o p) t n")).then_inc(y_ld, 16)
                for d in range(2 * DOWN):
                    s = raw_of_down(d, last)
                    half, b = divmod(d, DOWN)
                    load(s0 + 2 * FT + s, s % 2, down_rows[:, 2 * b:2 * b + 2, half * HALF:(half + 1) * HALF], 2)
                    if d in X_AFTER and not last:
                        load_x(s0 + 2 * FT + s + 1, (s + 1) % 2, g + 1, X_AFTER[d])

            over_groups(sp, body)
            for t in range(NB):
                sp.wait_ge(y_done, NB * (N_GROUPS - 1) + t + 1)
                sp.dma_start(out_rows[N_GROUPS - 1, :, t, :], y[:, t]).then_inc(y_out, 16)
            sp.wait_ge(y_out, 16 * (N_GROUPS - 1 + NB))

        def down_splits(split, split_x, g, last, after):
            for d in range(2 * DOWN):
                e = d + 2
                if e - 1 in X_AFTER and not last:
                    split_x(NX + g * S_PER + 2 * FT + raw_of_down(e, last) - 1, (raw_of_down(e, last) - 1) % 2, X_AFTER[e - 1], g)
                if e < 2 * DOWN:
                    split(NX + g * S_PER + 2 * FT + raw_of_down(e, last), raw_of_down(e, last) % 2, g * W_PER + 2 * FT + e, e % 2)
                elif not last:
                    m = e - 2 * DOWN
                    split(NX + (g + 1) * S_PER + m, m, (g + 1) * W_PER + m, m)
                after(d)

        def raw_landed(eng, s, parity):
            eng.wait_ge(raw_ld[parity], (s - parity + 2) * 8)

        @block.gpsimd
        def _(pool):
            for c, value in ((power, -0.5), (eps, LN_EPS), (minus, -1.0)):
                pool.memset(c[:, :], value).then_inc(fixed_set, 1)
            pool.wait_ge(fixed_set, 3)
            pool.wait_ge(small_ld, 32)

            def body(g, first, last):
                n0 = g * NB
                for t in range(NB):
                    pool.wait_ge(aggr_done, n0 + t + 1)
                    pool.tensor_tensor(rstd[:, t:t + 1], aggr[:, t, 1:2], eps[:, :], ALU.add).then_inc(rstd_done, 1)
                    pool.tensor_tensor(nmr[:, t:t + 1], aggr[:, t, 0:1], minus[:, :], ALU.mult).then_inc(rstd_done, 1)
                    pool.wait_ge(rstd_done, 4 * (n0 + t) + 2)
                    pool.tensor_tensor(rstd[:, t:t + 1], rstd[:, t:t + 1], power[:, :], ALU.pow).then_inc(rstd_done, 1)
                    pool.wait_ge(rstd_done, 4 * (n0 + t) + 3)
                    pool.tensor_tensor(nmr[:, t:t + 1], nmr[:, t:t + 1], rstd[:, t:t + 1], ALU.mult).then_inc(rstd_done, 1)
                for t in range(NB):
                    pool.wait_ge(normed, n0 + t + 1)
                    if not last:
                        pool.tensor_tensor(y[:, t], y[:, t], g_b[:, :], ALU.mult).then_inc(gained, 1)
                    pool.wait_ge(gained, n0 + t + 1)
                    pool.tensor_tensor(y[:, t], y[:, t], b_b[:, :], ALU.add).then_inc(y_done, 1)

            over_groups(pool, body)

        @block.tensor
        def _(pe):
            def product(out, a, w, start, stop):
                return pe.matmul(out, a, w, start=start, stop=stop)

            def body(g, first, last):
                s0, w0 = NX + g * S_PER, g * W_PER

                def gate_up(f, q, wait_bank):
                    for m, ps in enumerate((gate_ps, up_ps)):
                        pe.wait_ge(lo_done, s0 + 2 * f + m + 1)
                        if wait_bank:
                            pe.wait_ge(prod_done, g * FT + f - 1)
                        for k in range(KT):
                            cols = slice(k * P, (k + 1) * P)
                            for n, (w, x) in enumerate(((w_hi, x_hi), (w_hi, x_lo), (w_lo, x_hi))):
                                mm = product(ps[q][:, :], w[:, m, cols], x[:, k], k == 0 and n == 0, k == KT - 1 and n == 2)
                        mm.then_inc(used, 1)

                gate_up(0, 0, not first)
                gate_up(1, 1, not first)
                with pe.Fori(1, FT // 2) as f2:
                    for q in range(2):
                        gate_up(2 * f2 + q, q, True)
                for d in range(2 * DOWN):
                    half, b = divmod(d, DOWN)
                    pe.wait_ge(lo_done, s0 + 2 * FT + raw_of_down(d, last) + 1)
                    if half == 0:
                        pe.wait_ge(g_lo_done, g * FT + 2 * b + 2)
                    for j in range(2):
                        f = 2 * b + j
                        for t in range(NB):
                            if b == 0 and j == 0 and not (first and half == 0):
                                pe.wait_ge(added, NB * (2 * g + half - 1) + t + 1)
                            cols = slice(t * P, (t + 1) * P)
                            for n, (x, w) in enumerate(((g_hi, w_hi), (g_hi, w_lo), (g_lo, w_hi))):
                                mm = product(acc[t][:, :], x[:, f, cols], w[:, d % 2, j * HALF:(j + 1) * HALF],
                                             f == 0 and n == 0, f == FT - 1 and n == 2)
                    mm.then_inc(used, 1)

            over_groups(pe, body)

        @block.scalar
        def _(act):
            def high(s, parity, w, slot):
                raw_landed(act, s, parity)
                if not isinstance(w, int) or w >= 2:
                    act.wait_ge(used, w - 1)
                act.activation(w_hi[:, slot], raw[:, parity], ACT.Copy).then_inc(hi_done, 1)

            def high_x(s, parity, n, g):
                raw_landed(act, s, parity)
                if g is not None:
                    act.wait_ge(used, g * W_PER + 2 * FT)
                act.activation(x_hi[:, 2 * n:2 * n + 2], raw[:, parity].rearrange("p (a n) -> p a n", a=2), ACT.Copy).then_inc(hi_done, 1)

            for n in range(NX):
                high_x(n, n % 2, n, None)
            for m in range(2):
                high(NX + m, m, m, m)

            def norm(g):
                for t in range(NB):
                    act.wait_ge(rstd_done, 4 * (g * NB + t + 1))
                    act.activation(y[:, t], y[:, t], ACT.Identity, bias=nmr[:, t:t + 1], scale=rstd[:, t:t + 1]).then_inc(normed, 1)

            def body(g, first, last):
                s0, w0 = NX + g * S_PER, g * W_PER

                def tile(f, q, wait):
                    high(s0 + 2 * f + 2, 0, w0 + 2 * f + 2, 0)
                    act.wait_ge(used, w0 + 2 * f + 1)
                    if wait:
                        act.wait_ge(prod_done, g * FT + f - 1)
                    act.activation(silu[:, q], gate_ps[q][:, :], ACT.Silu).then_inc(silu_done, 1)
                    high(s0 + 2 * f + 3, 1, w0 + 2 * f + 3, 1)
                    act.wait_ge(prod_done, g * FT + f + 1)
                    act.activation(g_hi[:, bass.ds(f, 1)].rearrange("p o n -> p (o n)"), prod[:, q], ACT.Copy).then_inc(g_hi_done, 1)

                tile(0, 0, not first)
                tile(1, 1, not first)
                if not first:
                    norm(g - 1)
                with act.Fori(1, FT // 2) as f2:
                    for q in range(2):
                        tile(2 * f2 + q, q, True)
                down_splits(high, high_x, g, last, lambda d: None)
            over_groups(act, body)
            norm(N_GROUPS - 1)

        @block.vector
        def _(dve):
            def low(s, parity, w, slot):
                dve.wait_ge(hi_done, s + 1)
                dve.tensor_tensor(w_lo[:, slot], raw[:, parity], w_hi[:, slot].bitcast(F32), ALU.subtract).then_inc(lo_done, 1)

            def low_x(s, parity, n, g):
                dve.wait_ge(hi_done, s + 1)
                dve.tensor_tensor(x_lo[:, 2 * n:2 * n + 2], raw[:, parity].rearrange("p (a n) -> p a n", a=2),
                                  x_hi[:, 2 * n:2 * n + 2].bitcast(F32), ALU.subtract).then_inc(lo_done, 1)

            dve.wait_ge(small_ld, 32)
            for n in range(NX):
                low_x(n, n % 2, n, None)
            for m in range(2):
                low(NX + m, m, m, m)

            def moments(g, first):
                n0 = g * NB
                for t in range(NB):
                    dve.wait_ge(added, 2 * n0 + NB + t + 1)
                    if t or not first:
                        dve.wait_ge(aggr_done, n0 + t)
                    for half in range(2):
                        dve.bn_stats(stats[:, half], y[:, t, half * HALF:(half + 1) * HALF]).then_inc(stats_done, 1)
                    if t == 0 and not first:
                        dve.wait_ge(rstd_done, 4 * n0)
                    dve.wait_ge(stats_done, 2 * (n0 + t + 1))
                    if t or not first:
                        dve.wait_ge(marked, n0 + t)
                    dve.tensor_tensor(mark[:, :], g_b[:, 0:1], b_b[:, 0:1], ALU.add).then_inc(marked, 1)
                    dve.bn_aggr(aggr[:, t], stats[:, :, :].rearrange("p a s -> p (a s)")).then_inc(aggr_done, 1)

            def body(g, first, last):
                s0, w0 = NX + g * S_PER, g * W_PER

                def tile(f, q, wait):
                    low(s0 + 2 * f + 2, 0, w0 + 2 * f + 2, 0)
                    low(s0 + 2 * f + 3, 1, w0 + 2 * f + 3, 1)
                    dve.wait_ge(silu_done, g * FT + f + 1)
                    dve.wait_ge(used, w0 + 2 * f + 2)
                    if wait:
                        dve.wait_ge(g_lo_done, g * FT + f - 1)
                    dve.tensor_tensor(prod[:, q], silu[:, q], up_ps[q][:, :], ALU.mult).then_inc(prod_done, 1)
                    dve.wait_ge(g_hi_done, g * FT + f + 1)
                    cols = bass.ds(f, 1)
                    dve.tensor_tensor(g_lo[:, cols].rearrange("p o n -> p (o n)"), prod[:, q],
                                      g_hi[:, cols].rearrange("p o n -> p (o n)").bitcast(F32), ALU.subtract).then_inc(g_lo_done, 1)

                def after(d):
                    if (d + 1) % DOWN == 0:
                        half = d // DOWN
                        cols = slice(half * HALF, (half + 1) * HALF)
                        dve.wait_ge(used, w0 + 2 * FT + d + 1)
                        dve.wait_ge(y_ld, 16 * (g + 1))
                        for t in range(NB):
                            dve.scalar_tensor_tensor(y[:, t, cols], y[:, t, cols], ALPHA, acc[t][:, :], ALU.mult, ALU.add).then_inc(added, 1)

                tile(0, 0, not first)
                if not first:
                    moments(g - 1, isinstance(g, int) and g == 1)
                tile(1, 1, not first)
                with dve.Fori(1, FT // 2) as f2:
                    for q in range(2):
                        tile(2 * f2 + q, q, True)
                down_splits(low, low_x, g, last, after)

            over_groups(dve, body)
            moments(N_GROUPS - 1, False)
            for t in range(NB):
                dve.wait_ge(normed, (N_GROUPS - 1) * NB + t + 1)
                dve.wait_ge(gained, (N_GROUPS - 1) * NB + t)
                dve.tensor_tensor(y[:, t], y[:, t], g_b[:, :], ALU.mult).then_inc(gained, 1)


def layer(nc, ap, out):
    def scratch(name, rows, cols):
        return nc.dram_tensor(name, (rows, cols), F32, kind="Internal").ap()

    z = scratch("z_scratch", SEQ, IN_COLS)
    o_mix = scratch("o_scratch", SEQ, D_MODEL)
    h = scratch("h_scratch", SEQ, D_MODEL)
    h_t = scratch("ht_scratch", D_MODEL, SEQ)
    ident = ap["consts"][:, CCOL["ident"]:CCOL["ident"] + P]
    projection_phase(nc, ap["x_t"], ap["w_in"], ap["b_in"], ap["pos"], ap["freq"], z)
    with ExitStack() as ctx:
        kc = ctx.enter_context(nc.sbuf_tensor("kc", [P, GROUPS, P], F32R))
        vc = ctx.enter_context(nc.sbuf_tensor("vc", [P, GROUPS, HEAD], F32))
        compression_phase(nc, z, ap["cmp_pos"], ap["cmp_w1"], ap["cmp_w2"], ident, kc[:, :, :], vc[:, :, :])
        attention_phase(nc, z, ap["consts"], kc[:, :, :], vc[:, :, :], o_mix)
    mixing_phase(nc, ap["x"], o_mix, ap["gain"], ap["w_out"], ap["ln1_g"], ap["ln1_b"], ident, h, h_t)
    ffn_phase(nc, h, h_t, ap["w_gate"], ap["w_up"], ap["w_down"], ap["ln2_g"], ap["ln2_b"], out)


def kernel(x, positions, w_in, b_in, cmp_pos, cmp_w1, cmp_w2, mix_gain, w_out,
           ln1_g, ln1_b, w_gate, w_up, w_down, ln2_g, ln2_b):
    import concourse.bacc as _bacc
    from concourse.bass_utils import run_bass_kernel_spmd as _run

    own = (("dq", 512), ("dk", 64), ("dv", 64), ("iq", 256), ("iw", 8), ("ik", 32), ("nq", 512), ("kcm", 128),
           ("vcm", 128), ("ksl", 128), ("vsl", 128), ("kwn", 128), ("vwn", 128), ("ng", 24))
    start, at = {}, 0
    for name, n in own:
        start[name] = at
        at += n
    order = np.concatenate([np.arange(start[name], start[name] + n) for name, n in PARTS])
    freq = np.concatenate([500000.0 ** (-np.arange(8) / 8), 500000.0 ** (-np.arange(4) / 4)]).astype(np.float32)
    arrays = {
        "x": np.asarray(x)[0],
        "x_t": np.asarray(x)[0].T,
        "pos": np.asarray(positions)[0].reshape(TILES, P).T,
        "freq": np.broadcast_to(freq, (P, 12)),
        "w_in": np.asarray(w_in)[0][:, order],
        "b_in": np.asarray(b_in)[:, order],
        "cmp_pos": np.asarray(cmp_pos)[0].reshape(2, CMP_BLOCK // 2, P).transpose(2, 0, 1),
        "cmp_w1": np.asarray(cmp_w1)[0],
        "cmp_w2": np.asarray(cmp_w2)[0],
        "gain": np.asarray(mix_gain),
        "w_out": np.asarray(w_out)[0],
        "ln1_g": np.asarray(ln1_g), "ln1_b": np.asarray(ln1_b),
        "w_gate": np.asarray(w_gate)[0], "w_up": np.asarray(w_up)[0], "w_down": np.asarray(w_down)[0],
        "ln2_g": np.asarray(ln2_g), "ln2_b": np.asarray(ln2_b),
        "consts": constants(),
    }
    arrays = {f"in_{k}": np.ascontiguousarray(a) for k, a in arrays.items()}
    nc = _bacc.Bacc("TRN2", target_bir_lowering=False, num_devices=1)
    ap = {k[3:]: nc.dram_tensor(k, a.shape, mybir.dt.from_np(a.dtype), kind="ExternalInput").ap() for k, a in arrays.items()}
    out = nc.dram_tensor("out", (SEQ, D_MODEL), F32, kind="ExternalOutput").ap()
    layer(nc, ap, out)
    r = _run(nc, [arrays], core_ids=[0])
    return np.asarray(r.results[0]["out"]).reshape(1, SEQ, D_MODEL)
```
